# Optimizing a Trainium2 kernel written in Bass

```python
import math
import jax, jax.numpy as jnp
from jax import lax
import numpy as np

D_MODEL = 1024
BATCH = 1
SEQ = 512
DEPTH = 2
DEC_BATCH = 8
DEC_SEQ = 1
PAST_LEN = 1024
PAGE_SIZE = 128

N_MIXERS = 2
N_SSD_LAYERS = (DEPTH + 1) // 2
N_NSA_LAYERS = DEPTH // 2
NORM_EPS = 1e-6

SSD_D_INNER = 2 * D_MODEL
SSD_HEAD_DIM = 64
SSD_N_HEADS = SSD_D_INNER // SSD_HEAD_DIM
SSD_N_GROUPS = 8
SSD_HEADS_PER_GROUP = SSD_N_HEADS // SSD_N_GROUPS
SSD_D_STATE = 128
SSD_CONV_W = 4
SSD_CONV_DIM = SSD_D_INNER + 2 * SSD_N_GROUPS * SSD_D_STATE
SSD_CHUNK = 128
SSD_IN_DIM = SSD_D_INNER + SSD_CONV_DIM + SSD_N_HEADS

NSA_N_HEADS = 16
NSA_HEAD_DIM = 64
NSA_N_KV = 4
NSA_HEADS_PER_KV = NSA_N_HEADS // NSA_N_KV
NSA_WIDTH = NSA_N_HEADS * NSA_HEAD_DIM
NSA_KV_WIDTH = NSA_N_KV * NSA_HEAD_DIM
N_BRANCH = 3
CMP_BLOCK = 32
CMP_STRIDE = 16
CMP_HIDDEN = 128
SEL_BLOCK = 64
SEL_TOPK = 16
WINDOW = 512
NSA_QBLOCK = 64
FORCE_SCORE = 1e4
NSA_IN_DIM = NSA_WIDTH + 6 * NSA_KV_WIDTH + NSA_N_HEADS * N_BRANCH + N_BRANCH * NSA_WIDTH

REL_BUCKETS = 32
REL_MAX_DIST = 1024

kernel_name = 'nsa_ssd_hybrid_step'

def rmsnorm(x, w):
    xf = x.astype(jnp.float32)
    y = xf * lax.rsqrt(jnp.mean(xf * xf, axis=-1, keepdims=True) + NORM_EPS)
    return (y * w.astype(jnp.float32)).astype(x.dtype)

def rel_bucket(dist):
    n = jnp.maximum(dist, 0)
    exact = REL_BUCKETS // 2
    logv = jnp.log(jnp.maximum(n, 1).astype(jnp.float32) / exact) / math.log(REL_MAX_DIST / exact)
    large = jnp.minimum(exact + (logv * (REL_BUCKETS - exact)).astype(jnp.int32), REL_BUCKETS - 1)
    return jnp.where(n < exact, n, large)

def masked_softmax(s, mask):
    s = jnp.where(mask, s, -jnp.inf)
    m = jnp.max(s, axis=-1, keepdims=True)
    m = jnp.where(jnp.isfinite(m), m, 0.0)
    e = jnp.where(mask, jnp.exp(s - m), 0.0)
    den = jnp.sum(e, axis=-1, keepdims=True)
    return e / jnp.where(den > 0, den, 1.0)

def ssd_scan(xs, dt, a, bm, cm, h0):
    bsz, t = xs.shape[:2]
    lc = min(SSD_CHUNK, t)
    nc = -(-t // lc)
    pad = nc * lc - t
    if pad:
        xs = jnp.pad(xs, ((0, 0), (0, pad), (0, 0), (0, 0), (0, 0)))
        dt = jnp.pad(dt, ((0, 0), (0, pad), (0, 0), (0, 0)))
        bm = jnp.pad(bm, ((0, 0), (0, pad), (0, 0), (0, 0)))
        cm = jnp.pad(cm, ((0, 0), (0, pad), (0, 0), (0, 0)))
    g, r, p, n = SSD_N_GROUPS, SSD_HEADS_PER_GROUP, SSD_HEAD_DIM, SSD_D_STATE
    xdt = (xs * dt[..., None]).reshape(bsz, nc, lc, g, r, p)
    a_cs = jnp.cumsum((dt * a).reshape(bsz, nc, lc, g, r), axis=2)
    bc = bm.reshape(bsz, nc, lc, g, n)
    cc = cm.reshape(bsz, nc, lc, g, n)
    causal = jnp.tril(jnp.ones((lc, lc), dtype=bool))
    seg = a_cs[:, :, :, None] - a_cs[:, :, None, :]
    decay = jnp.exp(jnp.where(causal[:, :, None, None], seg, -jnp.inf))
    cb = jnp.einsum('bclgn,bcsgn->bclsg', cc, bc)
    y_diag = jnp.einsum('bclsg,bclsgr,bcsgrp->bclgrp', cb, decay, xdt)
    to_end = jnp.exp(a_cs[:, :, -1:] - a_cs)
    chunk_states = jnp.einsum('bclgn,bclgr,bclgrp->bcgrpn', bc, to_end, xdt)
    chunk_decay = jnp.exp(a_cs[:, :, -1])

    def body(h, inp):
        st, dc = inp
        return h * dc[..., None, None] + st, h

    h_last, h_prev = lax.scan(body, h0, (chunk_states.swapaxes(0, 1), chunk_decay.swapaxes(0, 1)))
    h_prev = h_prev.swapaxes(0, 1)
    y_off = jnp.einsum('bclgn,bcgrpn,bclgr->bclgrp', cc, h_prev, jnp.exp(a_cs))
    y = (y_diag + y_off).reshape(bsz, nc * lc, g, r, p)[:, :t]
    return y, h_last

def ssd_layer(x, conv_prev, ssm_prev, norm_w, w_in, conv_w, conv_b, dt_bias, a_log, d_skip, gnorm, w_out):
    f32 = jnp.float32
    bsz, t = x.shape[:2]
    g, r, p, n = SSD_N_GROUPS, SSD_HEADS_PER_GROUP, SSD_HEAD_DIM, SSD_D_STATE
    u = rmsnorm(x, norm_w) @ w_in
    z, xbc, dt_raw = jnp.split(u, [SSD_D_INNER, SSD_D_INNER + SSD_CONV_DIM], axis=-1)
    xpad = jnp.concatenate([conv_prev.astype(xbc.dtype), xbc], axis=1)
    conv = conv_b
    for k in range(SSD_CONV_W):
        conv = conv + xpad[:, k:k + t] * conv_w[k]
    xbc_act = jax.nn.silu(conv.astype(f32))
    new_conv = xpad[:, -(SSD_CONV_W - 1):]
    xs, bm, cm = jnp.split(xbc_act, [SSD_D_INNER, SSD_D_INNER + g * n], axis=-1)
    dt = jax.nn.softplus(dt_raw.astype(f32) + dt_bias.astype(f32))
    a = -jnp.exp(a_log.astype(f32))
    xs = xs.reshape(bsz, t, g, r, p)
    y, h_last = ssd_scan(xs, dt.reshape(bsz, t, g, r), a.reshape(g, r), bm.reshape(bsz, t, g, n),
                         cm.reshape(bsz, t, g, n), ssm_prev.astype(f32).reshape(bsz, g, r, p, n))
    y = y + xs * d_skip.astype(f32).reshape(g, r)[..., None]
    y = y.reshape(bsz, t, SSD_D_INNER) * jax.nn.silu(z.astype(f32))
    yg = y.reshape(bsz, t, SSD_N_GROUPS, -1)
    yg = yg * lax.rsqrt(jnp.mean(yg * yg, axis=-1, keepdims=True) + NORM_EPS)
    y = yg.reshape(bsz, t, SSD_D_INNER) * gnorm.astype(f32)
    out = x + y.astype(x.dtype) @ w_out
    return out, new_conv, h_last.reshape(bsz, SSD_N_HEADS, p, n).astype(x.dtype)

def compress(k, pe, w1, w2, n_blocks):
    bsz = k.shape[0]
    idx = jnp.arange(n_blocks)[:, None] * CMP_STRIDE + jnp.arange(CMP_BLOCK)[None, :]
    blk = k[:, idx] + pe[:, None, :]
    flat = blk.transpose(0, 1, 3, 2, 4).reshape(bsz, n_blocks, NSA_N_KV, CMP_BLOCK * NSA_HEAD_DIM)
    return jax.nn.silu(flat @ w1) @ w2

def nsa_mix(q, q_start, kv_full, kvw_all, kw_pos0, pe, w1, w2, rel_bias):
    f32 = jnp.float32
    bsz, tq = q.shape[:2]
    t = kv_full.shape[1]
    g, r, dh = NSA_N_KV, NSA_HEADS_PER_KV, NSA_HEAD_DIM
    nc = (t - CMP_BLOCK) // CMP_STRIDE + 1
    kc = compress(kv_full[:, :, 0], pe[0], w1[0], w2[0], nc).astype(f32)
    vc = compress(kv_full[:, :, 1], pe[1], w1[1], w2[1], nc).astype(f32)
    c_start = jnp.arange(nc) * CMP_STRIDE
    c_end = c_start + CMP_BLOCK - 1
    ns = -(-t // SEL_BLOCK)
    s_ids = jnp.arange(ns)
    s_start = s_ids * SEL_BLOCK
    overlap = jnp.clip(jnp.minimum(c_end[:, None], s_start[None, :] + SEL_BLOCK - 1)
                       - jnp.maximum(c_start[:, None], s_start[None, :]) + 1, 0).astype(f32) / CMP_STRIDE
    sel = jnp.pad(kv_full[:, :, 2:4], ((0, 0), (0, ns * SEL_BLOCK - t), (0, 0), (0, 0), (0, 0)))
    sel = sel.reshape(bsz, ns, SEL_BLOCK, 2, g, dh).transpose(3, 0, 4, 1, 2, 5).astype(f32)
    ks_blk, vs_blk = sel[0], sel[1]
    qb_len = min(NSA_QBLOCK, tq)
    nqb = -(-tq // qb_len)
    pad_q = nqb * qb_len - tq
    kvw_pad = jnp.pad(kvw_all, ((0, 0), (WINDOW, qb_len), (0, 0), (0, 0), (0, 0))).astype(f32)
    q_p = jnp.pad(q, ((0, 0), (0, pad_q), (0, 0), (0, 0)))
    qblocks = q_p.reshape(bsz, nqb, qb_len, g, r, dh).swapaxes(0, 1)
    pblocks = (q_start + jnp.arange(nqb * qb_len)).reshape(nqb, qb_len)
    tab = rel_bias.astype(f32).reshape(REL_BUCKETS, g, r).transpose(1, 2, 0)
    k_top = min(SEL_TOPK, ns)
    scale = NSA_HEAD_DIM ** -0.5
    bi = jnp.arange(bsz)[:, None, None, None]
    gi = jnp.arange(g)[None, :, None, None]
    g6 = jnp.arange(g)[None, :, None, None, None, None]
    r6 = jnp.arange(r)[None, None, :, None, None, None]

    def block_step(args):
        qb, pb = args
        qg = qb.astype(f32) * scale
        dist_c = pb[:, None] - c_end[None, :]
        s_c = jnp.einsum('bqgrd,bcgd->bgrqc', qg, kc) + tab[:, :, rel_bucket(dist_c)]
        p_c = masked_softmax(s_c, dist_c >= 0)
        o_c = jnp.einsum('bgrqc,bcgd->bqgrd', p_c, vc)
        imp = jnp.einsum('bgrqc,cs->bgqs', p_c, overlap)
        cur = pb[:, None] // SEL_BLOCK
        forced = (s_ids[None] == 0) | (s_ids[None] == cur) | (s_ids[None] == cur - 1)
        imp = jnp.where(forced, FORCE_SCORE, imp)
        imp = jnp.where(s_start[None] <= pb[:, None], imp, -FORCE_SCORE)
        top_val, top_idx = lax.top_k(imp, k_top)
        top_ok = top_val > -0.5 * FORCE_SCORE
        k_sel = ks_blk[bi, gi, top_idx]
        v_sel = vs_blk[bi, gi, top_idx]
        dist_s = pb[None, None, :, None, None] - (top_idx[..., None] * SEL_BLOCK + jnp.arange(SEL_BLOCK))
        ok_s = (dist_s >= 0) & top_ok[..., None]
        s_s = jnp.einsum('bqgrd,bgqksd->bgrqks', qg, k_sel) + tab[g6, r6, rel_bucket(dist_s)[:, :, None]]
        shp = s_s.shape
        p_s = masked_softmax(s_s.reshape(shp[:4] + (k_top * SEL_BLOCK,)),
                             ok_s.reshape(bsz, g, 1, qb_len, k_top * SEL_BLOCK)).reshape(shp)
        o_s = jnp.einsum('bgrqks,bgqksd->bqgrd', p_s, v_sel)
        p0 = pb[0]
        kvw = lax.dynamic_slice_in_dim(kvw_pad, p0 - kw_pos0, WINDOW + qb_len, axis=1)
        kpos_w = p0 - WINDOW + jnp.arange(WINDOW + qb_len)
        dist_w = pb[:, None] - kpos_w[None, :]
        ok_w = (dist_w >= 0) & (dist_w <= WINDOW) & (kpos_w[None, :] >= kw_pos0)
        s_w = jnp.einsum('bqgrd,bkgd->bgrqk', qg, kvw[:, :, 0]) + tab[:, :, rel_bucket(dist_w)]
        p_w = masked_softmax(s_w, ok_w)
        o_w = jnp.einsum('bgrqk,bkgd->bqgrd', p_w, kvw[:, :, 1])
        return jnp.stack([o_c, o_s, o_w], axis=2)

    out = lax.map(block_step, (qblocks, pblocks))
    out = out.swapaxes(0, 1).reshape(bsz, nqb * qb_len, N_BRANCH, NSA_N_HEADS, dh)
    return out[:, :tq]

def nsa_layer(x, q_start, past_kv, past_win, norm_w, w_in, pe, w1, w2, w_out, rel_bias):
    f32 = jnp.float32
    bsz, t = x.shape[:2]
    g, dh, h = NSA_N_KV, NSA_HEAD_DIM, NSA_N_HEADS
    u = rmsnorm(x, norm_w) @ w_in
    cuts = np.cumsum([NSA_WIDTH, 4 * NSA_KV_WIDTH, 2 * NSA_KV_WIDTH, h * N_BRANCH]).tolist()
    q, kv, kvw, gate, z = jnp.split(u, cuts, axis=-1)
    q = q.reshape(bsz, t, h, dh)
    kv = kv.reshape(bsz, t, 4, g, dh)
    kvw = kvw.reshape(bsz, t, 2, g, dh)
    gate = jax.nn.sigmoid(gate.astype(f32)).reshape(bsz, t, h, N_BRANCH)
    z = z.reshape(bsz, t, N_BRANCH, h, dh).astype(f32)
    if past_kv is None:
        kv_full, kvw_all, kw_pos0 = kv, kvw, 0
    else:
        kv_full = jnp.concatenate([past_kv.astype(kv.dtype), kv], axis=1)
        kvw_all = jnp.concatenate([past_win.astype(kvw.dtype), kvw], axis=1)
        kw_pos0 = q_start - past_win.shape[1]
    o = nsa_mix(q, q_start, kv_full, kvw_all, kw_pos0, pe, w1, w2, rel_bias)
    mixed = jnp.einsum('btchd,bthc->bthd', o * jax.nn.silu(z), gate)
    y = x + mixed.reshape(bsz, t, NSA_WIDTH).astype(x.dtype) @ w_out
    return y, kv, kvw_all

def setup_inputs(seed: int = 0) -> dict:
    key = jax.random.key(seed)
    ks = jax.random.split(key, 24)
    f32 = jnp.float32
    n_pages = PAST_LEN // PAGE_SIZE
    used = DEC_BATCH * n_pages
    n_phys = used + max(1, used // 4)
    win_len = min(WINDOW, PAST_LEN)
    g, dh = NSA_N_KV, NSA_HEAD_DIM

    def nrm(k, shape, s):
        return (s * jax.random.normal(k, shape)).astype(f32)

    x_prompt = nrm(ks[0], (BATCH, SEQ, D_MODEL), 1.0)
    x_sample = nrm(ks[1], (DEC_BATCH, DEC_SEQ, D_MODEL), 1.0)
    state_ssm = nrm(ks[2], (N_SSD_LAYERS, DEC_BATCH, SSD_N_HEADS, SSD_HEAD_DIM, SSD_D_STATE), 0.1)
    state_conv = nrm(ks[3], (N_SSD_LAYERS, DEC_BATCH, SSD_CONV_W - 1, SSD_CONV_DIM), 1.0)
    cache_kv = nrm(ks[4], (n_phys, N_NSA_LAYERS, PAGE_SIZE, 4, g, dh), 1.0)
    cache_win = nrm(ks[5], (N_NSA_LAYERS, DEC_BATCH, win_len, 2, g, dh), 1.0)
    page_table = jax.random.permutation(ks[6], n_phys)[:used].reshape(DEC_BATCH, n_pages).astype(jnp.int32)
    rel_bias = nrm(ks[7], (REL_BUCKETS, NSA_N_HEADS), 0.2)
    final_norm = 1.0 + nrm(ks[8], (D_MODEL,), 0.01)
    ssd_norm = 1.0 + nrm(ks[9], (N_SSD_LAYERS, D_MODEL), 0.01)
    ssd_w_in = nrm(ks[10], (N_SSD_LAYERS, D_MODEL, SSD_IN_DIM), D_MODEL ** -0.5)
    ssd_conv_w = nrm(ks[11], (N_SSD_LAYERS, SSD_CONV_W, SSD_CONV_DIM), SSD_CONV_W ** -0.5)
    ssd_conv_b = nrm(ks[12], (N_SSD_LAYERS, SSD_CONV_DIM), 0.01)
    dt0 = jnp.exp(jax.random.uniform(ks[13], (N_SSD_LAYERS, SSD_N_HEADS), minval=math.log(1e-3), maxval=math.log(1e-1)))
    ssd_dt_bias = (dt0 + jnp.log(-jnp.expm1(-dt0))).astype(f32)
    ssd_a_log = jnp.log(jax.random.uniform(ks[14], (N_SSD_LAYERS, SSD_N_HEADS), minval=1.0, maxval=16.0)).astype(f32)
    ssd_d = 1.0 + nrm(ks[15], (N_SSD_LAYERS, SSD_N_HEADS), 0.01)
    ssd_gnorm = 1.0 + nrm(ks[16], (N_SSD_LAYERS, SSD_D_INNER), 0.01)
    ssd_w_out = nrm(ks[17], (N_SSD_LAYERS, SSD_D_INNER, D_MODEL), SSD_D_INNER ** -0.5)
    nsa_norm = 1.0 + nrm(ks[18], (N_NSA_LAYERS, D_MODEL), 0.01)
    nsa_w_in = nrm(ks[19], (N_NSA_LAYERS, D_MODEL, NSA_IN_DIM), D_MODEL ** -0.5)
    nsa_cmp_pe = nrm(ks[20], (N_NSA_LAYERS, 2, CMP_BLOCK, dh), 0.02)
    nsa_cmp_w1 = nrm(ks[21], (N_NSA_LAYERS, 2, CMP_BLOCK * dh, CMP_HIDDEN), (CMP_BLOCK * dh) ** -0.5)
    nsa_cmp_w2 = nrm(ks[22], (N_NSA_LAYERS, 2, CMP_HIDDEN, dh), CMP_HIDDEN ** -0.5)
    nsa_w_out = nrm(ks[23], (N_NSA_LAYERS, NSA_WIDTH, D_MODEL), NSA_WIDTH ** -0.5)
    return {'x_prompt': x_prompt, 'x_sample': x_sample, 'state_ssm': state_ssm, 'state_conv': state_conv,
            'cache_kv': cache_kv, 'cache_win': cache_win, 'page_table': page_table,
            'rel_bias': rel_bias, 'final_norm': final_norm,
            'ssd_norm': ssd_norm, 'ssd_w_in': ssd_w_in, 'ssd_conv_w': ssd_conv_w, 'ssd_conv_b': ssd_conv_b,
            'ssd_dt_bias': ssd_dt_bias, 'ssd_a_log': ssd_a_log, 'ssd_d': ssd_d, 'ssd_gnorm': ssd_gnorm,
            'ssd_w_out': ssd_w_out,
            'nsa_norm': nsa_norm, 'nsa_w_in': nsa_w_in, 'nsa_cmp_pe': nsa_cmp_pe, 'nsa_cmp_w1': nsa_cmp_w1,
            'nsa_cmp_w2': nsa_cmp_w2, 'nsa_w_out': nsa_w_out}

def reference(x_prompt, x_sample, state_ssm, state_conv, cache_kv, cache_win, page_table,
              rel_bias, final_norm,
              ssd_norm, ssd_w_in, ssd_conv_w, ssd_conv_b, ssd_dt_bias, ssd_a_log, ssd_d, ssd_gnorm, ssd_w_out,
              nsa_norm, nsa_w_in, nsa_cmp_pe, nsa_cmp_w1, nsa_cmp_w2, nsa_w_out):
    n_pages = page_table.shape[1]
    past_len = n_pages * PAGE_SIZE
    win_len_s = cache_win.shape[2]
    xp, xs = x_prompt, x_sample
    ssm_p, conv_p, kv_p, win_p = [], [], [], []
    ssm_s, conv_s, kv_s, win_s = [], [], [], []
    for layer in range(DEPTH):
        j = layer // N_MIXERS
        if layer % N_MIXERS == 0:
            prm = (ssd_norm[j], ssd_w_in[j], ssd_conv_w[j], ssd_conv_b[j], ssd_dt_bias[j], ssd_a_log[j],
                   ssd_d[j], ssd_gnorm[j], ssd_w_out[j])
            conv0 = jnp.zeros((xp.shape[0], SSD_CONV_W - 1, SSD_CONV_DIM), xp.dtype)
            ssm0 = jnp.zeros((xp.shape[0], SSD_N_HEADS, SSD_HEAD_DIM, SSD_D_STATE), xp.dtype)
            xp, c, s = ssd_layer(xp, conv0, ssm0, *prm)
            conv_p.append(c)
            ssm_p.append(s)
            xs, c, s = ssd_layer(xs, state_conv[j], state_ssm[j], *prm)
            conv_s.append(c)
            ssm_s.append(s)
        else:
            prm = (nsa_norm[j], nsa_w_in[j], nsa_cmp_pe[j], nsa_cmp_w1[j], nsa_cmp_w2[j], nsa_w_out[j], rel_bias)
            xp, kv, kvw_all = nsa_layer(xp, 0, None, None, *prm)
            kv_p.append(kv)
            win_p.append(kvw_all[:, -min(WINDOW, kvw_all.shape[1]):])
            past = cache_kv[page_table, j].reshape(xs.shape[0], past_len, 4, NSA_N_KV, NSA_HEAD_DIM)
            xs, kv, kvw_all = nsa_layer(xs, past_len, past, cache_win[j], *prm)
            kv_s.append(kv)
            win_s.append(kvw_all[:, -win_len_s:])
    y_prompt = rmsnorm(xp, final_norm)
    y_sample = rmsnorm(xs, final_norm)
    return (y_prompt, y_sample, jnp.stack(ssm_p), jnp.stack(conv_p), jnp.stack(kv_p, axis=2), jnp.stack(win_p),
            jnp.stack(ssm_s), jnp.stack(conv_s), jnp.stack(kv_s, axis=2), jnp.stack(win_s))


_drawn_inputs = setup_inputs


def setup_inputs(seed=0):
    import zlib

    import numpy as np

    out = dict(_drawn_inputs(seed))
    spreads = {}
    factors = {'rel_bias': 5.364,
     'final_norm': 200.0,
     'ssd_norm': 3.685,
     'ssd_conv_b': 3.58,
     'ssd_d': 183.366,
     'ssd_gnorm': 7.996,
     'nsa_norm': 5.823,
     'nsa_cmp_pe': 8.0}
    for name, (base, spread) in spreads.items():
        noise = np.random.default_rng([zlib.crc32(name.encode()), seed]).standard_normal(out[name].shape)
        drawn = base * np.exp(spread * noise) if base else spread * noise
        out[name] = __import__('jax').numpy.asarray(drawn.astype(out[name].dtype))
    for name, factor in factors.items():
        out[name] = (out[name] * factor).astype(out[name].dtype)
    return out
```

```python
from contextlib import ExitStack

import numpy as np

import concourse.bass as bass
from concourse import mybir

ALU = mybir.AluOpType
ACT = mybir.ActivationFunctionType
F32 = mybir.dt.float32
I32 = mybir.dt.int32
AX = mybir.AxisListType

P = 128
D = 1024
KT = D // P
SEQ = 512
NB = 8
T = SEQ + NB
HALF = T // 2
PAST = 1024
PAGE = 128
EPS = 1e-6
NEG = -1e30
GUARD = -1e20

DI = 2 * D
SH = 32
SP_ = 64
SG = 8
SN = 128
CH = 128
NCH = SEQ // CH
CONV = DI + 2 * SG * SN
IN1 = DI + CONV + SH
CT = CONV // P
TAPS = 4

NH = 16
G = 4
R = 4
DH = 64
AW = NH * DH
IN2 = AW + 6 * G * DH + 3 * NH + 3 * AW
GATE0 = AW + 6 * G * DH
Z0 = GATE0 + 3 * NH
NCP = (SEQ - 32) // 16 + 1
NCS = (PAST + 1 - 32) // 16 + 1
NPAIR = PAST // 2
NWP = 512 // 2
SKEYS = PAST + 1
WKEYS = 512 + 1
NSEL = 17
KEYS = SKEYS + WKEYS + NCS
FLEN = 1023

CA = {}
_n = 0
for _name, _w in (("ident", P), ("ones", P), ("swap", P), ("group", NH), ("overlap", NSEL), ("order", 14),
                  ("causal", P), ("last", P), ("head", 4 * P), ("pair", 2 * P), ("samp", NB * P)):
    CA[_name] = (_n, _n + _w)
    _n += _w
CA_W = _n
CB_F, CB_S, CB_W = 0, FLEN, FLEN + KEYS
PR_N1, PR_N2, PR_NF, PR_CB, PR_GN, PR_W = 0, 8, 16, 24, 56, 72


def buckets(dist):
    n = np.maximum(dist, 0)
    logv = np.log(np.maximum(n, 1).astype(np.float32) / np.float32(16)) / np.float32(np.log(64.0))
    large = np.minimum(16 + (logv.astype(np.float32) * np.float32(16)).astype(np.int32), 31)
    return np.where(n < 16, n, large)


def constants():
    a = np.zeros((P, CA_W), np.float32)

    def put(name, x):
        a[:x.shape[0], CA[name][0]:CA[name][0] + x.shape[1]] = x

    i = np.arange(P)
    put("ident", np.eye(P))
    put("ones", np.ones((P, P)))
    put("causal", (i[None, :] >= i[:, None]))
    put("swap", (i[None, :] == (i[:, None] + 64) % P))
    put("last", np.repeat((i == P - 1)[:, None], P, 1))
    put("head", np.repeat(np.eye(4), P, 1))
    put("pair", np.stack([(np.arange(4)[:, None] == 2 * hp + i[None, :] // 64) for hp in range(2)], 1).reshape(4, -1))
    put("samp", np.repeat(np.eye(NB), P, 1))
    put("group", np.kron(np.eye(G), np.ones((R, R))))
    c0 = np.arange(NCS) * 16
    s0 = np.arange(NSEL) * 64
    ov = np.minimum(c0[:, None] + 31, s0[None] + 63) - np.maximum(c0[:, None], s0[None]) + 1
    put("overlap", np.maximum(ov, 0) / 16.0)
    put("order", np.repeat(np.arange(1, 15)[None], NH, 0))
    b = np.zeros((33, CB_W), np.float32)

    def onehot(at, dist):
        row = np.where(dist < 0, 32, buckets(dist))
        b[row, at + np.arange(len(dist))] = 1

    onehot(CB_F, np.arange(FLEN) - 511)
    pairs = np.arange(NPAIR)
    wp = np.arange(NWP)
    pos = np.concatenate([2 * pairs, 2 * pairs + 1, [PAST], PAST - 512 + 2 * wp, PAST - 512 + 2 * wp + 1, [PAST],
                          c0 + 31])
    onehot(CB_S, PAST - pos)
    return a, b


class Signal:

    def __init__(self, sem, per):
        self.sem, self.per, self.count = sem, per, 0

    def at(self, turn, n):
        return turn * self.per + n


class Steps:

    def __init__(self, eng, own):
        self.eng, self.own, self.used = eng, own, []

    def turn(self, i):
        for s in self.used:
            assert s.count == s.per, (s.sem, s.count, s.per)
            s.count = 0
        self.i, self.used = i, []

    def post(self, ins, sig=None):
        s = sig or self.own
        if s not in self.used:
            self.used.append(s)
        s.count += 1
        ins.then_inc(s.sem, 1)
        return s

    def link(self, ins, sig=None):
        s = self.post(ins, sig)
        self.eng.wait_ge(s.sem, s.at(self.i, s.count))


class Arena:

    def __init__(self, block, size):
        self.block, self.size, self.at = block, size, 0

    def take(self, n):
        a = self.at
        self.at += n
        assert self.at <= self.size, (self.at, self.size)
        return self.block[:, a:a + n]


def halves(psum, bank, parts=P):
    return psum[0:parts, bank:bank + 2, 0:HALF]


def build(nc, io):
    ctx = ExitStack()
    with ctx:
        _build(nc, io, ctx)


def _build(nc, io, ctx):
    stage_sems = []

    def sem(name):
        stage_sems.append(nc.alloc_semaphore(name=name))
        return stage_sems[-1]

    def free_semaphores():
        nc.clear_and_free_semaphores(stage_sems)
        nc.all_engine_barrier()
        stage_sems.clear()

    def sig(name, per=1):
        return Signal(sem(name), per)

    ARENA = 52200
    arena = Arena(ctx.enter_context(nc.sbuf_tensor("arena", [P, ARENA], F32)), ARENA)
    take = arena.take
    psum = ctx.enter_context(nc.psum_tensor("psum", [P, 8, 512], F32))

    scr_rows = nc.dram_tensor("scr_rows", [SH, 2, T], F32).ap()
    scr_f = nc.dram_tensor("scr_f", [NH, FLEN], F32).ap()
    scr_s = nc.dram_tensor("scr_s", [NH, KEYS], F32).ap()

    scr_new = nc.dram_tensor("scr_new", [NB, 6, G, DH], F32).ap()

    ca = take(CA_W)

    def const(name, rows=P):
        return ca[0:rows, CA[name][0]:CA[name][1]]

    ident, ones = const("ident"), const("ones")
    pT = take(PR_W)
    xT = take(KT * T).rearrange("p (k t) -> p k t", k=KT)
    xn_at = arena.at
    xn = take(KT * T).rearrange("p (k t) -> p k t", k=KT)
    base_all = arena.at

    cw = take(P)
    dsk = take(DI // P)
    st = take(CT * NB * 3).rearrange("p (c b t) -> p c b t", c=CT, b=NB)
    tail = take(CT * 11).rearrange("p (c n) -> p c n", c=CT)
    acs_tok = take(NCH * SH).rearrange("p (c h) -> p c h", c=NCH)
    toend = take(NCH * SH).rearrange("p (c h) -> p c h", c=NCH)
    decay = take(NCH * SH).rearrange("p (c h) -> p c h", c=NCH)
    base_ssd = arena.at

    cb = take(CB_W)
    xtok = take(4 * D).rearrange("p (a d) -> p a d", a=4)
    xsmp = take(D)
    prow = take(P)
    crow = take(P)
    srow = take(CONV)
    drow = take(16)
    rel = take(NH)
    brow = take(CB_W)
    hcol = take(3)
    wdt = take(KT * SH).rearrange("p (k n) -> p k n", k=KT)
    raw_dt = take(T)
    low = take(T)
    rows = take(2 * T).rearrange("p (r t) -> p r t", r=2)
    dta = take(T)
    std = take(T)
    rstd = take(T)

    ld_const, ld_x, ld_prm, ld_conv, ld_rel, ld_dt = (sem(n) for n in (
        "ld_const", "ld_x", "ld_prm", "ld_conv", "ld_rel", "ld_dt"))
    st_scr = sem("st_scr")
    st_pass = sem("st_pass")
    job_done, job_out = sem("job_done"), sem("job_out")
    sq_done, ssq_done, var_done, std_done, xn_done = (sem(n) for n in (
        "sq_done", "ssq_done", "var_done", "std_done", "xn_done"))
    rel_mask = sem("rel_mask")
    dtraw_done, dtlow_done, dtln_done, dta_done, rows_done, acs_done, acst_done, last_done, te_done, dec_done = (
        sem(n) for n in ("dtraw_done", "dtlow_done", "dtln_done", "dta_done", "rows_done", "acs_done",
                         "acst_done", "last_done", "te_done", "dec_done"))
    own = {e: {s: Signal(sem(f"{e}_own_{s}"), 1) for s in ("setup", "tail")} for e in ("act", "dve")}

    pieces = [(a, min(a + 512, b)) for lo, b in ((CB_F, CB_S), (CB_S, CB_W)) for a in range(lo, b, 512)]
    jobs = []

    def bank(j):
        return psum[:, j % 8, :]

    def tr(out, in_, k):
        return nc.tensor.transpose(out, in_, ident[0:k, 0:k])

    for kt in range(KT):
        jobs.append((lambda b, kt=kt: [tr(b[:, a * P:(a + 1) * P], xtok[:, a, kt * P:(kt + 1) * P], P)
                                       for a in range(4)],
                     xT[:, kt, 0:SEQ], lambda b: b, (ld_x, 32)))
    jobs.append((lambda b: [tr(b[:, kt * NB:(kt + 1) * NB], xsmp[0:NB, kt * P:(kt + 1) * P], NB) for kt in range(KT)],
                 xT[:, :, SEQ:T], lambda b: b[:, 0:KT * NB].rearrange("p (k b) -> p k b", k=KT), (ld_x, 32)))
    jobs.append((lambda b: [tr(b[:, 0:PR_W], prow[0:PR_W, :], PR_W)], pT, lambda b: b[:, 0:PR_W], (ld_prm, 128)))
    n_norm = len(jobs)
    jobs.append((lambda b: [tr(b[:, 0:P], crow, P)], cw, lambda b: b[:, 0:P], (ld_prm, 128)))
    jobs.append((lambda b: [nc.tensor.matmul(b[:, 0:16], const("pair", 2)[:, 0:P], drow[0:2, :], start=True, stop=True)],
                 dsk, lambda b: b[:, 0:16], (ld_prm, 128)))
    for lo, hi in ((0, 16), (16, 32)):
        jobs.append((lambda b, lo=lo, hi=hi: [tr(b[:, (c - lo) * 24:(c - lo + 1) * 24], srow[0:24, c * P:(c + 1) * P], 24)
                                              for c in range(lo, hi)],
                     st[:, lo:hi], lambda b: b[:, 0:16 * 24].rearrange("p (c b t) -> p c b t", c=16, b=NB), (ld_conv, 16)))
    for lo, hi in pieces:
        jobs.append((lambda b, lo=lo, hi=hi: [nc.tensor.matmul(b[0:NH, 0:hi - lo], rel[0:33, :], cb[0:33, lo:hi],
                                                               start=True, stop=True)],
                     brow[0:NH, lo:hi], lambda b, lo=lo, hi=hi: b[0:NH, 0:hi - lo], (ld_rel, 32)))

    def norm_act_squares(act, own_s):
        for k in range(KT):
            own_s.post(nc.scalar.activation(xn[:, k, :], xT[:, k, :], ACT.Square), own_s.sq)

    with nc.Block() as block:
        @block.sync
        def _(sp):
            sp.dma_start(ca, io["const_a"]).then_inc(ld_const, 16)
            sp.dma_start(xtok, io["x_prompt"][0].rearrange("(a p) d -> p a d", p=P)).then_inc(ld_x, 16)
            sp.dma_start(xsmp[0:NB, :], io["x_sample"].rearrange("b s d -> (b s) d")).then_inc(ld_x, 16)
            for at, name, n in ((PR_N1, "ssd_norm", 8), (PR_N2, "nsa_norm", 8), (PR_CB, "ssd_conv_b", 32),
                                (PR_GN, "ssd_gnorm", 16)):
                sp.dma_start(prow[at:at + n, :], io[name][0].rearrange("(r c) -> r c", c=P)).then_inc(ld_prm, 16)
            sp.dma_start(prow[PR_NF:PR_NF + 8, :], io["final_norm"].rearrange("(r c) -> r c", c=P)).then_inc(ld_prm, 16)
            sp.dma_start(crow[:, :], io["ssd_conv_w"][0].rearrange("k (r c) -> (k r) c", c=P)).then_inc(ld_prm, 16)
            for h2 in range(2):
                sp.dma_start(drow[h2:h2 + 1, :], bass.AP(io["ssd_d"].tensor, h2, [[SH, 1], [2, 16]]),
                             allow_slow_non_contiguous=True).then_inc(ld_prm, 16)
            for c, name in enumerate(("ssd_dt_bias", "ssd_a_log")):
                sp.dma_start(hcol[0:SH, c:c + 1], io[name].rearrange("a h -> h a"),
                             allow_slow_non_contiguous=True).then_inc(ld_dt, 16)
            sp.dma_start(wdt, io["ssd_w_in"][0][:, IN1 - SH:IN1].rearrange("(k p) n -> p k n", p=P)).then_inc(ld_dt, 16)
            sp.dma_start(srow[0:24, :], io["state_conv"][0].rearrange("b t c -> (b t) c")).then_inc(ld_conv, 16)
            sp.dma_start(cb[0:33, :], io["const_b"]).then_inc(ld_rel, 16)
            sp.dma_start(rel[0:32, :], io["rel_bias"]).then_inc(ld_rel, 16)
            sp.dma_start(io["conv_sample"][0][:, 0:2, :], io["state_conv"][0][:, 1:3, :]).then_inc(st_pass, 16)
            for b in range(NB):
                sp.dma_start(io["win_sample"][0][b, 0:511].rearrange("t k g d -> t (k g d)"),
                             io["cache_win"][0][b, 1:512].rearrange("t k g d -> t (k g d)")).then_inc(st_pass, 16)
            sp.wait_ge(job_out, len(jobs))
            sp.dma_start(scr_f, brow[0:NH, CB_F:CB_S]).then_inc(st_scr, 16)
            sp.dma_start(scr_s, brow[0:NH, CB_S:CB_W]).then_inc(st_scr, 16)
            sp.wait_ge(rows_done, 6)
            sp.dma_start(scr_rows, rows[0:SH]).then_inc(st_scr, 16)
            sp.wait_ge(st_scr, 48)

        @block.tensor
        def _(pe):
            pe.wait_ge(ld_const, 16)
            for j, (emit, _dst, _src, (s, v)) in enumerate(jobs):
                pe.wait_ge(s, v)
                if s is ld_rel:
                    pe.wait_ge(rel_mask, 1)
                if j >= 8:
                    pe.wait_ge(job_out, j - 7)
                emit(bank(j))[-1].then_inc(job_done, 1)
                if j == n_norm:
                    break
            pe.wait_ge(sq_done, KT)
            pe.wait_ge(job_out, n_norm)
            for h in range(2):
                for k in range(KT):
                    mm = nc.tensor.matmul(psum[:, 6 + h, 0:HALF], ones, xn[:, k, h * HALF:(h + 1) * HALF],
                                          start=(k == 0), stop=(k == KT - 1))
            mm.then_inc(ssq_done, 1)
            pe.wait_ge(xn_done, KT)
            pe.wait_ge(ld_dt, 48)
            for h in range(2):
                for k in range(KT):
                    mm = nc.tensor.matmul(psum[0:SH, 4 + h, 0:HALF], wdt[:, k, :], xn[:, k, h * HALF:(h + 1) * HALF],
                                          start=(k == 0), stop=(k == KT - 1))
            mm.then_inc(dtraw_done, 1)
            for j, (emit, _dst, _src, (s, v)) in enumerate(jobs):
                if j <= n_norm:
                    continue
                pe.wait_ge(s, v)
                if s is ld_rel:
                    pe.wait_ge(rel_mask, 1)
                pe.wait_ge(job_out, j if j <= n_norm + 4 else j - 3)
                emit(psum[:, j % 4, :])[-1].then_inc(job_done, 1)
            pe.wait_ge(rows_done, 6)
            for c in range(NCH):
                mm = tr(psum[:, 4, c * SH:(c + 1) * SH], rows[0:SH, 1, c * CH:(c + 1) * CH], SH)
            mm.then_inc(acs_done, 1)
            pe.wait_ge(acst_done, 1)
            nc.tensor.matmul(psum[:, 5, 0:NCH * SH], const("last"), acs_tok, start=True, stop=True).then_inc(last_done, 1)

        @block.scalar
        def _(act):
            def job_evac(j):
                act.wait_ge(job_done, j + 1)
                b = bank(j) if j <= n_norm else psum[:, j % 4, :]
                nc.scalar.activation(jobs[j][1], jobs[j][2](b), ACT.Copy).then_inc(job_out, 1)

            for j in range(n_norm + 1):
                job_evac(j)
            act.wait_ge(job_out, n_norm)
            for k in range(KT):
                nc.scalar.activation(xn[:, k, :], xT[:, k, :], ACT.Square).then_inc(sq_done, 1)
            act.wait_ge(var_done, 1)
            nc.scalar.activation(std, std, ACT.Sqrt).then_inc(std_done, 1)
            for j in range(n_norm + 1, len(jobs)):
                job_evac(j)
            s = Steps(act, Signal(own["act"]["setup"].sem, 4))
            s.turn(0)
            act.wait_ge(ld_dt, 48)
            s.post(nc.scalar.activation(hcol[0:SH, 2:3], hcol[0:SH, 1:2], ACT.Exp))
            act.wait_ge(dtlow_done, 1)
            s.link(nc.scalar.activation(low[0:SH, :], low[0:SH, :], ACT.Exp))
            nc.scalar.activation(low[0:SH, :], low[0:SH, :], ACT.Ln, bias=1.0).then_inc(dtln_done, 1)
            act.wait_ge(last_done, 1)
            nc.scalar.activation(decay, psum[:, 5, 0:NCH * SH].rearrange("p (c h) -> p c h", c=NCH), ACT.Exp).then_inc(dec_done, 1)
            act.wait_ge(te_done, 1)
            nc.scalar.activation(toend, toend, ACT.Exp).then_inc(dec_done, 1)
            act.wait_ge(dec_done, 2)

        @block.vector
        def _(dve):
            nc.vector.memset(rel[32:33, :], NEG).then_inc(rel_mask, 1)
            dve.wait_ge(ssq_done, 1)
            nc.vector.tensor_scalar(std.rearrange("p (h t) -> p h t", h=2), halves(psum, 6), 1.0 / D, EPS,
                                    ALU.mult, ALU.add).then_inc(var_done, 1)
            dve.wait_ge(std_done, 1)
            s = Steps(dve, Signal(own["dve"]["setup"].sem, 3))
            s.turn(0)
            s.link(nc.vector.reciprocal(rstd, std))
            for k in range(KT):
                nc.vector.scalar_tensor_tensor(xn[:, k, :], xT[:, k, :], pT[:, PR_N1 + k:PR_N1 + k + 1], rstd,
                                               ALU.mult, ALU.mult).then_inc(xn_done, 1)
            dve.wait_ge(dtraw_done, 1)
            s.link(nc.vector.tensor_scalar(raw_dt[0:SH, :].rearrange("p (h t) -> p h t", h=2), halves(psum, 4, SH),
                                           hcol[0:SH, 0:1], None, ALU.add))
            nc.vector.scalar_tensor_tensor(low[0:SH, :], raw_dt[0:SH, :], -1.0, raw_dt[0:SH, :],
                                           ALU.mult, ALU.min).then_inc(dtlow_done, 1)
            dve.wait_ge(dtln_done, 1)
            nc.vector.scalar_tensor_tensor(rows[0:SH, 0, :], raw_dt[0:SH, :], 0.0, low[0:SH, :],
                                           ALU.max, ALU.add).then_inc(rows_done, 1)
            dve.wait_ge(rows_done, 1)
            s.link(nc.vector.tensor_scalar(dta[0:SH, :], rows[0:SH, 0, :], hcol[0:SH, 2:3], -1.0, ALU.mult, ALU.mult))
            for c in range(NCH):
                nc.vector.tensor_tensor_scan(rows[0:SH, 1, c * CH:(c + 1) * CH], ones[0:SH, :],
                                             dta[0:SH, c * CH:(c + 1) * CH], 0.0, ALU.mult, ALU.add).then_inc(rows_done, 1)
            nc.vector.tensor_copy(rows[0:SH, 1, SEQ:T], dta[0:SH, SEQ:T]).then_inc(rows_done, 1)
            dve.wait_ge(acs_done, 1)
            nc.vector.tensor_copy(acs_tok, psum[:, 4, 0:NCH * SH].rearrange("p (c h) -> p c h", c=NCH)).then_inc(acst_done, 1)
            dve.wait_ge(acst_done, 1)
            dve.wait_ge(dec_done, 1)
            nc.vector.tensor_tensor(toend, psum[:, 5, 0:NCH * SH].rearrange("p (c h) -> p c h", c=NCH), acs_tok,
                                    ALU.subtract).then_inc(te_done, 1)


    arena.at = base_ssd
    yT = take(DI // P * T).rearrange("p (k t) -> p k t", k=DI // P)
    base_y = arena.at
    wx = take(KT * 256).rearrange("p (k n) -> p k n", k=KT)
    wbc = take(KT * 256).rearrange("p (k n) -> p k n", k=KT)
    wz = take(KT * 256).rearrange("p (k n) -> p k n", k=KT)
    raw = take(4 * (3 + T)).rearrange("p (c t) -> p c t", c=4)
    zraw = take(2 * T).rearrange("p (c t) -> p c t", c=2)
    zs = take(2 * T).rearrange("p (c t) -> p c t", c=2)
    acts = [take(4 * T).rearrange("p (c t) -> p c t", c=4) for _ in range(2)]
    xdtT = take(2 * T).rearrange("p (c t) -> p c t", c=2)
    xdt = take(NCH * 256).rearrange("p (c n) -> p c n", c=NCH)
    xdte = take(NCH * 256).rearrange("p (c n) -> p c n", c=NCH)
    btok = take(NCH * P).rearrange("p (c n) -> p c n", c=NCH)
    cbm = take(NCH * P).rearrange("p (c n) -> p c n", c=NCH)
    grow = take(2 * T).rearrange("p (r t) -> p r t", r=2)
    eexp = take(2 * T).rearrange("p (c t) -> p c t", c=2)
    hT = take(NCH * 256).rearrange("p (c n) -> p c n", c=NCH)
    seg = [take(SEQ).rearrange("p (c n) -> p c n", c=NCH) for _ in range(2)]
    y = take(2 * T).rearrange("p (c t) -> p c t", c=2)
    ytmp = take(2 * T).rearrange("p (c t) -> p c t", c=2)
    gstd = take(T)
    bcs = take(256)
    sst = take(NB * 256).rearrange("p (b q n) -> p b q n", b=NB, q=2)
    stmp = take(1024)
    ysmp = take(NB * 2).rearrange("p (b q) -> p b q", b=NB)
    hfin = take(256).rearrange("p (q n) -> p q n", q=2)

    ld_wx, ld_wbc, ld_wz, ld_row, ld_sst = (sem(n) for n in ("ld_wx", "ld_wbc", "ld_wz", "ld_row", "ld_sst"))
    st_hfin, st_sst = sem("st_hfin"), sem("st_sst")
    tile_full = sig("tile_full", 6)
    tile_out = sig("tile_out", 6)
    raw_zero = sem("raw_zero")
    init_x, conv_x_done, x_ready = sig("init_x"), sig("conv_x_done"), sig("x_ready")
    init_bc, conv_bc_done, bc_ready = sig("init_bc"), sig("conv_bc_done"), sig("bc_ready")
    z_ready = sig("z_ready")
    dtb_full, xdt_done, e_full, e_ready = sig("dtb_full"), sig("xdt_done"), sig("e_full"), sig("e_ready")
    tok_full, tok_out, tokx_done, cbm_done = sig("tok_full"), sig("tok_out"), sig("tokx_done"), sig("cbm_done")
    bc_out = sig("bc_out")
    state_full, h_done = sig("state_full"), sig("h_done")
    yoff_full, yoff_used = sig("yoff_full"), sig("yoff_used")
    sum_full, seg_done, dec_ready, mt_done, mt_used = (
        sig("sum_full", 4), sig("seg_done", 4), sig("dec_ready", 4), sig("mt_done", 4), sig("mt_used", 4))
    sbc_full, sbc_out, row_full, row_used = sig("sbc_full"), sig("sbc_out"), sig("row_full", 2), sig("row_used", 2)
    sdec_done, sst_done = sig("sdec_done"), sig("sst_done")
    hfin_full, hfin_out = sig("hfin_full"), sig("hfin_out")
    gated, sqg_done, ssg_full, varg_done, stdg_done, yt_done = (
        sig("gated"), sig("sqg_done"), sig("ssg_full"), sig("varg_done"), sig("stdg_done"), sig("yt_done"))
    dve_own, dve_x, dve_bc, dve_norm = sig("dve_ssd", 14), sig("dve_x", 2), sig("dve_bc", 2), sig("dve_norm")
    CB_ = PR_CB

    w_in = io["ssd_w_in"][0].rearrange("(k p) n -> p k n", p=P)
    ssm_in = io["state_ssm"][0].rearrange("b (g q h) p n -> g (h p) b q n", g=SG, q=2)
    ssm_out = io["ssm_sample"][0].rearrange("b (g q h) p n -> g (h p) b q n", g=SG, q=2)
    ssm_prompt = io["ssm_prompt"][0, 0].rearrange("(g q h) p n -> g (h p) q n", g=SG, q=2)

    carrier = sem("carrier")

    with nc.Block() as block:
        @block.sync
        def _(sp):
            def weights_x(g):
                sp.dma_start(wx, w_in[:, :, bass.ds(g * 256 + DI, 256)]).then_inc(ld_wx, 16)

            def weights_bc(g):
                sp.dma_start(wbc[:, :, 0:P], w_in[:, :, bass.ds(g * P + 2 * DI, P)]).then_inc(ld_wbc, 16)
                sp.dma_start(wbc[:, :, P:256], w_in[:, :, bass.ds(g * P + 2 * DI + SG * SN, P)]).then_inc(ld_wbc, 16)

            def weights_z(g):
                sp.dma_start(wz, w_in[:, :, bass.ds(g * 256, 256)]).then_inc(ld_wz, 16)

            weights_x(0)
            weights_bc(0)
            weights_z(0)
            with sp.Fori(0, SG - 1) as i:
                sp.wait_ge(tile_full.sem, tile_full.at(i, 2))
                weights_x(i + 1)
                sp.wait_ge(tile_full.sem, tile_full.at(i, 4))
                weights_bc(i + 1)
                sp.wait_ge(tile_full.sem, tile_full.at(i, 6))
                sp.sem_inc(carrier, 1)
                weights_z(i + 1)

        @block.gpsimd
        def _(pool):
            nc.gpsimd.memset(raw[:, :, 0:3], 0.0).then_inc(raw_zero, 1)

            def load_rows(i):
                pool.dma_start(grow[0:4], scr_rows[bass.ds(i * 4, 4)]).then_inc(ld_row, 16)

            def load_states(i):
                for q in range(2):
                    pool.dma_start(sst[:, :, q], ssm_in[bass.ds(i, 1), :, :, q].rearrange("o p b n -> (o p) b n"))\
                        .then_inc(ld_sst, 16)

            def turn(i, more=True):
                pool.wait_ge(e_ready.sem, e_ready.at(i, 1))
                pool.wait_ge(ld_sst, i * 32 + 32)
                nc.gpsimd.tensor_tensor(sst, sst, eexp[:, :, SEQ:T].rearrange("p q b -> p b q").unsqueeze(3)
                                        .to_broadcast([P, NB, 2, SN]), ALU.mult).then_inc(sdec_done.sem, 1)
                if more:
                    pool.wait_ge(sum_full.sem, sum_full.at(i, 4))
                    pool.sem_inc(carrier, 1)
                    load_rows(i + 1)
                pool.wait_ge(hfin_out.sem, hfin_out.at(i, 1))
                pool.sem_inc(carrier, 1)
                pool.dma_start(ssm_prompt[bass.ds(i, 1)].rearrange("o p q n -> (o p) q n"), hfin).then_inc(st_hfin, 16)
                pool.wait_ge(sst_done.sem, sst_done.at(i, 1))
                pool.wait_ge(row_used.sem, row_used.at(i, 2))
                pool.sem_inc(carrier, 1)
                for q in range(2):
                    pool.dma_start(ssm_out[bass.ds(i, 1), :, :, q].rearrange("o p b n -> (o p) b n"), sst[:, :, q])\
                        .then_inc(st_sst, 16)
                if more:
                    pool.wait_ge(st_sst, i * 32 + 32)
                    pool.sem_inc(carrier, 1)
                    load_states(i + 1)

            load_rows(0)
            load_states(0)
            turn(0)
            with pool.Fori(1, SG - 1) as i:
                turn(i)
            turn(SG - 1, more=False)
            pool.wait_ge(st_hfin, 16 * SG)
            pool.wait_ge(st_sst, 32 * SG)

        @block.tensor
        def _(pe):
            def project(g, n, first=False, part=None):
                w, s, per = ((wx, ld_wx, 16), (wbc, ld_wbc, 32), (wz, ld_wz, 16))[n // 2]
                if part != 1:
                    if n % 2 == 0:
                        pe.wait_ge(s, g * per + per)
                    if not (first and n < 2):
                        pe.wait_ge(tile_out.sem, tile_out.at(g, n - 1))
                b = n % 2 * 2
                for h in range(2) if part is None else (part,):
                    for k in range(KT):
                        mm = nc.tensor.matmul(psum[:, b + h, 0:HALF], w[:, k, n % 2 * P:(n % 2 + 1) * P],
                                              xn[:, k, h * HALF:(h + 1) * HALF], start=(k == 0), stop=(k == KT - 1))
                if part != 0:
                    mm.then_inc(tile_full.sem, 1)

            def rows_to_pairs(i, r, done):
                for q in range(2):
                    for h in range(2):
                        mm = nc.tensor.matmul(psum[:, 4 + 2 * q + h, 0:HALF], const("pair", 4)[:, q * P:(q + 1) * P],
                                              grow[0:4, r, h * HALF:(h + 1) * HALF], start=True, stop=True)
                mm.then_inc(done.sem, 1)

            def turn(i, j, more=True, first=False):
                act_ = acts[j]

                def nxt(n, part=None):
                    if more:
                        project(i + 1, n, part=part)

                pe.wait_ge(ld_row, i * 16 + 16)
                if not first:
                    pe.wait_ge(varg_done.sem, varg_done.at(i, 0))
                    pe.wait_ge(hfin_out.sem, hfin_out.at(i, 0))
                rows_to_pairs(i, 0, dtb_full)
                nxt(0, 0)
                pe.wait_ge(xdt_done.sem, xdt_done.at(i, 1))
                rows_to_pairs(i, 1, e_full)
                nxt(0, 1)
                nxt(1, 0)
                pe.wait_ge(bc_ready.sem, bc_ready.at(i, 1))
                pe.wait_ge(e_ready.sem, e_ready.at(i, 1))
                for c in range(NCH):
                    for q in range(2):
                        tr(psum[:, 4 + c // 2, (c % 2) * 256 + q * P:(c % 2) * 256 + (q + 1) * P],
                           xdtT[:, q, c * CH:(c + 1) * CH], P)
                for c in range(NCH):
                    tr(psum[:, 6, c * CH:(c + 1) * CH], act_[:, 2, c * CH:(c + 1) * CH], P)
                for c in range(NCH):
                    mm = nc.tensor.matmul(psum[:, 7, c * CH:(c + 1) * CH], act_[:, 2, c * CH:(c + 1) * CH],
                                          act_[:, 3, c * CH:(c + 1) * CH], start=True, stop=True)
                mm.then_inc(tok_full.sem, 1)
                nxt(1, 1)
                nxt(2, 0)
                pe.wait_ge(tok_out.sem, tok_out.at(i, 1))
                pe.wait_ge(bc_out.sem, bc_out.at(i, 1))
                pe.wait_ge(tokx_done.sem, tokx_done.at(i, 1))
                for c in range(NCH):
                    mm = nc.tensor.matmul(psum[:, 4 + c // 2, (c % 2) * 256:(c % 2) * 256 + 256], btok[:, c, :],
                                          xdte[:, c, :], start=True, stop=True)
                mm.then_inc(state_full.sem, 1)
                tr(psum[0:NB, 6, 0:P], act_[:, 2, SEQ:T], P)
                tr(psum[0:NB, 6, P:256], act_[:, 3, SEQ:T], P).then_inc(sbc_full.sem, 1)
                nxt(2, 1)
                pe.wait_ge(sbc_out.sem, sbc_out.at(i, 1))
                pe.wait_ge(h_done.sem, h_done.at(i, 1))
                pe.wait_ge(cbm_done.sem, cbm_done.at(i, 1))
                for q in range(2):
                    for c in range(1, NCH):
                        mm = nc.tensor.matmul(psum[:, 6 + q, c * CH:(c + 1) * CH], hT[:, c - 1, q * P:(q + 1) * P],
                                              act_[:, 3, c * CH:(c + 1) * CH], start=True, stop=True)
                mm.then_inc(yoff_full.sem, 1)
                for r in range(2):
                    if r:
                        pe.wait_ge(row_used.sem, row_used.at(i, 1))
                    for b in range(4):
                        mm = nc.tensor.matmul(psum[:, 4 + b // 2, (b % 2) * 256:(b % 2) * 256 + 256],
                                              const("samp", NB)[:, (4 * r + b) * P:(4 * r + b + 1) * P], bcs[0:NB, :],
                                              start=True, stop=True)
                    mm.then_inc(row_full.sem, 1)
                    nxt(3, r)

                def sums(h):
                    if h >= 2:
                        pe.wait_ge(seg_done.sem, seg_done.at(i, h - 1))
                    nc.tensor.matmul(psum[:, 4 + h % 2, :], const("head", 4)[:, h * P:(h + 1) * P], grow[0:4, 1, 0:SEQ],
                                     start=True, stop=True).then_inc(sum_full.sem, 1)

                def within(h):
                    pe.wait_ge(mt_done.sem, mt_done.at(i, h + 1))
                    if h == 0:
                        pe.wait_ge(yoff_used.sem, yoff_used.at(i, 1))
                    a = h % 2 * 64
                    for c in range(NCH):
                        mm = nc.tensor.matmul(psum[a:a + 64, 6 + h // 2, c * CH:(c + 1) * CH],
                                              xdt[:, c, h * 64:(h + 1) * 64], seg[h % 2][:, c, :], start=True, stop=True)
                    mm.then_inc(mt_used.sem, 1)

                pe.wait_ge(row_used.sem, row_used.at(i, 2))
                sums(0)
                sums(1)
                nxt(4, 0)
                within(0)
                sums(2)
                nxt(4, 1)
                within(1)
                sums(3)
                nxt(5, 0)
                within(2)
                within(3)
                pe.wait_ge(seg_done.sem, seg_done.at(i, 4))
                tr(psum[:, 5, 0:P], hT[:, NCH - 1, 0:P], P)
                tr(psum[:, 5, P:256], hT[:, NCH - 1, P:256], P).then_inc(hfin_full.sem, 1)
                nxt(5, 1)
                pe.wait_ge(sqg_done.sem, sqg_done.at(i, 1))
                for h in range(2):
                    for q in range(2):
                        mm = nc.tensor.matmul(psum[:, 6 + h, 0:HALF], ones, ytmp[:, q, h * HALF:(h + 1) * HALF],
                                              start=(q == 0), stop=(q == 1))
                mm.then_inc(ssg_full.sem, 1)

            for n in range(6):
                project(0, n, True)
            turn(0, 0, first=True)
            with pe.Fori(0, SG // 2 - 1) as i:
                turn(i * 2 + 1, 1)
                turn(i * 2 + 2, 0)
            turn(SG - 1, 1, more=False)

        @block.scalar
        def _(act):
            def evacuate(g, n):
                act.wait_ge(tile_full.sem, tile_full.at(g, n + 1))
                dst = raw[:, n, 3:3 + T] if n < 4 else zraw[:, n - 4, :]
                nc.scalar.activation(dst.rearrange("p (h t) -> p h t", h=2), halves(psum, n % 2 * 2),
                                     ACT.Copy).then_inc(tile_out.sem, 1)

            def last_tap(g, j, tiles, done):
                act.wait_ge(tile_out.sem, tile_out.at(g, tiles[-1] + 1))
                for c in tiles:
                    ct = (g * 2, g * 2 + 1, g + 16, g + 24)[c]
                    ins = nc.scalar.activation(acts[j][:, c, :], raw[:, c, 3:3 + T], ACT.Identity,
                                               bias=pT[:, bass.ds(ct + CB_, 1)], scale=cw[:, bass.ds(ct + 96, 1)])
                ins.then_inc(done.sem, 1)

            def turn(i, j, more=True, first=False):
                def nxt(n):
                    if more:
                        evacuate(i + 1, n)

                act_ = acts[j]
                act.wait_ge(conv_x_done.sem, conv_x_done.at(i, 1))
                nc.scalar.activation(act_[:, 0:2], act_[:, 0:2], ACT.Silu).then_inc(x_ready.sem, 1)
                act.wait_ge(tile_out.sem, tile_out.at(i, 6))
                nc.scalar.activation(zs, zraw, ACT.Silu).then_inc(z_ready.sem, 1)
                act.wait_ge(conv_bc_done.sem, conv_bc_done.at(i, 1))
                nc.scalar.activation(act_[:, 2:4], act_[:, 2:4], ACT.Silu).then_inc(bc_ready.sem, 1)
                if not first:
                    nc.scalar.activation(gstd, gstd, ACT.Sqrt).then_inc(stdg_done.sem, 1)
                act.wait_ge(e_full.sem, e_full.at(i, 1))
                nc.scalar.activation(eexp.rearrange("p q (h t) -> p (q h) t", h=2), psum[:, 4:8, 0:HALF],
                                     ACT.Exp).then_inc(e_ready.sem, 1)
                nxt(0)
                act.wait_ge(tok_full.sem, tok_full.at(i, 1))
                nc.scalar.activation(btok, psum[:, 6, :].rearrange("p (c n) -> p c n", c=NCH), ACT.Copy).then_inc(bc_out.sem, 1)
                act.wait_ge(tokx_done.sem, tokx_done.at(i, 1))
                nc.scalar.activation(xdt, psum[:, 4:6, :].rearrange("p b (c n) -> p (b c) n", c=2),
                                     ACT.Copy).then_inc(tok_out.sem, 1)
                nxt(1)
                act.wait_ge(sbc_full.sem, sbc_full.at(i, 1))
                nc.scalar.activation(bcs[0:NB, :], psum[0:NB, 6, 0:256], ACT.Copy).then_inc(sbc_out.sem, 1)
                if more:
                    last_tap(i + 1, 1 - j, (0, 1), init_x)
                nxt(2)
                for h in range(4):
                    act.wait_ge(seg_done.sem, seg_done.at(i, h + 1))
                    nc.scalar.activation(seg[h % 2], seg[h % 2], ACT.Exp).then_inc(dec_ready.sem, 1)
                    if h == 1:
                        nxt(3)
                        if more:
                            last_tap(i + 1, 1 - j, (2, 3), init_bc)
                act.wait_ge(hfin_full.sem, hfin_full.at(i, 1))
                if not first:
                    act.wait_ge(st_hfin, i * 16)
                nc.scalar.activation(hfin, psum[:, 5, 0:256].rearrange("p (q n) -> p q n", q=2),
                                     ACT.Copy).then_inc(hfin_out.sem, 1)
                act.wait_ge(z_ready.sem, z_ready.at(i, 1))
                nxt(4)
                nxt(5)
                act.wait_ge(gated.sem, gated.at(i, 1))
                nc.scalar.activation(ytmp, y, ACT.Square).then_inc(sqg_done.sem, 1)
                act.wait_ge(varg_done.sem, varg_done.at(i, 1))

            act.wait_ge(raw_zero, 1)
            for n in range(6):
                evacuate(0, n)
                if n == 3:
                    last_tap(0, 0, (0, 1), init_x)
                    last_tap(0, 0, (2, 3), init_bc)
            turn(0, 0, first=True)
            with act.Fori(0, SG // 2 - 1) as i:
                turn(i * 2 + 1, 1)
                turn(i * 2 + 2, 0)
            turn(SG - 1, 1, more=False)
            nc.scalar.activation(gstd, gstd, ACT.Sqrt).then_inc(stdg_done.sem, 1)

        @block.vector
        def _(dve):
            class Taps:

                def __init__(self, g, j, tiles, own, init, done):
                    self.g, self.act_, self.tiles, self.init, self.done = g, acts[j], tiles, init, done
                    self.s = Steps(dve, own)
                    self.s.turn(g)

                def tap(self, k):
                    g, act_ = self.g, self.act_
                    if k == 0:
                        dve.wait_ge(self.init.sem, self.init.at(g, 1))
                    else:
                        dve.wait_ge(self.s.own.sem, self.s.own.at(g, k))
                    for c in self.tiles:
                        ct = (g * 2, g * 2 + 1, g + 16, g + 24)[c]
                        w = cw[:, bass.ds(ct + 32 * k, 1)]
                        nc.vector.scalar_tensor_tensor(act_[:, c, 0:SEQ], raw[:, c, k:k + SEQ], w,
                                                       act_[:, c, 0:SEQ], ALU.mult, ALU.add)
                        ins = nc.vector.scalar_tensor_tensor(act_[:, c, SEQ:T], st[:, bass.ds(ct, 1), :, k], w,
                                                             act_[:, c, SEQ:T], ALU.mult, ALU.add)
                    if k < 2:
                        self.s.post(ins)
                        return
                    for c in self.tiles:
                        ct = (g * 2, g * 2 + 1, g + 16, g + 24)[c]
                        ins = nc.vector.tensor_copy(tail[:, bass.ds(ct, 1), :], raw[:, c:c + 1, SEQ:SEQ + 11])
                    self.s.post(ins, self.done)
                    self.s.turn(g)

            def taps_bc(g, j):
                bc = Taps(g, j, (2, 3), dve_bc, init_bc, conv_bc_done)
                for k in range(3):
                    bc.tap(k)

            def normalise(g):
                s = Steps(dve, dve_norm)
                s.turn(g)
                dve.wait_ge(stdg_done.sem, stdg_done.at(g, 1))
                s.link(nc.vector.reciprocal(gstd, gstd))
                for q in range(2):
                    ins = nc.vector.scalar_tensor_tensor(yT[:, bass.ds(g * 2 + q, 1), :].rearrange("p o t -> p (o t)"),
                                                         y[:, q, :], pT[:, bass.ds(g * 2 + (PR_GN + q), 1)], gstd,
                                                         ALU.mult, ALU.mult)
                s.post(ins, yt_done)
                s.turn(g)

            def turn(i, j, more=True, first=False):
                act_ = acts[j]
                s = Steps(dve, dve_own)
                s.turn(i)
                dve.wait_ge(dtb_full.sem, dtb_full.at(i, 1))
                dve.wait_ge(x_ready.sem, x_ready.at(i, 1))
                for q in range(2):
                    ins = nc.vector.tensor_tensor(xdtT[:, q, :].rearrange("p (h t) -> p h t", h=2),
                                                  act_[:, q, :].rearrange("p (h t) -> p h t", h=2),
                                                  halves(psum, 4 + 2 * q), ALU.mult)
                s.post(ins, xdt_done)
                if not first:
                    normalise(i - 1)
                dve.wait_ge(tok_full.sem, tok_full.at(i, 1))
                for c in range(NCH):
                    ins = nc.vector.tensor_tensor(xdte[:, c, :].rearrange("p (h n) -> p h n", h=4),
                                                  psum[:, 4 + c // 2, (c % 2) * 256:(c % 2) * 256 + 256]
                                                  .rearrange("p (h n) -> p h n", h=4),
                                                  toend[:, c, bass.ds(i * 4, 4)].unsqueeze(2).to_broadcast([P, 4, 64]),
                                                  ALU.mult)
                s.post(ins, tokx_done)
                s.post(nc.vector.tensor_tensor(cbm, psum[:, 7, :].rearrange("p (c n) -> p c n", c=NCH),
                                               const("causal").unsqueeze(1).to_broadcast([P, NCH, P]), ALU.mult),
                       cbm_done)
                taps = Taps(i + 1, 1 - j, (0, 1), dve_x, init_x, conv_x_done)

                def tap(k):
                    if more:
                        taps.tap(k)

                dve.wait_ge(state_full.sem, state_full.at(i, 1))

                def new_state(c):
                    return psum[:, 4 + c // 2, (c % 2) * 256:(c % 2) * 256 + 256]

                s.link(nc.vector.tensor_copy(hT[:, 0, :], new_state(0)))
                for c in range(1, NCH):
                    s.link(nc.vector.tensor_tensor(hT[:, c, :].rearrange("p (h n) -> p h n", h=4),
                                                   hT[:, c - 1, :].rearrange("p (h n) -> p h n", h=4),
                                                   decay[:, c, bass.ds(i * 4, 4)].unsqueeze(2).to_broadcast([P, 4, 64]),
                                                   ALU.mult))
                    s.link(nc.vector.tensor_tensor(hT[:, c, :], hT[:, c, :], new_state(c), ALU.add),
                           h_done if c == NCH - 1 else None)
                dve.wait_ge(yoff_full.sem, yoff_full.at(i, 1))
                dve.wait_ge(e_ready.sem, e_ready.at(i, 1))
                ins = nc.vector.tensor_tensor(ytmp[:, :, CH:SEQ], psum[:, 6:8, CH:SEQ], eexp[:, :, CH:SEQ], ALU.mult)
                s.post(ins, yoff_used)
                for r in range(2):
                    b0 = 4 * r
                    dve.wait_ge(row_full.sem, row_full.at(i, r + 1))
                    rows4 = psum[:, 4:6, :].rearrange("p k (b s n) -> p (k b) s n", b=2, s=2)
                    tmp = stmp.rearrange("p (b q n) -> p b q n", b=4, q=2)
                    for q in range(2):
                        ins = nc.vector.tensor_tensor(tmp[:, :, q, :], rows4[:, :, 0, :],
                                                      xdtT[:, q, SEQ + b0:SEQ + b0 + 4].unsqueeze(2)
                                                      .to_broadcast([P, 4, SN]), ALU.mult)
                    s.link(ins)
                    if r == 0:
                        dve.wait_ge(sdec_done.sem, sdec_done.at(i, 1))
                    s.link(nc.vector.tensor_tensor(sst[:, b0:b0 + 4], sst[:, b0:b0 + 4], tmp, ALU.add),
                           sst_done if r else None)
                    for q in range(2):
                        ins = nc.vector.tensor_tensor(tmp[:, :, q, :], sst[:, b0:b0 + 4, q, :], rows4[:, :, 1, :],
                                                      ALU.mult)
                    s.link(ins, row_used)
                    s.link(nc.vector.tensor_reduce(ysmp[:, b0:b0 + 4, :], tmp, AX.X, ALU.add))
                    tap(r)
                def differences(h):
                    dve.wait_ge(sum_full.sem, sum_full.at(i, h + 1))
                    if h >= 2:
                        dve.wait_ge(mt_used.sem, mt_used.at(i, h - 1))
                    for c in range(NCH):
                        ins = nc.vector.tensor_scalar(seg[h % 2][:, c, :], psum[:, 4 + h % 2, c * CH:(c + 1) * CH],
                                                      acs_tok[:, c, bass.ds(i * 4 + h, 1)], 0.0, ALU.subtract, ALU.min)
                    s.post(ins, seg_done)

                def product(h):
                    dve.wait_ge(dec_ready.sem, dec_ready.at(i, h + 1))
                    s.post(nc.vector.tensor_tensor(seg[h % 2], seg[h % 2], cbm, ALU.mult), mt_done)

                dve.wait_ge(cbm_done.sem, cbm_done.at(i, 1))
                differences(0)
                differences(1)
                product(0)
                product(1)
                tap(2)
                differences(2)
                differences(3)
                product(2)
                product(3)
                dve.wait_ge(mt_used.sem, mt_used.at(i, 4))
                for q in range(2):
                    ins = nc.vector.scalar_tensor_tensor(y[:, q, 0:SEQ], act_[:, q, 0:SEQ], dsk[:, bass.ds(i * 2 + q, 1)],
                                                         psum[:, 6 + q, :], ALU.mult, ALU.add)
                s.link(ins)
                s.post(nc.vector.tensor_tensor(y[:, :, CH:SEQ], y[:, :, CH:SEQ], ytmp[:, :, CH:SEQ], ALU.add))
                for q in range(2):
                    ins = nc.vector.scalar_tensor_tensor(y[:, q, SEQ:T], act_[:, q, SEQ:T], dsk[:, bass.ds(i * 2 + q, 1)],
                                                         ysmp[:, :, q], ALU.mult, ALU.add)
                s.link(ins)
                dve.wait_ge(z_ready.sem, z_ready.at(i, 1))
                s.link(nc.vector.tensor_tensor(y, y, zs, ALU.mult), gated)
                dve.wait_ge(ssg_full.sem, ssg_full.at(i, 1))
                s.post(nc.vector.tensor_scalar(gstd.rearrange("p (h t) -> p h t", h=2), halves(psum, 6), 1.0 / 256, EPS,
                                               ALU.mult, ALU.add), varg_done)
                s.turn(i)
                if more:
                    taps_bc(i + 1, 1 - j)

            dve.wait_ge(raw_zero, 1)
            x0 = Taps(0, 0, (0, 1), dve_x, init_x, conv_x_done)
            for k in range(3):
                x0.tap(k)
            taps_bc(0, 0)
            turn(0, 0, first=True)
            with dve.Fori(0, SG // 2 - 1) as i:
                turn(i * 2 + 1, 1)
                turn(i * 2 + 2, 0)
            turn(SG - 1, 1, more=False)
            normalise(SG - 1)
            dve.wait_ge(yt_done.sem, SG)


    def project_out(name, kin, src, w_dram, rooms, norm_row, last=False, extra=None):
        w2 = rooms
        w_view = w_dram.rearrange("(k p) n -> p k n", p=P)
        ld = [sem(f"{name}_ld{j}") for j in range(2)]
        full, added = sig(f"{name}_full", 4), sig(f"{name}_added", 4)
        sq, ssq, var, sd, rs, xnd = (sem(f"{name}_{x}") for x in ("sq", "ssq", "var", "sd", "rs", "xn"))
        turns = KT // 4
        with nc.Block() as block:
            @block.sync
            def _(sp):
                def load(i, j):
                    sp.dma_start(w2[j], w_view[:, :, bass.ds(i * 512 + j * 256, 256)]).then_inc(ld[j], 16)

                for j in range(2):
                    load(0, j)
                with sp.Fori(0, turns - 1) as i:
                    for j in range(2):
                        sp.wait_ge(full.sem, full.at(i, 2 * j + 2))
                        load(i + 1, j)
                if extra:
                    extra["sync"](sp)

            @block.tensor
            def _(pe):
                def turn(i, first=False):
                    for n in range(4):
                        if n % 2 == 0:
                            pe.wait_ge(ld[n // 2], i * 16 + 16)
                        if not (first and n < 2):
                            pe.wait_ge(added.sem, added.at(i, n - 1))
                        for k in range(kin):
                            for h in range(2):
                                mm = nc.tensor.matmul(psum[:, n % 2 * 2 + h, 0:HALF],
                                                      w2[n // 2][:, k, n % 2 * P:(n % 2 + 1) * P],
                                                      src[:, k, h * HALF:(h + 1) * HALF],
                                                      start=(k == 0), stop=(k == kin - 1))
                        mm.then_inc(full.sem, 1)

                turn(0, True)
                if extra:
                    extra["tensor"](pe)
                with pe.Fori(1, turns) as i:
                    turn(i)
                pe.wait_ge(sq, KT)
                for h in range(2):
                    for k in range(KT):
                        mm = nc.tensor.matmul(psum[:, 2 + h, 0:HALF], ones, xn[:, k, h * HALF:(h + 1) * HALF],
                                              start=(k == 0), stop=(k == KT - 1))
                mm.then_inc(ssq, 1)

            @block.scalar
            def _(act):
                if extra:
                    extra["scalar"](act)
                for k in range(KT):
                    act.wait_ge(added.sem, k + 1)
                    nc.scalar.activation(xn[:, k, :], xT[:, k, :], ACT.Square).then_inc(sq, 1)
                act.wait_ge(var, 1)
                nc.scalar.activation(std2, std2, ACT.Sqrt).then_inc(sd, 1)

            @block.vector
            def _(dve):
                def turn(i):
                    for n in range(4):
                        dve.wait_ge(full.sem, full.at(i, n + 1))
                        x = xT[:, bass.ds(i * 4 + n, 1), :].rearrange("p o (h t) -> p (o h) t", h=2)
                        nc.vector.tensor_tensor(x, halves(psum, n % 2 * 2), x, ALU.add).then_inc(added.sem, 1)

                with dve.Fori(0, turns) as i:
                    turn(i)
                dve.wait_ge(ssq, 1)
                nc.vector.tensor_scalar(std2.rearrange("p (h t) -> p h t", h=2), halves(psum, 2), 1.0 / D, EPS,
                                        ALU.mult, ALU.add).then_inc(var, 1)
                dve.wait_ge(sd, 1)
                nc.vector.reciprocal(rstd2, std2).then_inc(rs, 1)
                dve.wait_ge(rs, 1)
                for k in range(KT):
                    nc.vector.scalar_tensor_tensor(xn[:, k, :], xT[:, k, :], pT[:, norm_row + k:norm_row + k + 1],
                                                   rstd2, ALU.mult, ALU.mult).then_inc(xnd, 1)
                dve.wait_ge(xnd, KT)

    arena.at = base_y
    std2, rstd2 = take(T), take(T)
    w_rooms = [take(16 * 256).rearrange("p (k n) -> p k n", k=16) for _ in range(2)]
    conv_rows = take(CONV)
    tr_full, tr_out, st_conv = sem("tr_full"), sem("tr_out"), sem("st_conv")

    def conv_pe(pe):
        for j in range(8):
            if j >= 4:
                pe.wait_ge(tr_out, j - 3)
            for c in range(4):
                mm = tr(psum[0:11, 4 + j % 4, c * P:(c + 1) * P], tail[:, 4 * j + c, :], P)
            mm.then_inc(tr_full, 1)

    def conv_act(act):
        for j in range(8):
            act.wait_ge(tr_full, j + 1)
            nc.scalar.activation(conv_rows[0:11, j * 512:(j + 1) * 512], psum[0:11, 4 + j % 4, :], ACT.Copy).then_inc(tr_out, 1)

    def conv_sp(sp):
        sp.wait_ge(tr_out, 8)
        sp.dma_start(io["conv_prompt"][0, 0], conv_rows[0:3, :]).then_inc(st_conv, 16)
        sp.dma_start(io["conv_sample"][0][:, 2, :], conv_rows[3:11, :]).then_inc(st_conv, 16)
        sp.wait_ge(st_conv, 32)
        sp.wait_ge(st_pass, 16 * 9)

    project_out("o1", 16, yT, io["ssd_w_out"][0], w_rooms, PR_N2,
                extra={"sync": conv_sp, "tensor": conv_pe, "scalar": conv_act})

    free_semaphores()
    arena.at = base_all
    mixed = take(KT * T).rearrange("p (k t) -> p k t", k=KT)
    qsm = take(KT * NB).rearrange("p (k b) -> p k b", k=KT)
    zsm = take(3 * KT * NB).rearrange("p (r k b) -> p r k b", r=3, k=KT)
    kns = take(2 * G * NB).rearrange("p (r g b) -> p r g b", r=2, g=G)
    gsm = take(3 * NB).rearrange("p (r b) -> p r b", r=3)
    w1 = take(2 * 16 * P).rearrange("p (t j n) -> p t j n", t=2, j=16)
    w2k = take(P)
    w2v = take(DH)
    pebias = take(2)
    base_smp = arena.at
    gtok = take(4 * 3 * NH).rearrange("p (a h r) -> p a h r", a=4, r=3)
    base_nsa = arena.at
    per = take(P)
    peT = take(32)
    wg = take(KT * 3 * NH).rearrange("p (k n) -> p k n", k=KT)
    gT = take(T)
    ld_w1, ld_pre = sem("ld_w1"), sem("ld_pre")
    pre_pet, pre_pec, pre_full, pre_out, pre_gt, pre_gto, pre_gs = (sem(n) for n in (
        "pre_pet", "pre_pec", "pre_full", "pre_out", "pre_gt", "pre_gto", "pre_gs"))
    n_in = io["nsa_w_in"][0].rearrange("(k p) n -> p k n", p=P)

    with nc.Block() as block:
        @block.sync
        def _(sp):
            sp.dma_start(per[0:32, :], io["nsa_cmp_pe"][0].rearrange("t (j a) d -> (t j) (a d)", a=2)).then_inc(ld_pre, 16)
            sp.dma_start(wg, n_in[:, :, GATE0:Z0]).then_inc(ld_pre, 16)
            for t in range(2):
                sp.dma_start(w1[:, t], io["nsa_cmp_w1"][0, t].rearrange("(j p) n -> p j n", p=P)).then_inc(ld_w1, 16)
                sp.dma_start(w2k[:, t * DH:(t + 1) * DH], io["nsa_cmp_w2"][0, 0]).then_inc(ld_w1, 16)
            sp.dma_start(w2v, io["nsa_cmp_w2"][0, 1]).then_inc(ld_w1, 16)

        @block.tensor
        def _(pe):
            pe.wait_ge(ld_pre, 32)
            tr(psum[:, 0, 0:32], per[0:32, :], 32).then_inc(pre_pet, 1)
            for h in range(2):
                for k in range(KT):
                    nc.tensor.matmul(psum[0:3 * NH, 2 + h, 0:HALF], wg[:, k, :], xn[:, k, h * HALF:(h + 1) * HALF],
                                     start=(k == 0), stop=(k == KT - 1))
            for r in range(3):
                for k in range(KT):
                    mm = nc.tensor.matmul(psum[0:NH, 4, r * NB:(r + 1) * NB], wg[:, k, r:3 * NH:3], xn[:, k, SEQ:T],
                                          start=(k == 0), stop=(k == KT - 1))
            mm.then_inc(pre_gs, 1)
            pe.wait_ge(pre_gto, 2)
            for a in range(4):
                mm = tr(psum[:, 5, a * 48:(a + 1) * 48], gT[0:48, a * P:(a + 1) * P], 48)
            mm.then_inc(pre_gt, 1)
            pe.wait_ge(ld_w1, 80)
            pe.wait_ge(pre_pec, 1)
            for t in range(2):
                for j in range(16):
                    mm = nc.tensor.matmul(psum[:, 1, t:t + 1], w1[:, t, j, :], peT[:, t * 16 + j:t * 16 + j + 1],
                                          start=(j == 0), stop=(j == 15))
            mm.then_inc(pre_full, 1)

        @block.scalar
        def _(act):
            act.wait_ge(pre_gs, 1)
            nc.scalar.activation(gT[0:48, :].rearrange("p (h t) -> p h t", h=2), halves(psum, 2, 48), ACT.Sigmoid).then_inc(pre_gto, 1)
            nc.scalar.activation(gsm[0:NH], psum[0:NH, 4, 0:3 * NB].rearrange("p (r b) -> p r b", r=3), ACT.Sigmoid).then_inc(pre_gto, 1)
            act.wait_ge(pre_gto, 2)

        @block.vector
        def _(dve):
            dve.wait_ge(pre_pet, 1)
            nc.vector.tensor_copy(peT, psum[:, 0, 0:32]).then_inc(pre_pec, 1)
            dve.wait_ge(pre_gt, 1)
            nc.vector.tensor_copy(gtok, psum[:, 5, 0:192].rearrange("p (a h r) -> p a h r", a=4, r=3)).then_inc(pre_out, 1)
            dve.wait_ge(pre_full, 1)
            nc.vector.tensor_copy(pebias, psum[:, 1, 0:2]).then_inc(pre_out, 1)
            dve.wait_ge(pre_out, 2)

    arena.at = base_nsa
    slot_a = take(KT * 256).rearrange("p (k n) -> p k n", k=KT)
    slot_b = take(KT * 256).rearrange("p (k n) -> p k n", k=KT)
    slot_c = take(KT * P).rearrange("p (k n) -> p k n", k=KT)
    slot_d = take(KT * 256).rearrange("p (k n) -> p k n", k=KT)
    qraw = take(2 * T).rearrange("p (c t) -> p c t", c=2)
    kvraw = take(3 * T).rearrange("p (c t) -> p c t", c=3)
    zraw2 = take(6 * T).rearrange("p (c t) -> p c t", c=6)
    qT = take(2 * T).rearrange("p (c t) -> p c t", c=2)
    zs2 = take(6 * T).rearrange("p (c t) -> p c t", c=6)
    kd = take(2 * T).rearrange("p (r t) -> p r t", r=2)
    kcs = take(2 * T).rearrange("p (r t) -> p r t", r=2)
    vtok = take(4 * 3 * P).rearrange("p (a c n) -> p a c n", a=4, c=3)
    smtok = take(3 * P)
    strip = take(4 * SEQ).rearrange("p (h k) -> p h k", h=4)
    bct = take(4 * SEQ).rearrange("p (h q) -> p h q", h=4)
    shared = take(5 * SEQ)
    s_sb = [shared[:, j * SEQ:(j + 1) * SEQ] for j in range(3)]
    p_t = [shared[:, (3 + j) * SEQ:(4 + j) * SEQ] for j in range(2)]
    pct = shared[:, 0:4 * SEQ].rearrange("p (h q) -> p h q", h=4)
    osb = take(4 * 3 * 2 * P).rearrange("p (a r i n) -> p a r i n", a=4, r=3, i=2)
    mixt = shared[:, 0:SEQ]
    hid = take(2 * NCP).rearrange("p (t c) -> p t c", t=2)
    kct = take(NCP)
    vc = take(DH)
    cbias = take(16 * NCP).rearrange("p (e n) -> p e n", e=2)
    sc = take(16 * NCP).rearrange("p (e n) -> p e n", e=2)
    mx = take(16)
    dn = take(16)
    rg = take(16)
    top = take(32)
    ntop = take(32)
    den = take(32).rearrange("p (h u) -> p h u", h=4)
    rgs = take(8)

    ld_a, ld_b, ld_c, ld_d, ld_dup, ld_strip, st_kv = (sem(n) for n in (
        "ld_a", "ld_b", "ld_c", "ld_d", "ld_dup", "ld_strip", "st_kv"))
    NT = 11
    UN = 32
    t_full, t_out = sig("t_full", NT), sig("t_out", NT)
    q_ready, z2_ready = sig("q_ready"), sig("z2_ready")
    kvt_full, kvt_out, cap_done = sig("kvt_full"), sig("kvt_out", 2), sig("cap_done")
    hid_full, hid_out, ckv_full, ckv_out, cb_full, cb_out = (
        sig("hid_full"), sig("hid_out"), sig("ckv_full"), sig("ckv_out"), sig("cb_full"), sig("cb_out"))
    sc_full, sc_ready, ec_done, pct_full, pct_out, oc_full, oc_out = (
        sig("sc_full"), sig("sc_ready"), sig("ec_done"), sig("pct_full"), sig("pct_out", 2), sig("oc_full"), sig("oc_out"))
    s_full, s_out, p_ready, pt_full, pt_act, pt_dve, pv_done, head_out = (
        sig("s_full", UN), sig("s_out", UN), sig("p_ready", UN), sig("pt_full", UN), sig("pt_act", UN // 2),
        sig("pt_dve", UN // 2), sig("pv_done", UN), sig("head_out", 4))
    of_full, of_out = sig("of_full", 6), sig("of_out", 6)
    top_done = sig("top_done", UN)
    carrier = sem("carrier2")
    dve_nsa = sig("dve_nsa", 3 + 4 + 8 + 4)

    def unit(u):
        return u // 8, u % 8 // 4, u % 4

    with nc.Block() as block:
        @block.sync
        def _(sp):
            kv_w = n_in[:, :, AW:AW + 1536].rearrange("p k (t n) -> p k t n", t=6)

            def load_q(g):
                sp.dma_start(slot_a, n_in[:, :, bass.ds(g * 256, 256)]).then_inc(ld_a, 16)

            def load_kv(g):
                for t in range(4):
                    sp.dma_start(slot_b[:, :, t * DH:(t + 1) * DH],
                                 n_in[:, :, bass.ds(g * DH + (AW + 256 * t), DH)]).then_inc(ld_b, 16)

            def load_w(g):
                for t in range(2):
                    sp.dma_start(slot_c[:, :, t * DH:(t + 1) * DH],
                                 n_in[:, :, bass.ds(g * DH + (AW + 256 * (4 + t)), DH)]).then_inc(ld_c, 16)

            def load_z(g, r, slot, s):
                sp.dma_start(slot, n_in[:, :, bass.ds(g * 256 + (Z0 + AW * r), 256)]).then_inc(s, 16)

            def strips(i):
                for h in range(4):
                    sp.dma_start(strip[:, h, :], bass.AP(scr_f.tensor, (i * 4 + h) * FLEN + 384, [[1, P], [1, SEQ]]))\
                        .then_inc(ld_strip, 16)
                    sp.dma_start(bct[0:NCP, h, :], bass.AP(scr_f.tensor, (i * 4 + h) * FLEN, [[16, NCP], [1, SEQ]]))\
                        .then_inc(ld_strip, 16)

            def stores(i):
                sp.wait_ge(kvt_out.sem, kvt_out.at(i, 2))
                for a in range(4):
                    sp.dma_start(io["kv_prompt"][0, a * P:(a + 1) * P, 0, :, bass.ds(i, 1), :].rearrange("s t o d -> s t (o d)"),
                                 vtok[:, a, 0:2, :].rearrange("p c (t d) -> p (c t) d", t=2)).then_inc(st_kv, 16)
                    sp.dma_start(io["win_prompt"][0, 0, a * P:(a + 1) * P, :, bass.ds(i, 1), :].rearrange("s t o d -> s t (o d)"),
                                 vtok[:, a, 2, :].rearrange("p (t d) -> p t d", t=2)).then_inc(st_kv, 16)
                sp.dma_start(io["kv_sample"][:, 0, 0, :, bass.ds(i, 1), :].rearrange("s t o d -> s t (o d)"),
                             smtok[0:NB, 0:256].rearrange("p (t d) -> p t d", t=4)).then_inc(st_kv, 16)
                sp.dma_start(io["win_sample"][0, :, 511, :, bass.ds(i, 1), :].rearrange("s t o d -> s t (o d)"),
                             smtok[0:NB, 256:384].rearrange("p (t d) -> p t d", t=2)).then_inc(st_kv, 16)
                sp.dma_start(scr_new[:, :, bass.ds(i, 1), :].rearrange("s t o d -> s t (o d)"),
                             smtok[0:NB, 0:384].rearrange("p (t d) -> p t d", t=6)).then_inc(st_kv, 16)

            def early_loads(i, first=False):
                if not first:
                    sp.wait_ge(t_full.sem, t_full.at(i - 1, 11))
                load_q(i)
                load_kv(i)
                load_w(i)
                load_z(i, 0, slot_d, ld_d)

            def late_loads(i):
                sp.wait_ge(t_full.sem, t_full.at(i, 2))
                load_z(i, 1, slot_a, ld_a)
                sp.wait_ge(t_full.sem, t_full.at(i, 4))
                load_z(i, 2, slot_b, ld_b)

            def turn(i, more=True, first=False):
                if more:
                    early_loads(i + 1)
                if not first:
                    sp.wait_ge(s_out.sem, s_out.at(i, 0))
                strips(i)
                stores(i)
                if more:
                    late_loads(i + 1)

            early_loads(0, True)
            late_loads(0)
            turn(0, first=True)
            with sp.Fori(1, G - 1) as i:
                turn(i)
            turn(G - 1, more=False)
            sp.wait_ge(st_kv, 16 * 11 * G)

        @block.gpsimd
        def _(pool):
            def turn(i, first=False):
                pool.wait_ge(t_out.sem, t_out.at(i, 5))
                if not first:
                    pool.wait_ge(pv_done.sem, pv_done.at(i, 0))
                    pool.wait_ge(cap_done.sem, cap_done.at(i, 0))
                    pool.sem_inc(carrier, 1)
                for half in range(2):
                    lo = slice(half * 64, half * 64 + 64)
                    n = T - half
                    for r in range(2):
                        pool.dma_start(kd[lo, r, :], kvraw[0:64, 1 + r, :]).then_inc(ld_dup, 16)
                        pool.dma_start(kcs[lo, r, 0:n], kvraw[r * 64:r * 64 + 64, 0, half:T]).then_inc(ld_dup, 16)
                pool.wait_ge(q_ready.sem, q_ready.at(i, 1))
                pool.wait_ge(z2_ready.sem, z2_ready.at(i, 1))
                nc.gpsimd.tensor_copy(qsm[:, bass.ds(i * 2, 2), :], qT[:, :, SEQ:T])
                for r in range(3):
                    nc.gpsimd.tensor_copy(zsm[:, r, bass.ds(i * 2, 2), :], zs2[:, 2 * r:2 * r + 2, SEQ:T])
                pool.wait_ge(ld_dup, i * 128 + 128)
                for r in range(2):
                    ins = nc.gpsimd.tensor_copy(kns[:, r, bass.ds(i, 1), :], kd[:, r:r + 1, SEQ:T])
                ins.then_inc(cap_done.sem, 1)

            turn(0, True)
            with pool.Fori(1, G) as i:
                turn(i)
            pool.wait_ge(cap_done.sem, G)

        @block.tensor
        def _(pe):
            def project(g, n, first=False):
                w, at, s, v = {0: (slot_a, 0, ld_a, g * 32 + 16), 1: (slot_a, 1, ld_a, g * 32 + 16),
                               2: (slot_b, 0, ld_b, g * 80 + 64), 3: (slot_b, 1, ld_b, g * 80 + 64),
                               4: (slot_c, 0, ld_c, g * 32 + 32),
                               5: (slot_d, 0, ld_d, g * 16 + 16), 6: (slot_d, 1, ld_d, g * 16 + 16),
                               7: (slot_a, 0, ld_a, g * 32 + 32), 8: (slot_a, 1, ld_a, g * 32 + 32),
                               9: (slot_b, 0, ld_b, g * 80 + 80), 10: (slot_b, 1, ld_b, g * 80 + 80)}[n]
                pe.wait_ge(s, v)
                if not (first and n == 0):
                    pe.wait_ge(t_out.sem, t_out.at(g, n))
                for k in range(KT):
                    for h in range(2):
                        mm = nc.tensor.matmul(psum[:, h, 0:HALF], w[:, k, at * P:(at + 1) * P],
                                              xn[:, k, h * HALF:(h + 1) * HALF], start=(k == 0), stop=(k == KT - 1))
                mm.then_inc(t_full.sem, 1)

            def turn(i, more=True, first=False):
                def nxt(n):
                    if more:
                        project(i + 1, n)

                pe.wait_ge(t_out.sem, t_out.at(i, 5))
                if not first:
                    pe.wait_ge(of_out.sem, of_out.at(i, 0))
                for c in range(3):
                    for a in range(4):
                        tr(psum[:, 2 + c, a * P:(a + 1) * P], kvraw[:, c, a * P:(a + 1) * P], P)
                for c in range(3):
                    mm = tr(psum[0:NB, 5, c * P:(c + 1) * P], kvraw[:, c, SEQ:T], P)
                mm.then_inc(kvt_full.sem, 1)
                nxt(0)
                pe.wait_ge(ld_dup, i * 128 + 128)
                for t in range(2):
                    for j in range(16):
                        mm = nc.tensor.matmul(psum[:, 6, t * NCP:(t + 1) * NCP], w1[:, t, j, :],
                                              kcs[:, t, 2 * j:2 * j + 16 * (NCP - 1) + 1:16], start=(j == 0), stop=(j == 15))
                mm.then_inc(hid_full.sem, 1)
                nxt(1)
                pe.wait_ge(hid_out.sem, hid_out.at(i, 1))
                nc.tensor.matmul(psum[:, 7, 0:NCP], w2k, hid[:, 0, :], start=True, stop=True)
                nc.tensor.matmul(psum[0:NCP, 7, 64:128], hid[:, 1, :], w2v, start=True, stop=True).then_inc(ckv_full.sem, 1)
                pe.wait_ge(ld_strip, i * 128 + 128)
                pe.wait_ge(kvt_out.sem, kvt_out.at(i, 2))
                pe.sem_inc(carrier, 1)
                for h in range(4):
                    for a in range(4):
                        o = (h // 2 * 4 + a) * NCP
                        mm = tr(psum[:, 2 + h % 2, o:o + NCP], bct[0:NCP, h, a * P:(a + 1) * P], NCP)
                mm.then_inc(cb_full.sem, 1)
                nxt(2)
                pe.wait_ge(q_ready.sem, q_ready.at(i, 1))
                pe.wait_ge(ckv_out.sem, ckv_out.at(i, 1))
                for h in range(4):
                    lo = slice(h % 2 * 64, h % 2 * 64 + 64)
                    for a in range(4):
                        o = (h // 2 * 4 + a) * NCP
                        mm = nc.tensor.matmul(psum[:, 4 + h % 2, o:o + NCP], qT[lo, h // 2, a * P:(a + 1) * P],
                                              kct[lo, :], start=True, stop=True)
                mm.then_inc(sc_full.sem, 1)
                nxt(3)
                pe.wait_ge(ec_done.sem, ec_done.at(i, 1))
                pe.wait_ge(cb_out.sem, cb_out.at(i, 1))
                for h in range(4):
                    for a in range(4):
                        o = (h // 2 * 4 + a) * NCP
                        mm = tr(psum[0:NCP, (2, 3, 6, 7)[h], a * P:(a + 1) * P], sc[:, h % 2, o:o + NCP], P)
                mm.then_inc(pct_full.sem, 1)
                nxt(4)
                pe.wait_ge(pct_out.sem, pct_out.at(i, 2))
                for h in range(4):
                    for a in range(4):
                        o = (h * 4 + a) * DH
                        mm = nc.tensor.matmul(psum[:, 4 + o // 512, o % 512:o % 512 + DH], pct[0:NCP, h, a * P:(a + 1) * P],
                                              vc[0:NCP, :], start=True, stop=True)
                mm.then_inc(oc_full.sem, 1)
                for u in range(UN + 2):
                    if u < UN:
                        h, r, a = unit(u)
                        lo = slice(h % 2 * 64, h % 2 * 64 + 64)
                        n = (a + 1) * P
                        if u >= 3:
                            pe.wait_ge(s_out.sem, s_out.at(i, u - 2))
                        if u == 2:
                            pe.wait_ge(oc_out.sem, oc_out.at(i, 1))
                        nc.tensor.matmul(psum[:, 2 + u % 3, 0:n], qT[lo, h // 2, a * P:(a + 1) * P], kd[lo, r, 0:n],
                                         start=True, stop=True).then_inc(s_full.sem, 1)
                    if 1 <= u <= UN:
                        v = u - 1
                        a = unit(v)[2]
                        pe.wait_ge(p_ready.sem, p_ready.at(i, v + 1))
                        if v == 0:
                            pe.wait_ge(oc_out.sem, oc_out.at(i, 1))
                        if v >= 2:
                            w = pt_act if v % 2 else pt_dve
                            pe.wait_ge(w.sem, w.at(i, v // 2))
                        for b in range(a + 1):
                            mm = tr(psum[:, 5 + v % 2, b * P:(b + 1) * P], s_sb[v % 3][:, b * P:(b + 1) * P], P)
                        mm.then_inc(pt_full.sem, 1)
                    if u >= 2:
                        v = u - 2
                        h, r, a = unit(v)
                        w = pt_act if v % 2 else pt_dve
                        pe.wait_ge(w.sem, w.at(i, v // 2 + 1))
                        if v % 8 == 0 and v:
                            pe.wait_ge(head_out.sem, head_out.at(i, v // 8))
                        for b in range(a + 1):
                            mm = nc.tensor.matmul(psum[:, 7, v % 8 * DH:(v % 8 + 1) * DH], p_t[v % 2][:, b * P:(b + 1) * P],
                                                  vtok[:, b, 1 + r, DH:P], start=(b == 0), stop=(b == a))
                        mm.then_inc(pv_done.sem, 1)
                    if u % 5 == 4 and u // 5 < 6:
                        nxt(5 + u // 5)
                pe.wait_ge(head_out.sem, head_out.at(i, 4))
                for j in range(6):
                    for a in range(4):
                        mm = tr(psum[:, 2 + j, a * P:(a + 1) * P], osb[:, a, j // 2, j % 2, :], P)
                    mm.then_inc(of_full.sem, 1)

            for n in range(NT):
                project(0, n, True)
            turn(0, first=True)
            with pe.Fori(1, G - 1) as i:
                turn(i)
            turn(G - 1, more=False)

        @block.scalar
        def _(act):
            def evacuate(g, n):
                act.wait_ge(t_full.sem, t_full.at(g, n + 1))
                dst = qraw[:, n, :] if n < 2 else kvraw[:, n - 2, :] if n < 5 else zraw2[:, n - 5, :]
                nc.scalar.activation(dst.rearrange("p (h t) -> p h t", h=2), halves(psum, 0), ACT.Copy).then_inc(t_out.sem, 1)

            def turn(i, more=True, first=False):
                def nxt(n):
                    if more:
                        evacuate(i + 1, n)

                act.wait_ge(t_out.sem, t_out.at(i, NT))
                if not first:
                    act.wait_ge(pv_done.sem, pv_done.at(i, 0))
                    act.wait_ge(cap_done.sem, cap_done.at(i, 0))
                nc.scalar.activation(qT, qraw, ACT.Copy, scale=DH ** -0.5).then_inc(q_ready.sem, 1)
                if not first:
                    act.wait_ge(of_out.sem, of_out.at(i, 0))
                nc.scalar.activation(zs2, zraw2, ACT.Silu).then_inc(z2_ready.sem, 1)
                act.wait_ge(kvt_full.sem, kvt_full.at(i, 1))
                if not first:
                    act.wait_ge(st_kv, i * (16 * 11))
                for c in range(3):
                    ins = nc.scalar.activation(vtok[:, :, c, :], psum[:, 2 + c, :].rearrange("p (a n) -> p a n", a=4), ACT.Copy)
                ins.then_inc(kvt_out.sem, 1)
                nc.scalar.activation(smtok[0:NB, :], psum[0:NB, 5, 0:384], ACT.Copy).then_inc(kvt_out.sem, 1)
                act.wait_ge(q_ready.sem, q_ready.at(i, 1))
                nxt(0)
                act.wait_ge(hid_full.sem, hid_full.at(i, 1))
                for t in range(2):
                    ins = nc.scalar.activation(hid[:, t, :], psum[:, 6, t * NCP:(t + 1) * NCP], ACT.Silu,
                                               bias=pebias[:, t:t + 1])
                ins.then_inc(hid_out.sem, 1)
                nxt(1)
                act.wait_ge(ckv_full.sem, ckv_full.at(i, 1))
                nc.scalar.activation(kct, psum[:, 7, 0:NCP], ACT.Copy)
                nc.scalar.activation(vc[0:NCP, :], psum[0:NCP, 7, 64:128], ACT.Copy).then_inc(ckv_out.sem, 1)
                act.wait_ge(cb_full.sem, cb_full.at(i, 1))
                nc.scalar.activation(cbias.rearrange("p e (x c) -> p e x c", c=NCP)[:, :, :, ::-1],
                                     psum[:, 2:4, 0:8 * NCP].rearrange("p e (x c) -> p e x c", c=NCP), ACT.Copy).then_inc(cb_out.sem, 1)
                act.wait_ge(ld_dup, i * 128 + 128)
                nxt(2)
                act.wait_ge(sc_ready.sem, sc_ready.at(i, 1))
                nc.scalar.activation(sc, sc, ACT.Exp).then_inc(ec_done.sem, 1)
                nxt(3)
                act.wait_ge(pct_full.sem, pct_full.at(i, 1))
                if not first:
                    act.wait_ge(of_out.sem, of_out.at(i, 0))
                for j in range(2):
                    nc.scalar.activation(pct[0:NCP, 2 * j:2 * j + 2, :], psum[0:NCP, (2, 6)[j]:(4, 8)[j], :],
                                         ACT.Copy).then_inc(pct_out.sem, 1)
                nxt(4)
                act.wait_ge(z2_ready.sem, z2_ready.at(i, 1))
                for u in range(UN + 1):
                    if u < UN:
                        h, r, a = unit(u)
                        n = (a + 1) * P
                        act.wait_ge(s_out.sem, s_out.at(i, u + 1))
                        nc.scalar.activation(s_sb[u % 3][:, 0:n], s_sb[u % 3][:, 0:n], ACT.Exp, bias=ntop[:, u:u + 1],
                                             accum_out=den[:, h, u % 8:u % 8 + 1]).then_inc(p_ready.sem, 1)
                    if u >= 1 and (u - 1) % 2:
                        v = u - 1
                        n = (unit(v)[2] + 1) * P
                        act.wait_ge(pt_full.sem, pt_full.at(i, v + 1))
                        if v >= 2:
                            act.wait_ge(pv_done.sem, pv_done.at(i, v - 1))
                        nc.scalar.activation(p_t[1][:, 0:n], psum[:, 6, 0:n], ACT.Copy).then_inc(pt_act.sem, 1)
                    if u % 5 == 4 and u // 5 < 6:
                        nxt(5 + u // 5)

            for n in range(NT):
                evacuate(0, n)
            turn(0, first=True)
            with act.Fori(1, G - 1) as i:
                turn(i)
            turn(G - 1, more=False)

        @block.vector
        def _(dve):
            def turn(i):
                s = Steps(dve, dve_nsa)
                s.turn(i)
                dve.wait_ge(sc_full.sem, sc_full.at(i, 1))
                dve.wait_ge(cb_out.sem, cb_out.at(i, 1))
                s.link(nc.vector.tensor_tensor(sc, psum[:, 4:6, 0:8 * NCP], cbias, ALU.add))
                sc_b = sc.rearrange("p e (x c) -> p (e x) c", c=NCP)
                s.link(nc.vector.tensor_reduce(mx, sc_b, AX.X, ALU.max))
                s.link(nc.vector.tensor_scalar(mx, mx, GUARD, None, ALU.max))
                s.post(nc.vector.tensor_tensor(sc_b, sc_b, mx.unsqueeze(2).to_broadcast([P, 16, NCP]), ALU.subtract),
                       sc_ready)
                dve.wait_ge(ec_done.sem, ec_done.at(i, 1))
                s.link(nc.vector.tensor_reduce(dn, sc_b, AX.X, ALU.add))
                s.link(nc.vector.tensor_scalar(dn, dn, 1e-30, None, ALU.max))
                s.link(nc.vector.reciprocal(dn, dn))
                for h in range(4):
                    o = h % 2 * 8 + h // 2 * 4
                    ins = nc.vector.tensor_tensor(rg[:, h * 4:h * 4 + 4], dn[:, o:o + 4],
                                                  gtok[:, :, bass.ds(i * 4 + h, 1), 0].rearrange("p a o -> p (a o)"), ALU.mult)
                s.link(ins)
                dve.wait_ge(oc_full.sem, oc_full.at(i, 1))
                for h in range(4):
                    ins = nc.vector.tensor_tensor(osb[:, :, 0, h // 2, h % 2 * DH:(h % 2 + 1) * DH],
                                                  psum[:, 4 + h // 2, h % 2 * 256:h % 2 * 256 + 256].rearrange("p (a d) -> p a d", a=4),
                                                  rg[:, h * 4:h * 4 + 4].unsqueeze(2).to_broadcast([P, 4, DH]), ALU.mult)
                s.post(ins, oc_out)
                dve.wait_ge(ld_strip, i * 128 + 128)
                for u in range(UN + 2):
                    if u < UN:
                        h, r, a = unit(u)
                        n = (a + 1) * P
                        if u >= 3:
                            dve.wait_ge(pt_full.sem, pt_full.at(i, u - 2))
                        dve.wait_ge(s_full.sem, s_full.at(i, u + 1))
                        dve.sem_inc(carrier, 1)
                        nc.vector.tensor_tensor_reduce(out=s_sb[u % 3][:, 0:n], in0=psum[:, 2 + u % 3, 0:n],
                                                       in1=strip[:, h, n - 1::-1], scale=1.0, scalar=-3e38,
                                                       op0=ALU.add, op1=ALU.max, accum_out=top[:, u:u + 1])\
                            .then_inc(top_done.sem, 1)
                        dve.wait_ge(top_done.sem, top_done.at(i, u + 1))
                        s.post(nc.vector.tensor_scalar(ntop[:, u:u + 1], top[:, u:u + 1], -1.0, None, ALU.mult), s_out)
                    if u >= 1 and (u - 1) % 2 == 0 and u - 1 < UN:
                        v = u - 1
                        n = (unit(v)[2] + 1) * P
                        dve.wait_ge(pt_full.sem, pt_full.at(i, v + 1))
                        if v >= 2:
                            dve.wait_ge(pv_done.sem, pv_done.at(i, v - 1))
                        s.post(nc.vector.tensor_copy(p_t[0][:, 0:n], psum[:, 5, 0:n]), pt_dve)
                    if u >= 2 and (u - 2) % 8 == 7:
                        h = (u - 2) // 8
                        dve.wait_ge(p_ready.sem, p_ready.at(i, h * 8 + 8))
                        s.link(nc.vector.reciprocal(rgs, den[:, h, :]))
                        s.link(nc.vector.tensor_tensor(rgs.rearrange("p (r a) -> p r a", r=2), rgs.rearrange("p (r a) -> p r a", r=2),
                                                       gtok[:, :, bass.ds(i * 4 + h, 1), 1:3].rearrange("p a o r -> p (o r) a"),
                                                       ALU.mult))
                        dve.wait_ge(pv_done.sem, pv_done.at(i, h * 8 + 8))
                        s.link(nc.vector.tensor_tensor(osb[:, :, 1:3, h // 2, h % 2 * DH:(h % 2 + 1) * DH].rearrange("p a r d -> p r a d"),
                                                       psum[:, 7, :].rearrange("p (r a d) -> p r a d", r=2, a=4),
                                                       rgs.rearrange("p (r a) -> p r a", r=2).unsqueeze(3).to_broadcast([P, 2, 4, DH]),
                                                       ALU.mult), head_out)
                for j in range(6):
                    r, k = j // 2, j % 2
                    m = mixed[:, bass.ds(i * 2 + k, 1), 0:SEQ].rearrange("p o t -> p (o t)")
                    dve.wait_ge(of_full.sem, of_full.at(i, j + 1))
                    if r == 0:
                        s.link(nc.vector.tensor_tensor(m, psum[:, 2 + j, :], zs2[:, j, 0:SEQ], ALU.mult), of_out)
                    else:
                        s.link(nc.vector.tensor_tensor(mixt, psum[:, 2 + j, :], zs2[:, j, 0:SEQ], ALU.mult))
                        s.link(nc.vector.tensor_tensor(m, m, mixt, ALU.add), of_out)
                s.turn(i)

            with dve.Fori(0, G) as i:
                turn(i)


    free_semaphores()
    arena.at = base_smp
    pages = [take(4 * 2 * 1024).rearrange("p (t a c) -> p t a c", t=4, a=2) for _ in range(2)]
    wins = [take(2 * 2 * 512).rearrange("p (t a c) -> p t a c", t=2, a=2) for _ in range(2)]
    vnew = [take(512) for _ in range(2)]
    kct_s = arena.block[:, xn_at:xn_at + 2 * G * NPAIR].rearrange("p (t g n) -> p t g n", t=2, g=G)
    order = [ca[:, CA["causal"][0] + j * 1024:CA["causal"][0] + (j + 1) * 1024] for j in range(2)]
    kselt = take(2 * 2 * NPAIR).rearrange("p (h a n) -> p h a n", h=2, a=2)
    kwint = take(2 * 2 * NWP).rearrange("p (h a n) -> p h a n", h=2, a=2)
    hid_s = take(2 * G * NCS).rearrange("p (t n) -> p t n", t=2)
    kcmp = take(2 * NCS).rearrange("p (h n) -> p h n", h=2)
    vcmp = take(G * DH)
    s_row = take(KEYS)
    b_row = take(KEYS)
    qsw = take(KT * NB).rearrange("p (k b) -> p k b", k=KT)
    qb = take(2 * NH * NB).rearrange("p (g h b) -> p g h b", g=2, h=NH)
    qcur = take(2 * NH).rearrange("p (g h) -> p g h", g=2)
    kcur = take(2 * 2).rearrange("p (r g) -> p r g", r=2)
    pcg = take(NCS)
    pcT = take(2 * NH)
    impH = take(NSEL)
    cand = take(14)
    keyed = take(14)
    dropped = take(16)
    stat = take(12)
    ptb = take(12 * NH)
    ptn = take(2 * NH)
    o_all = take(NB * 6 * NH).rearrange("p (b n) -> p b n", b=NB)
    o_swp = kselt.rearrange("p h a n -> p (h a n)")[:, 0:NB * 6 * NH].rearrange("p (b n) -> p b n", b=NB)
    msm = take(KT * NB).rearrange("p (k b) -> p k b", k=KT)
    mtmp = take(KT * NB).rearrange("p (k b) -> p k b", k=KT)
    ptab = take(64).bitcast(I32)
    S_SEL, S_NEWS, S_WIN, S_NEWW, S_CMP = 0, SKEYS - 1, SKEYS, SKEYS + WKEYS - 1, SKEYS + WKEYS

    ld_tab, ld_bias = sem("ld_tab"), sem("ld_bias")
    ld_cmp = [sem("ld_cmp0"), sem("ld_cmp1")]
    ld_pg = [sem("ld_pg0"), sem("ld_pg1")]
    NLD = 16 * 11
    swap_full, swap_out, qb_done, pad_done, osw_full, osw_out, msm_done = (
        sem(n) for n in ("swap_full", "swap_out", "qb_done", "pad_done", "osw_full", "osw_out", "msm_done"))
    ord_done = sig("ord_done", 4)
    tk_full, tk_out, ts_full, ts_out = sig("tk_full", 8), sig("tk_out", 8), sig("ts_full", 6), sig("ts_out", 6)
    h_full, h_out, kv_full, kv_out = sig("h_full", 2), sig("h_out", 2), sig("kvs_full"), sig("kvs_out", 2)
    cur_done, score_full, score_used, c_ready, c_exp, pc_done = (
        sig("cur_done"), sig("score_full"), sig("score_used"), sig("c_ready"), sig("c_exp"), sig("pc_done"))
    pcT_full, pcT_out, imp_full, imp_out, grp_full = (
        sig("pcT_full"), sig("pcT_out"), sig("imp_full"), sig("imp_out"), sig("grp_full"))
    w_ready, sel_ready, w_exp, sel_exp, probs_done = (
        sig("w_ready"), sig("sel_ready"), sig("w_exp"), sig("sel_exp"), sig("probs_done"))
    ptb_full, ptb_out, os_full, os_out = sig("ptb_full"), sig("ptb_out", 2), sig("os_full"), sig("os_out")
    dve_smp = sig("dve_smp", 0)
    dve_smp.per = 15
    dve_end = sig("dve_end", 6)
    carrier = sem("carrier3")

    with nc.Block() as block:
        @block.sync
        def _(sp):
            sp.dma_start(ptab[0:1, :], io["page_table"].rearrange("b n -> (b n)").unsqueeze(0)).then_inc(ld_tab, 16)
            sp.dma_start(b_row[0:NH, :], scr_s).then_inc(ld_bias, 16)
            sp.wait_ge(ld_tab, 16)
            sp.wait_ge(pad_done, 2)

            def load_half(b, j, half, landed):
                for n in range(8):
                    page = sp.value_load(ptab[0:1, bass.ds(b * 8 + n, 1)], min_val=0, max_val=io["cache_kv"].shape[0] - 1)
                    sp.dma_start(pages[j][n % 2 * 64:n % 2 * 64 + 64, n // 2, :, half * 512:half * 512 + 512],
                                 io["cache_kv"][bass.ds(page, 1), 0, :, 2 * half:2 * half + 2]
                                 .rearrange("o (p a) t g d -> (o p) a (t g d)", a=2)).then_inc(landed[j], 16)

            def load(b, j):
                load_half(b, j, 1, ld_pg)
                sp.dma_start(wins[j].rearrange("p t a c -> p t (a c)"),
                             io["cache_win"][0, bass.ds(b, 1)].rearrange("o (t p a) k g d -> p (o t) (a k g d)", t=2, a=2))\
                    .then_inc(ld_pg[j], 16)
                for r in range(2):
                    sp.dma_start(vnew[j][0:1, r * 256:(r + 1) * 256],
                                 scr_new[bass.ds(b, 1), 3 + 2 * r].rearrange("o g d -> o (g d)")).then_inc(ld_pg[j], 16)

            load_half(0, 0, 0, ld_cmp)
            load(0, 0)
            load_half(1, 1, 0, ld_cmp)
            load(1, 1)
            with sp.Fori(1, NB // 2) as i:
                for j in range(2):
                    sp.wait_ge(ord_done.sem, ord_done.at(i * 2 + j, -4))
                    sp.sem_inc(carrier, 1)
                    load_half(i * 2 + j, j, 0, ld_cmp)
                    sp.wait_ge(os_full.sem, os_full.at(i * 2 + j, -1))
                    sp.sem_inc(carrier, 1)
                    load(i * 2 + j, j)

        @block.gpsimd
        def _(pool):
            nc.gpsimd.memset(vnew[0], 0.0)
            nc.gpsimd.memset(vnew[1], 0.0).then_inc(pad_done, 1)
            nc.gpsimd.memset(ptn, 0.0)
            nc.gpsimd.memset(dropped, 0.0)
            nc.gpsimd.memset(qb, 0.0).then_inc(pad_done, 1)

        @block.tensor
        def _(pe):
            def turn_kv(b, j, first, lo, hi):
                for n in range(lo, hi):
                    if n % 2 == 0:
                        pe.wait_ge(ord_done.sem, ord_done.at(b, n // 2 + 1))
                    if not (first and n < 2):
                        if n == 0:
                            pe.wait_ge(ts_out.sem, ts_out.at(b, -1))
                        elif n == 1:
                            pe.wait_ge(ts_out.sem, ts_out.at(b, 0))
                        else:
                            pe.wait_ge(tk_out.sem, tk_out.at(b, n - 1))
                    for g in range(G):
                        at = (n % 2 * G + g) * P
                        mm = tr(psum[:, 4 + n % 2, g * P:(g + 1) * P], order[n // 2 % 2][:, at:at + P], P)
                    mm.then_inc(tk_full.sem, 1)

            def turn_keys(b, j, first):
                pe.wait_ge(ld_pg[j], ld_of(b, j))
                for n in range(6):
                    pe.wait_ge(tk_out.sem, tk_out.at(b, 7 + min(n, 1)))
                    if n >= 2:
                        pe.wait_ge(ts_out.sem, ts_out.at(b, n - 1))
                    for t in range(4):
                        if n < 4:
                            src = pages[j][:, t, n % 2, 512 + n // 2 * P:512 + n // 2 * P + P]
                        else:
                            src = wins[j][:, t % 2, t // 2, (n - 4) * P:(n - 4) * P + P]
                        mm = tr(psum[:, 4 + n % 2, t * P:(t + 1) * P], src, P)
                    mm.then_inc(ts_full.sem, 1)

            def compress(b, t, first):
                pe.wait_ge(tk_out.sem, tk_out.at(b, 8))
                if t:
                    pe.wait_ge(h_out.sem, h_out.at(b, 1))
                elif not first:
                    pe.wait_ge(kv_out.sem, kv_out.at(b, 0))
                for j in range(16):
                    mm = nc.tensor.matmul(psum[:, 6, t * 256:t * 256 + G * NCS],
                                          w1[:, t, j, :], kct_s[:, t, :, j:j + 8 * (NCS - 1) + 1:8],
                                          start=(j == 0), stop=(j == 15))
                mm.then_inc(h_full.sem, 1)

            def second(b, first):
                pe.wait_ge(h_out.sem, h_out.at(b, 2))
                if not first:
                    pe.wait_ge(ptb_out.sem, ptb_out.at(b, 0))
                for g in range(G):
                    nc.tensor.matmul(psum[g % 2 * DH:(g % 2 + 1) * DH, 7, 256 + g // 2 * NCS:256 + (g // 2 + 1) * NCS],
                                     w2k[:, 0:DH], hid_s[:, 0, g * NCS:(g + 1) * NCS], start=True, stop=True)
                for g in range(G):
                    mm = nc.tensor.matmul(psum[0:NCS, 6, g * DH:(g + 1) * DH], hid_s[:, 1, g * NCS:(g + 1) * NCS], w2v,
                                          start=True, stop=True)
                mm.then_inc(kv_full.sem, 1)

            def turn(b, j, more=True, first=False):
                pe.wait_ge(cur_done.sem, cur_done.at(b, 1))
                pe.wait_ge(kv_out.sem, kv_out.at(b, 2))
                pe.wait_ge(ts_out.sem, ts_out.at(b, 6))
                if not first:
                    pe.wait_ge(os_out.sem, os_out.at(b, 0))
                for a in range(2):
                    for g in range(2):
                        nc.tensor.matmul(psum[0:NH, a, :], qcur[:, g, :], kselt[:, g, a, :], start=(g == 0), stop=(g == 1))
                for g in range(2):
                    nc.tensor.matmul(psum[0:NH, 2, :], qcur[:, g, :], kwint[:, g].rearrange("p a n -> p (a n)"),
                                     start=(g == 0), stop=(g == 1))
                for r in range(2):
                    for g in range(2):
                        nc.tensor.matmul(psum[0:NH, 3, r:r + 1], qcur[:, g, :], kcur[:, r, g:g + 1],
                                         start=(g == 0), stop=(g == 1))
                for g in range(2):
                    mm = nc.tensor.matmul(psum[0:NH, 3, 64:64 + NCS], qcur[:, g, :], kcmp[:, g, :],
                                          start=(g == 0), stop=(g == 1))
                mm.then_inc(score_full.sem, 1)
                if more:
                    turn_kv(b + 1, 1 - j, False, 0, 4)
                pe.wait_ge(pc_done.sem, pc_done.at(b, 1))
                pe.wait_ge(score_used.sem, score_used.at(b, 1))
                pe.sem_inc(carrier, 1)
                tr(psum[0:NCS, 3, 0:NH], s_row[0:NH, S_CMP:S_CMP + NCS], NH)
                tr(psum[0:NCS, 3, NH:2 * NH], pcg[0:NH, :], NH).then_inc(pcT_full.sem, 1)
                if more:
                    turn_kv(b + 1, 1 - j, False, 4, 8)
                    compress(b + 1, 0, False)
                pe.wait_ge(pcT_out.sem, pcT_out.at(b, 1))
                pe.sem_inc(carrier, 1)
                nc.tensor.matmul(psum[0:NH, 3, 64:64 + NSEL], pcT[0:NCS, 0:NH], const("overlap", NCS),
                                 start=True, stop=True).then_inc(imp_full.sem, 1)
                if more:
                    turn_keys(b + 1, 1 - j, False)
                pe.wait_ge(imp_out.sem, imp_out.at(b, 1))
                pe.sem_inc(carrier, 1)
                nc.tensor.matmul(psum[0:NH, 3, 128:128 + NSEL], const("group", NH), impH[0:NH, :],
                                 start=True, stop=True).then_inc(grp_full.sem, 1)
                if more:
                    compress(b + 1, 1, False)
                pe.wait_ge(probs_done.sem, probs_done.at(b, 1))
                pe.sem_inc(carrier, 1)
                for n in range(12):
                    at = n * P if n < 8 else S_WIN + (n - 8) * P
                    tr(psum[:, 7, n * NH:(n + 1) * NH], s_row[0:NH, at:at + P], NH)
                for r, at in enumerate((S_NEWS, S_NEWW)):
                    mm = tr(psum[0:1, 7, (12 + r) * NH:(13 + r) * NH], s_row[0:NH, at:at + 1], NH)
                mm.then_inc(ptb_full.sem, 1)
                pe.wait_ge(ptb_out.sem, ptb_out.at(b, 2))
                for g in range(2):
                    def out(r):
                        o = (g * 3 + r) * NH
                        return psum[:, 2, o:o + NH]

                    nc.tensor.matmul(out(0), vcmp[0:NCS, g * P:(g + 1) * P], pcT[0:NCS, NH:2 * NH], start=True, stop=True)
                    for n in range(8):
                        nc.tensor.matmul(out(1), pages[j][:, n % 4, n // 4, 768 + g * P:768 + (g + 1) * P],
                                         ptb[:, n * NH:(n + 1) * NH], start=(n == 0), stop=False)
                    nc.tensor.matmul(out(1), vnew[j][:, g * P:(g + 1) * P], ptn[:, 0:NH], start=False, stop=True)
                    for n in range(4):
                        nc.tensor.matmul(out(2), wins[j][:, n % 2, n // 2, 256 + g * P:256 + (g + 1) * P],
                                         ptb[:, (8 + n) * NH:(9 + n) * NH], start=(n == 0), stop=False)
                    mm = nc.tensor.matmul(out(2), vnew[j][:, 256 + g * P:256 + (g + 1) * P], ptn[:, NH:2 * NH],
                                          start=False, stop=True)
                mm.then_inc(os_full.sem, 1)
                if more:
                    second(b + 1, False)

            def ld_of(b, j):
                return (b - j) * (NLD // 2) + NLD

            nc.tensor.matmul(psum[:, 7, 0:KT * NB], const("swap"), qsm.rearrange("p k b -> p (k b)"),
                             start=True, stop=True).then_inc(swap_full, 1)
            turn_kv(0, 0, True, 0, 8)
            compress(0, 0, True)
            turn_keys(0, 0, True)
            compress(0, 1, True)
            pe.wait_ge(swap_out, 1)
            second(0, True)
            pe.wait_ge(pad_done, 2)
            turn(0, 0, first=True)
            turn(1, 1)
            with pe.Fori(1, NB // 2 - 1) as i:
                turn(i * 2, 0)
                turn(i * 2 + 1, 1)
            turn(NB - 2, 0)
            turn(NB - 1, 1, more=False)
            pe.wait_ge(os_out.sem, NB)
            for h in range(2):
                mm = nc.tensor.matmul(psum[:, h, 0:384], const("swap"), o_all[:, 4 * h:4 * h + 4, :].rearrange("p b n -> p (b n)"),
                                      start=True, stop=True)
            mm.then_inc(osw_full, 1)

        @block.scalar
        def _(act):
            def kv_out_of(b, n):
                act.wait_ge(tk_full.sem, tk_full.at(b, n + 1))
                nc.scalar.activation(kct_s[:, n % 2, :, n // 2 * P:(n // 2 + 1) * P],
                                     psum[:, 4 + n % 2, :].rearrange("p (g n) -> p g n", g=G), ACT.Copy).then_inc(tk_out.sem, 1)

            def hidden(b, t):
                act.wait_ge(h_full.sem, h_full.at(b, t + 1))
                nc.scalar.activation(hid_s[:, t, :], psum[:, 6, t * 256:t * 256 + G * NCS], ACT.Silu,
                                     bias=pebias[:, t:t + 1]).then_inc(h_out.sem, 1)

            def second_out(b):
                act.wait_ge(kv_full.sem, kv_full.at(b, 1))
                nc.scalar.activation(kcmp, psum[:, 7, 256:256 + 2 * NCS].rearrange("p (h n) -> p h n", h=2), ACT.Copy).then_inc(kv_out.sem, 1)
                nc.scalar.activation(vcmp[0:NCS, :], psum[0:NCS, 6, 0:256], ACT.Copy).then_inc(kv_out.sem, 1)

            def turn(b, more=True):
                if more:
                    act.wait_ge(h_full.sem, h_full.at(b, 2))
                    for n in range(4):
                        kv_out_of(b + 1, n)
                act.wait_ge(c_ready.sem, c_ready.at(b, 1))
                nc.scalar.activation(s_row[0:NH, S_CMP:S_CMP + NCS], s_row[0:NH, S_CMP:S_CMP + NCS], ACT.Exp,
                                     bias=stat[0:NH, 0:1], accum_out=stat[0:NH, 1:2]).then_inc(c_exp.sem, 1)
                if more:
                    for n in range(4, 8):
                        kv_out_of(b + 1, n)
                act.wait_ge(w_ready.sem, w_ready.at(b, 1))
                nc.scalar.activation(s_row[0:NH, S_WIN:S_CMP], s_row[0:NH, S_WIN:S_CMP], ACT.Exp,
                                     bias=stat[0:NH, 4:5], accum_out=stat[0:NH, 5:6]).then_inc(w_exp.sem, 1)
                if more:
                    hidden(b + 1, 0)
                act.wait_ge(sel_ready.sem, sel_ready.at(b, 1))
                nc.scalar.activation(s_row[0:NH, S_SEL:S_WIN], s_row[0:NH, S_SEL:S_WIN], ACT.Exp,
                                     bias=stat[0:NH, 8:9], accum_out=stat[0:NH, 9:10]).then_inc(sel_exp.sem, 1)
                if more:
                    hidden(b + 1, 1)
                act.wait_ge(ptb_full.sem, ptb_full.at(b, 1))
                nc.scalar.activation(ptb, psum[:, 7, 0:12 * NH], ACT.Copy).then_inc(ptb_out.sem, 1)
                nc.scalar.activation(ptn[0:1, :], psum[0:1, 7, 12 * NH:14 * NH], ACT.Copy).then_inc(ptb_out.sem, 1)
                if more:
                    act.wait_ge(os_full.sem, os_full.at(b, 1))
                    second_out(b + 1)

            act.wait_ge(swap_full, 1)
            nc.scalar.activation(qsw, psum[:, 7, 0:KT * NB].rearrange("p (k b) -> p k b", k=KT), ACT.Copy).then_inc(swap_out, 1)
            act.wait_ge(pad_done, 2)
            for n in range(8):
                kv_out_of(0, n)
            hidden(0, 0)
            hidden(0, 1)
            second_out(0)
            with act.Fori(0, NB - 1) as b:
                turn(b)
            turn(NB - 1, more=False)

        @block.vector
        def _(dve):
            def current(b):
                nc.vector.tensor_copy(qcur, qb[:, :, :, bass.ds(b, 1)].rearrange("p g h o -> p g (h o)"))
                k4 = kns.rearrange("p r (h e) b -> p r h e b", e=2)
                for e in range(2):
                    lo = slice(e * 64, e * 64 + 64)
                    ins = nc.vector.tensor_copy(kcur[lo], k4[lo, :, :, e, bass.ds(b, 1)].rearrange("p r h o -> p r (h o)"))
                ins.then_inc(cur_done.sem, 1)

            def ordered(b, j, t):
                if t == 0:
                    dve.wait_ge(ld_cmp[j], (b - j) * 64 + 128)
                if t >= 2:
                    dve.wait_ge(tk_full.sem, tk_full.at(b, 2 * t - 2))
                nc.vector.tensor_copy(order[t % 2].rearrange("p (c a d) -> p a c d", a=2, d=DH),
                                      pages[j][:, t, :, 0:512].rearrange("p a (c d) -> p a c d", d=DH)).then_inc(ord_done.sem, 1)

            def keys_out_of(b, n):
                dve.wait_ge(ts_full.sem, ts_full.at(b, n + 1))
                dst = kselt[:, n // 2, n % 2, :] if n < 4 else kwint[:, n - 4].rearrange("p a n -> p (a n)")
                nc.vector.tensor_copy(dst, psum[:, 4 + n % 2, :]).then_inc(ts_out.sem, 1)

            def turn(b, j, more=True, first=False):
                s = Steps(dve, dve_smp)
                s.turn(b)
                if more:
                    for t in range(2):
                        if not first:
                            dve.wait_ge(tk_full.sem, tk_full.at(b + 1, 0))
                        ordered(b + 1, 1 - j, t)
                row = s_row[0:NH]
                bias = b_row[0:NH]
                dve.wait_ge(score_full.sem, score_full.at(b, 1))
                if not (isinstance(b, int) and b == 0):
                    dve.wait_ge(ptb_full.sem, ptb_full.at(b, 0))
                s.link(nc.vector.tensor_tensor(row[:, S_CMP:], psum[0:NH, 3, 64:64 + NCS], bias[:, S_CMP:], ALU.add))
                s.link(nc.vector.tensor_reduce(stat[0:NH, 0:1], row[:, S_CMP:], AX.X, ALU.max))
                s.post(nc.vector.tensor_scalar(stat[0:NH, 0:1], stat[0:NH, 0:1], -1.0, None, ALU.mult), c_ready)
                nc.vector.tensor_tensor(row[:, S_NEWS:S_NEWS + 1], psum[0:NH, 3, 0:1], bias[:, S_NEWS:S_NEWS + 1], ALU.add)
                nc.vector.tensor_tensor(row[:, S_NEWW:S_NEWW + 1], psum[0:NH, 3, 1:2], bias[:, S_NEWW:S_NEWW + 1], ALU.add)
                nc.vector.tensor_tensor(row[:, S_WIN:S_NEWW], psum[0:NH, 2, :], bias[:, S_WIN:S_NEWW], ALU.add)
                s.link(nc.vector.tensor_tensor(row[:, S_SEL:S_NEWS].rearrange("p (a n) -> p a n", a=2), psum[0:NH, 0:2, :],
                                               bias[:, S_SEL:S_NEWS].rearrange("p (a n) -> p a n", a=2), ALU.add), score_used)
                s.link(nc.vector.tensor_reduce(stat[0:NH, 4:5], row[:, S_WIN:S_CMP], AX.X, ALU.max))
                s.post(nc.vector.tensor_scalar(stat[0:NH, 4:5], stat[0:NH, 4:5], -1.0, None, ALU.mult), w_ready)
                dve.wait_ge(c_exp.sem, c_exp.at(b, 1))
                s.link(nc.vector.reciprocal(stat[0:NH, 2:3], stat[0:NH, 1:2]))
                s.link(nc.vector.tensor_scalar(row[:, S_CMP:], row[:, S_CMP:], stat[0:NH, 2:3], None, ALU.mult))
                s.post(nc.vector.tensor_scalar(pcg[0:NH, :], row[:, S_CMP:], gsm[0:NH, 0, bass.ds(b, 1)], None, ALU.mult),
                       pc_done)
                if more:
                    for t in range(2, 4):
                        ordered(b + 1, 1 - j, t)
                dve.wait_ge(pcT_full.sem, pcT_full.at(b, 1))
                s.post(nc.vector.tensor_copy(pcT[0:NCS, :], psum[0:NCS, 3, 0:2 * NH]), pcT_out)
                dve.wait_ge(imp_full.sem, imp_full.at(b, 1))
                s.post(nc.vector.tensor_copy(impH[0:NH, :], psum[0:NH, 3, 64:64 + NSEL]), imp_out)
                if more:
                    for n in range(6):
                        keys_out_of(b + 1, n)
                dve.wait_ge(grp_full.sem, grp_full.at(b, 1))
                s.link(nc.vector.tensor_reduce(stat[0:NH, 3:4], psum[0:NH, 3, 129:143], AX.X, ALU.min))
                s.link(nc.vector.tensor_scalar(cand[0:NH, :], psum[0:NH, 3, 129:143], stat[0:NH, 3:4], None, ALU.is_le))
                s.link(nc.vector.tensor_tensor(keyed[0:NH, :], cand[0:NH, :], const("order", NH), ALU.mult))
                s.link(nc.vector.tensor_reduce(stat[0:NH, 7:8], keyed[0:NH, :], AX.X, ALU.max))
                s.link(nc.vector.tensor_scalar(dropped[0:NH, 1:15], keyed[0:NH, :], stat[0:NH, 7:8], NEG, ALU.is_equal, ALU.mult))
                sel = row[:, S_SEL:S_NEWS].rearrange("p (a s n) -> p a s n", a=2, s=16)
                s.link(nc.vector.tensor_tensor(sel, sel, dropped[0:NH, :].unsqueeze(1).unsqueeze(3).to_broadcast([NH, 2, 16, 32]),
                                               ALU.add))
                s.link(nc.vector.tensor_reduce(stat[0:NH, 8:9], row[:, S_SEL:S_WIN], AX.X, ALU.max))
                s.post(nc.vector.tensor_scalar(stat[0:NH, 8:9], stat[0:NH, 8:9], -1.0, None, ALU.mult), sel_ready)
                dve.wait_ge(w_exp.sem, w_exp.at(b, 1))
                s.link(nc.vector.reciprocal(stat[0:NH, 6:7], stat[0:NH, 5:6]))
                s.link(nc.vector.tensor_scalar(row[:, S_WIN:S_CMP], row[:, S_WIN:S_CMP], stat[0:NH, 6:7],
                                               gsm[0:NH, 2, bass.ds(b, 1)], ALU.mult, ALU.mult))
                dve.wait_ge(sel_exp.sem, sel_exp.at(b, 1))
                s.link(nc.vector.reciprocal(stat[0:NH, 10:11], stat[0:NH, 9:10]))
                s.link(nc.vector.tensor_scalar(row[:, S_SEL:S_WIN], row[:, S_SEL:S_WIN], stat[0:NH, 10:11],
                                               gsm[0:NH, 1, bass.ds(b, 1)], ALU.mult, ALU.mult), probs_done)
                if more:
                    current(b + 1)
                dve.wait_ge(os_full.sem, os_full.at(b, 1))
                s.link(nc.vector.tensor_copy(o_all[:, bass.ds(b, 1), :].rearrange("p o n -> p (o n)"), psum[:, 2, 0:6 * NH]), os_out)
                s.turn(b)

            dve.wait_ge(pad_done, 2)
            dve.wait_ge(swap_out, 1)
            dve.wait_ge(ld_bias, 16)
            for gp in range(2):
                for g2 in range(2):
                    lo = slice(g2 * 64, g2 * 64 + 64)
                    for h2 in range(2):
                        src = qsm if g2 == h2 else qsw
                        g = 2 * gp + g2
                        ins = nc.vector.tensor_copy(qb[lo, gp, 4 * g + h2:4 * g + 4:2, :], src[lo, 2 * g:2 * g + 2, :])
            ins.then_inc(qb_done, 1)
            dve.wait_ge(qb_done, 1)
            current(0)
            for t in range(4):
                ordered(0, 0, t)
            for n in range(6):
                keys_out_of(0, n)
            turn(0, 0)
            turn(1, 1)
            with dve.Fori(1, NB // 2 - 1) as i:
                turn(i * 2, 0)
                turn(i * 2 + 1, 1)
            turn(NB - 2, 0)
            turn(NB - 1, 1, more=False)
            dve.wait_ge(osw_full, 1)
            nc.vector.tensor_copy(o_swp.rearrange("p (h b) n -> p h (b n)", h=2), psum[:, 0:2, 0:384]).then_inc(osw_out, 1)
            dve.wait_ge(osw_out, 1)
            s = Steps(dve, dve_end)
            s.turn(0)
            for r in range(3):
                for gp in range(2):
                    for g2 in range(2):
                        g = 2 * gp + g2
                        for h2 in range(2):
                            lo = slice(h2 * 64, h2 * 64 + 64)
                            src = o_all if g2 == h2 else o_swp
                            at = (gp * 3 + r) * NH + 4 * g + h2
                            ins = nc.vector.tensor_tensor((mtmp if r else msm)[lo, 2 * g:2 * g + 2, :],
                                                          src[lo, :, at:at + 3:2].rearrange("p b i -> p i b"),
                                                          zsm[lo, r, 2 * g:2 * g + 2, :], ALU.mult)
                s.link(ins)
                if r:
                    s.link(nc.vector.tensor_tensor(msm, msm, mtmp, ALU.add))
            s.link(nc.vector.tensor_copy(mixed[:, :, SEQ:T], msm))
            s.turn(0)


    arena.at = base_smp
    std2, rstd2 = take(T), take(T)
    w_rooms = [take(KT * 256).rearrange("p (k n) -> p k n", k=KT) for _ in range(2)]
    project_out("o2", KT, mixed, io["nsa_w_out"][0], w_rooms, PR_NF)
    ytok = take(4 * D).rearrange("p (a d) -> p a d", a=4)
    ysamp = take(D)
    y_full, y_out, st_y = sem("y_full"), sem("y_out"), sem("st_y")
    with nc.Block() as block:
        @block.tensor
        def _(pe):
            for j in range(10):
                if j >= 8:
                    pe.wait_ge(y_out, j - 7)
                a, half = j // 2, j % 2
                for c in range(4):
                    k = half * 4 + c
                    if a < 4:
                        mm = tr(psum[:, j % 8, c * P:(c + 1) * P], xn[:, k, a * P:(a + 1) * P], P)
                    else:
                        mm = tr(psum[0:NB, j % 8, c * P:(c + 1) * P], xn[:, k, SEQ:T], P)
                mm.then_inc(y_full, 1)

        @block.scalar
        def _(act):
            for j in range(10):
                act.wait_ge(y_full, j + 1)
                a, half = j // 2, j % 2
                cols = slice(half * 512, half * 512 + 512)
                if a < 4:
                    nc.scalar.activation(ytok[:, a, cols], psum[:, j % 8, :], ACT.Copy).then_inc(y_out, 1)
                else:
                    nc.scalar.activation(ysamp[0:NB, cols], psum[0:NB, j % 8, :], ACT.Copy).then_inc(y_out, 1)

        @block.sync
        def _(sp):
            for a in range(4):
                sp.wait_ge(y_out, 2 * a + 2)
                sp.dma_start(io["y_prompt"][0, a * P:(a + 1) * P, :], ytok[:, a, :]).then_inc(st_y, 16)
            sp.wait_ge(y_out, 10)
            sp.dma_start(io["y_sample"].rearrange("b s d -> (b s) d"), ysamp[0:NB, :]).then_inc(st_y, 16)
            sp.wait_ge(st_y, 80)


INS = ['x_prompt', 'x_sample', 'state_ssm', 'state_conv', 'cache_kv', 'cache_win', 'page_table', 'rel_bias',
       'final_norm', 'ssd_norm', 'ssd_w_in', 'ssd_conv_w', 'ssd_conv_b', 'ssd_dt_bias', 'ssd_a_log', 'ssd_d',
       'ssd_gnorm', 'ssd_w_out', 'nsa_norm', 'nsa_w_in', 'nsa_cmp_pe', 'nsa_cmp_w1', 'nsa_cmp_w2', 'nsa_w_out']
OUTS = [("y_prompt", (1, SEQ, D)), ("y_sample", (NB, 1, D)), ("ssm_prompt", (1, 1, SH, SP_, SN)),
        ("conv_prompt", (1, 1, 3, CONV)), ("kv_prompt", (1, SEQ, 1, 4, G, DH)), ("win_prompt", (1, 1, 512, 2, G, DH)),
        ("ssm_sample", (1, NB, SH, SP_, SN)), ("conv_sample", (1, NB, 3, CONV)),
        ("kv_sample", (NB, 1, 1, 4, G, DH)), ("win_sample", (1, NB, 512, 2, G, DH))]


def kernel(**inputs):
    import concourse.bacc as _bacc
    from concourse.bass_utils import run_bass_kernel_spmd as _run

    nc = _bacc.Bacc("TRN2", target_bir_lowering=False, num_devices=1)
    arrays = {name: np.ascontiguousarray(inputs[name]) for name in INS}
    arrays["const_a"], arrays["const_b"] = constants()
    io = {name: nc.dram_tensor("in_" + name, a.shape, mybir.dt.from_np(a.dtype), kind="ExternalInput").ap()
          for name, a in arrays.items()}
    for name, shape in OUTS:
        io[name] = nc.dram_tensor("out_" + name, shape, F32, kind="ExternalOutput").ap()
    build(nc, io)
    r = _run(nc, [{"in_" + name: a for name, a in arrays.items()}], core_ids=[0])
    return tuple(r.results[0]["out_" + name] for name, _shape in OUTS)
```

```python
from contextlib import ExitStack

import numpy as np

import concourse.bass as bass
from concourse import mybir

ALU = mybir.AluOpType
ACT = mybir.ActivationFunctionType
F32 = mybir.dt.float32
I32 = mybir.dt.int32
AX = mybir.AxisListType

P = 128
D = 1024
KT = D // P
SEQ = 512
NB = 8
T = SEQ + NB
HALF = T // 2
PAST = 1024
EPS = 1e-6
NEG = -1e30
GUARD = -1e20

DI = 2 * D
SH = 32
SP_ = 64
SG = 8
SN = 128
CH = 128
NCH = SEQ // CH
CONV = DI + 2 * SG * SN
IN1 = DI + CONV + SH
CT = CONV // P

NH = 16
G = 4
R = 4
DH = 64
AW = NH * DH
GATE0 = AW + 6 * G * DH
Z0 = GATE0 + 3 * NH
NCP = (SEQ - 32) // 16 + 1
NCS = (PAST + 1 - 32) // 16 + 1
NPAIR = PAST // 2
NWP = 512 // 2
SKEYS = PAST + 1
WKEYS = 512 + 1
NSEL = 17
KEYS = SKEYS + WKEYS + NCS
FLEN = 1023

CA = {}
_n = 0
for _name, _w in (("ident", P), ("ones", P), ("swap", P), ("group", NH), ("overlap", NSEL), ("order", 14),
                  ("causal", P), ("last", P), ("head", 4 * P), ("pair", 2 * P), ("samp", NB * P)):
    CA[_name] = (_n, _n + _w)
    _n += _w
CA_W = _n
CB_F, CB_S, CB_W = 0, FLEN, FLEN + KEYS
PR_N1, PR_N2, PR_NF, PR_CB, PR_GN, PR_W = 0, 8, 16, 24, 56, 72


def buckets(dist):
    n = np.maximum(dist, 0)
    logv = np.log(np.maximum(n, 1).astype(np.float32) / np.float32(16)) / np.float32(np.log(64.0))
    large = np.minimum(16 + (logv.astype(np.float32) * np.float32(16)).astype(np.int32), 31)
    return np.where(n < 16, n, large)


def constants():
    a = np.zeros((P, CA_W), np.float32)

    def put(name, x):
        a[:x.shape[0], CA[name][0]:CA[name][0] + x.shape[1]] = x

    i = np.arange(P)
    put("ident", np.eye(P))
    put("ones", np.ones((P, P)))
    put("causal", (i[None, :] >= i[:, None]))
    put("swap", (i[None, :] == (i[:, None] + 64) % P))
    put("last", np.repeat((i == P - 1)[:, None], P, 1))
    put("head", np.repeat(np.eye(4), P, 1))
    put("pair", np.stack([(np.arange(4)[:, None] == 2 * hp + i[None, :] // 64) for hp in range(2)], 1).reshape(4, -1))
    put("samp", np.repeat(np.eye(NB), P, 1))
    put("group", np.kron(np.eye(G), np.ones((R, R))))
    c0 = np.arange(NCS) * 16
    s0 = np.arange(NSEL) * 64
    ov = np.minimum(c0[:, None] + 31, s0[None] + 63) - np.maximum(c0[:, None], s0[None]) + 1
    put("overlap", np.maximum(ov, 0) / 16.0)
    put("order", np.repeat(np.arange(1, 15)[None], NH, 0))
    b = np.zeros((33, CB_W), np.float32)

    def onehot(at, dist):
        row = np.where(dist < 0, 32, buckets(dist))
        b[row, at + np.arange(len(dist))] = 1

    onehot(CB_F, np.arange(FLEN) - 511)
    pairs = np.arange(NPAIR)
    wp = np.arange(NWP)
    pos = np.concatenate([2 * pairs, 2 * pairs + 1, [PAST], PAST - 512 + 2 * wp, PAST - 512 + 2 * wp + 1, [PAST],
                          c0 + 31])
    onehot(CB_S, PAST - pos)
    return a, b


class Signal:

    def __init__(self, sem, per):
        self.sem, self.per, self.count = sem, per, 0

    def at(self, turn, n):
        return turn * self.per + n


class Steps:

    def __init__(self, eng, own):
        self.eng, self.own, self.used = eng, own, []

    def turn(self, i):
        for s in self.used:
            assert s.count == s.per, (s.sem, s.count, s.per)
            s.count = 0
        self.i, self.used = i, []

    def post(self, ins, sig=None):
        s = sig or self.own
        if s not in self.used:
            self.used.append(s)
        s.count += 1
        ins.then_inc(s.sem, 1)
        return s

    def link(self, ins, sig=None):
        s = self.post(ins, sig)
        self.eng.wait_ge(s.sem, s.at(self.i, s.count))


class Arena:

    def __init__(self, block, size):
        self.block, self.size, self.at = block, size, 0

    def take(self, n):
        a = self.at
        self.at += n
        assert self.at <= self.size, (self.at, self.size)
        return self.block[:, a:a + n]

    def take_top(self, n):
        self.size -= n
        assert self.at <= self.size, (self.at, self.size)
        return self.block[:, self.size:self.size + n]


def halves(psum, bank, parts=P):
    return psum[0:parts, bank:bank + 2, 0:HALF]


def build(nc, io):
    ctx = ExitStack()
    with ctx:
        _build(nc, io, ctx)


def _build(nc, io, ctx):
    stage_sems = []

    def sem(name):
        stage_sems.append(nc.alloc_semaphore(name=name))
        return stage_sems[-1]

    def free_semaphores():
        nc.clear_and_free_semaphores(stage_sems)
        nc.all_engine_barrier()
        stage_sems.clear()

    def sig(name, per=1):
        return Signal(sem(name), per)

    ARENA = 52200
    arena = Arena(ctx.enter_context(nc.sbuf_tensor("arena", [P, ARENA], F32)), ARENA)
    take = arena.take
    psum = ctx.enter_context(nc.psum_tensor("psum", [P, 8, 512], F32))

    scr_rows = nc.dram_tensor("scr_rows", [SH, 2, T], F32).ap()
    scr_f = nc.dram_tensor("scr_f", [NH, FLEN], F32).ap()
    scr_s = nc.dram_tensor("scr_s", [NH, KEYS], F32).ap()

    scr_new = nc.dram_tensor("scr_new", [NB, 6, G, DH], F32).ap()

    ca = take(CA_W)

    def const(name, rows=P):
        return ca[0:rows, CA[name][0]:CA[name][1]]

    ident, ones = const("ident"), const("ones")
    pT = take(PR_W)
    xT = take(KT * T).rearrange("p (k t) -> p k t", k=KT)
    xn_at = arena.at
    xn = take(KT * T).rearrange("p (k t) -> p k t", k=KT)
    base_all = arena.at

    cw = take(P)
    dsk = take(DI // P)
    st = take(CT * NB * 3).rearrange("p (c b t) -> p c b t", c=CT, b=NB)
    tail = take(CT * 11).rearrange("p (c n) -> p c n", c=CT)
    acs_tok = take(NCH * SH).rearrange("p (c h) -> p c h", c=NCH)
    toend = take(NCH * SH).rearrange("p (c h) -> p c h", c=NCH)
    decay = take(NCH * SH).rearrange("p (c h) -> p c h", c=NCH)

    yT = take(DI // P * T).rearrange("p (k t) -> p k t", k=DI // P)
    base_y = arena.at
    wx = take(KT * 256).rearrange("p (k n) -> p k n", k=KT)
    wbc = take(KT * 256).rearrange("p (k n) -> p k n", k=KT)
    wz = take(KT * 256).rearrange("p (k n) -> p k n", k=KT)
    raw = take(4 * (3 + T)).rearrange("p (c t) -> p c t", c=4)
    zraw = take(2 * T).rearrange("p (c t) -> p c t", c=2)
    base_turn = arena.at
    ld_wx, ld_wbc, ld_wz = sem("ld_wx"), sem("ld_wbc"), sem("ld_wz")
    tile_full = sig("tile_full", 6)
    tile_out = sig("tile_out", 6)
    w_in = io["ssd_w_in"][0].rearrange("(k p) n -> p k n", p=P)

    def weights_x(sp, g):
        sp.dma_start(wx, w_in[:, :, bass.ds(g * 256 + DI, 256)]).then_inc(ld_wx, 16)

    def weights_bc(sp, g):
        sp.dma_start(wbc[:, :, 0:P], w_in[:, :, bass.ds(g * P + 2 * DI, P)]).then_inc(ld_wbc, 16)
        sp.dma_start(wbc[:, :, P:256], w_in[:, :, bass.ds(g * P + 2 * DI + SG * SN, P)]).then_inc(ld_wbc, 16)

    def weights_z(sp, g):
        sp.dma_start(wz, w_in[:, :, bass.ds(g * 256, 256)]).then_inc(ld_wz, 16)

    def keep_window(sp, b):
        sp.dma_start(io["win_sample"][0, bass.ds(b, 1), 0:511].rearrange("o t k g d -> (o t) (k g d)"),
                     io["cache_win"][0, bass.ds(b, 1), 1:512].rearrange("o t k g d -> (o t) (k g d)")).then_inc(st_pass, 16)

    def ssd_project(pe, g, n, first=False, part=None):
        w, s, per = ((wx, ld_wx, 16), (wbc, ld_wbc, 32), (wz, ld_wz, 16))[n // 2]
        if part != 1:
            if n % 2 == 0:
                pe.wait_ge(s, g * per + per)
            if not (first and n < 2):
                pe.wait_ge(tile_out.sem, tile_out.at(g, n - 1))
        b = n % 2 * 2
        for h in range(2) if part is None else (part,):
            for k in range(KT):
                mm = nc.tensor.matmul(psum[:, b + h, 0:HALF], w[:, k, n % 2 * P:(n % 2 + 1) * P],
                                      xn[:, k, h * HALF:(h + 1) * HALF], start=(k == 0), stop=(k == KT - 1))
        if part != 0:
            mm.then_inc(tile_full.sem, 1)

    def ssd_evacuate(act, g, n):
        act.wait_ge(tile_full.sem, tile_full.at(g, n + 1))
        dst = raw[:, n, 3:3 + T] if n < 4 else zraw[:, n - 4, :]
        nc.scalar.activation(dst.rearrange("p (h t) -> p h t", h=2), halves(psum, n % 2 * 2),
                             ACT.Copy).then_inc(tile_out.sem, 1)

    cb = take(CB_W)
    xtok = take(4 * D).rearrange("p (a d) -> p a d", a=4)
    xsmp = take(D)
    prow = take(P)
    crow = take(P)
    srow = take(CONV)
    drow = take(16)
    rel = take(NH)
    brow = take(CB_W)
    hcol = take(3)
    wdt = take(KT * SH).rearrange("p (k n) -> p k n", k=KT)
    raw_dt = take(T)
    low = take(T)
    rows = take(2 * T).rearrange("p (r t) -> p r t", r=2)
    dta = take(T)
    std = take(T)
    rstd = take(T)
    sumsq0 = take(T)

    ld_const, ld_prm, ld_conv, ld_rel, ld_dt = (sem(n) for n in ("ld_const", "ld_prm", "ld_conv", "ld_rel", "ld_dt"))
    ld_x = [sem(f"ld_x{a}") for a in range(5)]
    st_scr = sem("st_scr")
    st_pass = sem("st_pass")
    job_done, job_out = sem("job_done"), sem("job_out")
    sq_done, ssq_done, var_done, std_done, xn_done = (sem(n) for n in (
        "sq_done", "ssq_done", "var_done", "std_done", "xn_done"))
    rel_mask = sem("rel_mask")
    summed = sem("summed")
    dtraw_done, dtlow_done, dtln_done, rows_done, acs_done, acst_done, last_done, te_done, dec_done = (
        sem(n) for n in ("dtraw_done", "dtlow_done", "dtln_done", "rows_done", "acs_done",
                         "acst_done", "last_done", "te_done", "dec_done"))
    act_setup, dve_setup = sig("act_setup"), sig("dve_setup", 3)

    pieces = [(a, min(a + 512, b)) for lo, b in ((CB_F, CB_S), (CB_S, CB_W)) for a in range(lo, b, 512)]
    jobs = []

    def bank(j):
        return psum[:, j % 8, :]

    def tr(out, in_, k):
        return nc.tensor.transpose(out, in_, ident[0:k, 0:k])

    for a in range(4):
        for half in range(2):
            jobs.append((lambda b, a=a, half=half: [tr(b[:, c * P:(c + 1) * P],
                                                       xtok[:, a, (half * 4 + c) * P:(half * 4 + c + 1) * P], P)
                                                    for c in range(4)],
                         xT[:, half * 4:half * 4 + 4, a * P:(a + 1) * P], lambda b: b.rearrange("p (c n) -> p c n", c=4),
                         (ld_x[a], 16)))
    jobs.append((lambda b: [tr(b[:, kt * NB:(kt + 1) * NB], xsmp[0:NB, kt * P:(kt + 1) * P], NB) for kt in range(KT)],
                 xT[:, :, SEQ:T], lambda b: b[:, 0:KT * NB].rearrange("p (k b) -> p k b", k=KT), (ld_x[4], 16)))
    jobs.append((lambda b: [tr(b[:, 0:PR_W], prow[0:PR_W, :], PR_W)], pT, lambda b: b[:, 0:PR_W], (ld_prm, 128)))
    n_norm = len(jobs)
    for lo, hi in pieces:
        jobs.append((lambda b, lo=lo, hi=hi: [nc.tensor.matmul(b[0:NH, 0:hi - lo], rel[0:33, :], cb[0:33, lo:hi],
                                                               start=True, stop=True)],
                     brow[0:NH, lo:hi], lambda b, lo=lo, hi=hi: b[0:NH, 0:hi - lo], (ld_rel, 32)))
    n_bias = len(jobs)
    jobs.append((lambda b: [tr(b[:, 0:P], crow, P)], cw, lambda b: b[:, 0:P], (ld_prm, 128)))
    jobs.append((lambda b: [nc.tensor.matmul(b[:, 0:16], const("pair", 2)[:, 0:P], drow[0:2, :], start=True, stop=True)],
                 dsk, lambda b: b[:, 0:16], (ld_prm, 128)))
    for lo, hi in ((0, 16), (16, 32)):
        jobs.append((lambda b, lo=lo, hi=hi: [tr(b[:, (c - lo) * 24:(c - lo + 1) * 24], srow[0:24, c * P:(c + 1) * P], 24)
                                              for c in range(lo, hi)],
                     st[:, lo:hi], lambda b: b[:, 0:16 * 24].rearrange("p (c b t) -> p c b t", c=16, b=NB), (ld_conv, 16)))

    def job_bank(j):
        return bank(j) if j <= n_norm else psum[:, j % 4, :] if j < n_bias else psum[:, 6 + j % 2, :]

    with nc.Block() as block:
        @block.sync
        def _(sp):
            sp.dma_start(ca[:, 0:256], io["const_a"][:, 0:256]).then_inc(ld_const, 16)
            for a in range(4):
                sp.dma_start(xtok[:, a, :], io["x_prompt"][0, a * P:(a + 1) * P, :]).then_inc(ld_x[a], 16)
            sp.dma_start(xsmp[0:NB, :], io["x_sample"].rearrange("b s d -> (b s) d")).then_inc(ld_x[4], 16)
            for at, name, n in ((PR_N1, "ssd_norm", 8), (PR_N2, "nsa_norm", 8), (PR_CB, "ssd_conv_b", 32),
                                (PR_GN, "ssd_gnorm", 16)):
                sp.dma_start(prow[at:at + n, :], io[name][0].rearrange("(r c) -> r c", c=P)).then_inc(ld_prm, 16)
            sp.dma_start(prow[PR_NF:PR_NF + 8, :], io["final_norm"].rearrange("(r c) -> r c", c=P)).then_inc(ld_prm, 16)
            sp.dma_start(crow[:, :], io["ssd_conv_w"][0].rearrange("k (r c) -> (k r) c", c=P)).then_inc(ld_prm, 16)
            for h2 in range(2):
                sp.dma_start(drow[h2:h2 + 1, :], bass.AP(io["ssd_d"].tensor, h2, [[SH, 1], [2, 16]]),
                             allow_slow_non_contiguous=True).then_inc(ld_prm, 16)
            for c, name in enumerate(("ssd_dt_bias", "ssd_a_log")):
                sp.dma_start(hcol[0:SH, c:c + 1], io[name].rearrange("a h -> h a"),
                             allow_slow_non_contiguous=True).then_inc(ld_dt, 16)
            sp.dma_start(wdt, io["ssd_w_in"][0][:, IN1 - SH:IN1].rearrange("(k p) n -> p k n", p=P)).then_inc(ld_dt, 16)
            sp.dma_start(srow[0:24, :], io["state_conv"][0].rearrange("b t c -> (b t) c")).then_inc(ld_conv, 16)
            sp.dma_start(cb[0:33, :], io["const_b"]).then_inc(ld_rel, 16)
            sp.dma_start(rel[0:32, :], io["rel_bias"]).then_inc(ld_rel, 16)
            weights_x(sp, 0)
            sp.dma_start(ca[:, 256:], io["const_a"][:, 256:]).then_inc(ld_const, 16)
            weights_bc(sp, 0)
            weights_z(sp, 0)
            sp.dma_start(io["conv_sample"][0][:, 0:2, :], io["state_conv"][0][:, 1:3, :]).then_inc(st_pass, 16)
            sp.wait_ge(job_out, n_bias)
            sp.dma_start(scr_f, brow[0:NH, CB_F:CB_S]).then_inc(st_scr, 16)
            sp.dma_start(scr_s, brow[0:NH, CB_S:CB_W]).then_inc(st_scr, 16)
            sp.wait_ge(rows_done, 6)
            sp.dma_start(scr_rows, rows[0:SH]).then_inc(st_scr, 16)
            sp.wait_ge(st_scr, 48)

        @block.tensor
        def _(pe):
            pe.wait_ge(ld_const, 16)
            for j, (emit, _dst, _src, (s, v)) in enumerate(jobs):
                pe.wait_ge(s, v)
                if s is ld_rel:
                    pe.wait_ge(rel_mask, 1)
                if j >= 8:
                    pe.wait_ge(job_out, j - 7)
                emit(bank(j))[-1].then_inc(job_done, 1)
                if j == n_norm:
                    break
            def job(j):
                _emit, (s, v) = jobs[j][0], jobs[j][3]
                pe.wait_ge(s, v)
                if s is ld_rel:
                    pe.wait_ge(rel_mask, 1)
                _emit(job_bank(j))[-1].then_inc(job_done, 1)

            for j in range(n_norm + 1, n_norm + 4):
                pe.wait_ge(job_out, n_norm + 1)
                job(j)
            pe.wait_ge(summed, KT - 1)
            for h in range(2):
                mm = nc.tensor.matmul(psum[:, 6 + h, 0:HALF], ones, sumsq0[:, h * HALF:(h + 1) * HALF],
                                      start=True, stop=True)
            mm.then_inc(ssq_done, 1)
            for j in range(n_norm + 4, n_bias):
                pe.wait_ge(job_out, j - 3)
                job(j)
            pe.wait_ge(ld_dt, 48)
            for h in range(2):
                for k in range(KT):
                    if h == 0:
                        pe.wait_ge(xn_done, k + 1)
                    mm = nc.tensor.matmul(psum[0:SH, 4 + h, 0:HALF], wdt[:, k, :], xn[:, k, h * HALF:(h + 1) * HALF],
                                          start=(k == 0), stop=(k == KT - 1))
            mm.then_inc(dtraw_done, 1)
            pe.wait_ge(job_out, n_bias)
            pe.wait_ge(ld_const, 32)
            ssd_project(pe, 0, 0, True)
            ssd_project(pe, 0, 1, True)
            job(n_bias)
            job(n_bias + 1)
            ssd_project(pe, 0, 2, True)
            pe.wait_ge(rows_done, 6)
            for c in range(NCH):
                mm = tr(psum[:, 4, c * SH:(c + 1) * SH], rows[0:SH, 1, c * CH:(c + 1) * CH], SH)
            mm.then_inc(acs_done, 1)
            ssd_project(pe, 0, 3, True)
            pe.wait_ge(acst_done, 1)
            nc.tensor.matmul(psum[:, 5, 0:NCH * SH], const("last"), acs_tok, start=True, stop=True).then_inc(last_done, 1)
            ssd_project(pe, 0, 4, True)
            pe.wait_ge(job_out, n_bias + 2)
            job(n_bias + 2)
            job(n_bias + 3)
            ssd_project(pe, 0, 5, True)

        @block.scalar
        def _(act):
            def job_evac(j):
                act.wait_ge(job_done, j + 1)
                nc.scalar.activation(jobs[j][1], jobs[j][2](job_bank(j)), ACT.Copy).then_inc(job_out, 1)

            for j in range(n_norm + 1):
                job_evac(j)
            act.wait_ge(job_out, n_norm)
            for k in range(KT):
                nc.scalar.activation(xn[:, k, :], xT[:, k, :], ACT.Square).then_inc(sq_done, 1)
            act.wait_ge(var_done, 1)
            nc.scalar.activation(std, std, ACT.Sqrt).then_inc(std_done, 1)
            for j in range(n_norm + 1, n_bias):
                job_evac(j)
            s = Steps(act, act_setup)
            s.turn(0)
            act.wait_ge(ld_dt, 48)
            s.post(nc.scalar.activation(hcol[0:SH, 2:3], hcol[0:SH, 1:2], ACT.Exp))
            act.wait_ge(dtlow_done, 1)
            s.link(nc.scalar.activation(low[0:SH, :], low[0:SH, :], ACT.Exp))
            nc.scalar.activation(low[0:SH, :], low[0:SH, :], ACT.Ln, bias=1.0).then_inc(dtln_done, 1)
            ssd_evacuate(act, 0, 0)
            ssd_evacuate(act, 0, 1)
            job_evac(n_bias)
            job_evac(n_bias + 1)
            ssd_evacuate(act, 0, 2)
            ssd_evacuate(act, 0, 3)
            act.wait_ge(last_done, 1)
            nc.scalar.activation(decay, psum[:, 5, 0:NCH * SH].rearrange("p (c h) -> p c h", c=NCH), ACT.Exp).then_inc(dec_done, 1)
            act.wait_ge(te_done, 1)
            nc.scalar.activation(toend, toend, ACT.Exp).then_inc(dec_done, 1)
            ssd_evacuate(act, 0, 4)
            job_evac(n_bias + 2)
            job_evac(n_bias + 3)
            ssd_evacuate(act, 0, 5)
            act.wait_ge(dec_done, 2)

        @block.vector
        def _(dve):
            nc.vector.memset(rel[32:33, :], NEG).then_inc(rel_mask, 1)
            for k in range(1, KT):
                dve.wait_ge(sq_done, k + 1)
                if k > 1:
                    dve.wait_ge(summed, k - 1)
                nc.vector.tensor_tensor(sumsq0, xn[:, 0, :] if k == 1 else sumsq0, xn[:, k, :], ALU.add).then_inc(summed, 1)
            dve.wait_ge(ssq_done, 1)
            nc.vector.tensor_scalar(std.rearrange("p (h t) -> p h t", h=2), halves(psum, 6), 1.0 / D, EPS,
                                    ALU.mult, ALU.add).then_inc(var_done, 1)
            dve.wait_ge(std_done, 1)
            s = Steps(dve, dve_setup)
            s.turn(0)
            s.link(nc.vector.reciprocal(rstd, std))
            for k in range(KT):
                nc.vector.scalar_tensor_tensor(xn[:, k, :], xT[:, k, :], pT[:, PR_N1 + k:PR_N1 + k + 1], rstd,
                                               ALU.mult, ALU.mult).then_inc(xn_done, 1)
            dve.wait_ge(dtraw_done, 1)
            s.link(nc.vector.tensor_scalar(raw_dt[0:SH, :].rearrange("p (h t) -> p h t", h=2), halves(psum, 4, SH),
                                           hcol[0:SH, 0:1], None, ALU.add))
            nc.vector.scalar_tensor_tensor(low[0:SH, :], raw_dt[0:SH, :], -1.0, raw_dt[0:SH, :],
                                           ALU.mult, ALU.min).then_inc(dtlow_done, 1)
            dve.wait_ge(dtln_done, 1)
            nc.vector.scalar_tensor_tensor(rows[0:SH, 0, :], raw_dt[0:SH, :], 0.0, low[0:SH, :],
                                           ALU.max, ALU.add).then_inc(rows_done, 1)
            dve.wait_ge(rows_done, 1)
            s.link(nc.vector.tensor_scalar(dta[0:SH, :], rows[0:SH, 0, :], hcol[0:SH, 2:3], -1.0, ALU.mult, ALU.mult))
            for c in range(NCH):
                nc.vector.tensor_tensor_scan(rows[0:SH, 1, c * CH:(c + 1) * CH], ones[0:SH, :],
                                             dta[0:SH, c * CH:(c + 1) * CH], 0.0, ALU.mult, ALU.add).then_inc(rows_done, 1)
            nc.vector.tensor_copy(rows[0:SH, 1, SEQ:T], dta[0:SH, SEQ:T]).then_inc(rows_done, 1)
            dve.wait_ge(acs_done, 1)
            nc.vector.tensor_copy(acs_tok, psum[:, 4, 0:NCH * SH].rearrange("p (c h) -> p c h", c=NCH)).then_inc(acst_done, 1)
            dve.wait_ge(acst_done, 1)
            dve.wait_ge(dec_done, 1)
            nc.vector.tensor_tensor(toend, psum[:, 5, 0:NCH * SH].rearrange("p (c h) -> p c h", c=NCH), acs_tok,
                                    ALU.subtract).then_inc(te_done, 1)


    arena.at = base_turn
    o1_rooms = [arena.block[:, base_y + j * 4096:base_y + (j + 1) * 4096].rearrange("p (k n) -> p k n", k=16)
                for j in range(2)]
    o1_begun = 2 * (SG - 1)
    o1_ld = [sem("o1_ld0"), sem("o1_ld1")]
    zs = take(2 * T).rearrange("p (c t) -> p c t", c=2)
    acts = [take(4 * T).rearrange("p (c t) -> p c t", c=4) for _ in range(2)]
    xdtT = take(2 * T).rearrange("p (c t) -> p c t", c=2)
    xdt = take(NCH * 256).rearrange("p (c n) -> p c n", c=NCH)
    xdte = take(NCH * 256).rearrange("p (c n) -> p c n", c=NCH)
    btok = take(NCH * P).rearrange("p (c n) -> p c n", c=NCH)
    cbm = take(NCH * P).rearrange("p (c n) -> p c n", c=NCH)
    grow = take(2 * T).rearrange("p (r t) -> p r t", r=2)
    eexp = take(2 * T).rearrange("p (c t) -> p c t", c=2)
    hT = take(NCH * 256).rearrange("p (c n) -> p c n", c=NCH)
    seg = [take(SEQ).rearrange("p (c n) -> p c n", c=NCH) for _ in range(2)]
    y = take(2 * T).rearrange("p (c t) -> p c t", c=2)
    ytmp = take(2 * T).rearrange("p (c t) -> p c t", c=2)
    gstd = take(T)
    bcs = take(256)
    sst = take(NB * 256).rearrange("p (b q n) -> p b q n", b=NB, q=2)
    stmp = take(1024)
    ysmp = take(NB * 2).rearrange("p (b q) -> p b q", b=NB)
    hfin = take(256).rearrange("p (q n) -> p q n", q=2)

    ld_row, ld_sst = sem("ld_row"), sem("ld_sst")
    st_hfin, st_sst = sem("st_hfin"), sem("st_sst")
    raw_zero = sem("raw_zero")
    init_x, conv_x_done, x_ready = sig("init_x"), sig("conv_x_done"), sig("x_ready")
    init_bc, conv_bc_done, bc_ready = sig("init_bc"), sig("conv_bc_done"), sig("bc_ready")
    z_ready = sig("z_ready")
    dtb_full, xdt_done, e_full, e_ready = sig("dtb_full"), sig("xdt_done"), sig("e_full"), sig("e_ready")
    tok_full, tok_out, tokx_done, cbm_done = sig("tok_full"), sig("tok_out"), sig("tokx_done"), sig("cbm_done")
    bc_out = sig("bc_out")
    state_full, h_done = sig("state_full"), sig("h_done")
    yoff_full, yoff_used = sig("yoff_full"), sig("yoff_used")
    sum_full, seg_done, dec_ready, mt_done, mt_used = (
        sig("sum_full", 4), sig("seg_done", 4), sig("dec_ready", 4), sig("mt_done", 4), sig("mt_used", 4))
    sbc_full, sbc_out, row_full, row_used = sig("sbc_full"), sig("sbc_out"), sig("row_full", 2), sig("row_used", 2)
    sdec_done, sst_done = sig("sdec_done"), sig("sst_done")
    hfin_full, hfin_out = sig("hfin_full"), sig("hfin_out")
    gated, sqg_done, ssg_full, varg_done, stdg_done, yt_done = (
        sig("gated"), sig("sqg_done"), sig("ssg_full"), sig("varg_done"), sig("stdg_done"), sig("yt_done"))
    dve_own, dve_x, dve_bc, dve_norm = sig("dve_ssd", 14), sig("dve_x", 2), sig("dve_bc", 2), sig("dve_norm")
    CB_ = PR_CB

    ssm_in = io["state_ssm"][0].rearrange("b (g q h) p n -> g (h p) b q n", g=SG, q=2)
    ssm_out = io["ssm_sample"][0].rearrange("b (g q h) p n -> g (h p) b q n", g=SG, q=2)
    ssm_prompt = io["ssm_prompt"][0, 0].rearrange("(g q h) p n -> g (h p) q n", g=SG, q=2)

    carrier = sem("carrier")

    with nc.Block() as block:
        @block.sync
        def _(sp):
            with sp.Fori(0, SG - 1) as i:
                sp.wait_ge(tile_full.sem, tile_full.at(i, 2))
                weights_x(sp, i + 1)
                sp.wait_ge(tile_full.sem, tile_full.at(i, 4))
                weights_bc(sp, i + 1)
                sp.wait_ge(tile_full.sem, tile_full.at(i, 6))
                sp.sem_inc(carrier, 1)
                weights_z(sp, i + 1)
                keep_window(sp, i)
            sp.wait_ge(tile_full.sem, SG * 6 - 2)
            sp.dma_start(o1_rooms[0], io["ssd_w_out"][0].rearrange("(k p) n -> p k n", p=P)[:, :, 0:256]).then_inc(o1_ld[0], 16)
            sp.wait_ge(tile_full.sem, SG * 6)
            sp.wait_ge(conv_x_done.sem, SG)
            sp.wait_ge(conv_bc_done.sem, SG)
            sp.dma_start(o1_rooms[1], io["ssd_w_out"][0].rearrange("(k p) n -> p k n", p=P)[:, :, 256:512]).then_inc(o1_ld[1], 16)
            keep_window(sp, NB - 1)

        @block.gpsimd
        def _(pool):
            nc.gpsimd.memset(raw[:, :, 0:3], 0.0).then_inc(raw_zero, 1)

            def load_rows(i):
                pool.dma_start(grow[0:4], scr_rows[bass.ds(i * 4, 4)]).then_inc(ld_row, 16)

            def load_states(i):
                for q in range(2):
                    pool.dma_start(sst[:, :, q], ssm_in[bass.ds(i, 1), :, :, q].rearrange("o p b n -> (o p) b n"))\
                        .then_inc(ld_sst, 16)

            def turn(i, more=True):
                pool.wait_ge(e_ready.sem, e_ready.at(i, 1))
                pool.wait_ge(ld_sst, i * 32 + 32)
                nc.gpsimd.tensor_tensor(sst, sst, eexp[:, :, SEQ:T].rearrange("p q b -> p b q").unsqueeze(3)
                                        .to_broadcast([P, NB, 2, SN]), ALU.mult).then_inc(sdec_done.sem, 1)
                if more:
                    pool.wait_ge(sum_full.sem, sum_full.at(i, 4))
                    pool.sem_inc(carrier, 1)
                    load_rows(i + 1)
                pool.wait_ge(hfin_out.sem, hfin_out.at(i, 1))
                pool.sem_inc(carrier, 1)
                pool.dma_start(ssm_prompt[bass.ds(i, 1)].rearrange("o p q n -> (o p) q n"), hfin).then_inc(st_hfin, 16)
                pool.wait_ge(sst_done.sem, sst_done.at(i, 1))
                pool.wait_ge(row_used.sem, row_used.at(i, 2))
                pool.sem_inc(carrier, 1)
                for q in range(2):
                    pool.dma_start(ssm_out[bass.ds(i, 1), :, :, q].rearrange("o p b n -> (o p) b n"), sst[:, :, q])\
                        .then_inc(st_sst, 16)
                if more:
                    pool.wait_ge(st_sst, i * 32 + 32)
                    pool.sem_inc(carrier, 1)
                    load_states(i + 1)

            load_rows(0)
            load_states(0)
            turn(0)
            with pool.Fori(1, SG - 1) as i:
                turn(i)
            turn(SG - 1, more=False)
            pool.wait_ge(st_hfin, 16 * SG)
            pool.wait_ge(st_sst, 32 * SG)

        @block.tensor
        def _(pe):
            def rows_to_pairs(i, r, done):
                for q in range(2):
                    for h in range(2):
                        mm = nc.tensor.matmul(psum[:, 4 + 2 * q + h, 0:HALF], const("pair", 4)[:, q * P:(q + 1) * P],
                                              grow[0:4, r, h * HALF:(h + 1) * HALF], start=True, stop=True)
                mm.then_inc(done.sem, 1)

            def turn(i, j, more=True, first=False):
                act_ = acts[j]

                def nxt(n, part):
                    if more:
                        ssd_project(pe, i + 1, n, part=part)
                    else:
                        project_out_terms(2 * n + part)

                pe.wait_ge(ld_row, i * 16 + 16)
                if not first:
                    pe.wait_ge(varg_done.sem, varg_done.at(i, 0))
                    pe.wait_ge(hfin_out.sem, hfin_out.at(i, 0))
                rows_to_pairs(i, 0, dtb_full)
                nxt(0, 0)
                pe.wait_ge(xdt_done.sem, xdt_done.at(i, 1))
                rows_to_pairs(i, 1, e_full)
                nxt(0, 1)
                nxt(1, 0)
                pe.wait_ge(bc_ready.sem, bc_ready.at(i, 1))
                pe.wait_ge(e_ready.sem, e_ready.at(i, 1))
                for c in range(NCH):
                    for q in range(2):
                        tr(psum[:, 4 + c // 2, (c % 2) * 256 + q * P:(c % 2) * 256 + (q + 1) * P],
                           xdtT[:, q, c * CH:(c + 1) * CH], P)
                for c in range(NCH):
                    tr(psum[:, 6, c * CH:(c + 1) * CH], act_[:, 2, c * CH:(c + 1) * CH], P)
                for c in range(NCH):
                    mm = nc.tensor.matmul(psum[:, 7, c * CH:(c + 1) * CH], act_[:, 2, c * CH:(c + 1) * CH],
                                          act_[:, 3, c * CH:(c + 1) * CH], start=True, stop=True)
                mm.then_inc(tok_full.sem, 1)
                nxt(1, 1)
                nxt(2, 0)
                pe.wait_ge(tok_out.sem, tok_out.at(i, 1))
                pe.wait_ge(bc_out.sem, bc_out.at(i, 1))
                pe.wait_ge(tokx_done.sem, tokx_done.at(i, 1))
                for c in range(NCH):
                    mm = nc.tensor.matmul(psum[:, 4 + c // 2, (c % 2) * 256:(c % 2) * 256 + 256], btok[:, c, :],
                                          xdte[:, c, :], start=True, stop=True)
                mm.then_inc(state_full.sem, 1)
                tr(psum[0:NB, 6, 0:P], act_[:, 2, SEQ:T], P)
                tr(psum[0:NB, 6, P:256], act_[:, 3, SEQ:T], P).then_inc(sbc_full.sem, 1)
                nxt(2, 1)
                pe.wait_ge(sbc_out.sem, sbc_out.at(i, 1))
                pe.wait_ge(h_done.sem, h_done.at(i, 1))
                pe.wait_ge(cbm_done.sem, cbm_done.at(i, 1))
                for q in range(2):
                    for c in range(1, NCH):
                        mm = nc.tensor.matmul(psum[:, 6 + q, c * CH:(c + 1) * CH], hT[:, c - 1, q * P:(q + 1) * P],
                                              act_[:, 3, c * CH:(c + 1) * CH], start=True, stop=True)
                mm.then_inc(yoff_full.sem, 1)
                for r in range(2):
                    if r:
                        pe.wait_ge(row_used.sem, row_used.at(i, 1))
                    for b in range(4):
                        mm = nc.tensor.matmul(psum[:, 4 + b // 2, (b % 2) * 256:(b % 2) * 256 + 256],
                                              const("samp", NB)[:, (4 * r + b) * P:(4 * r + b + 1) * P], bcs[0:NB, :],
                                              start=True, stop=True)
                    mm.then_inc(row_full.sem, 1)
                    nxt(3, r)

                def sums(h):
                    if h >= 2:
                        pe.wait_ge(seg_done.sem, seg_done.at(i, h - 1))
                    nc.tensor.matmul(psum[:, 4 + h % 2, :], const("head", 4)[:, h * P:(h + 1) * P], grow[0:4, 1, 0:SEQ],
                                     start=True, stop=True).then_inc(sum_full.sem, 1)

                def within(h):
                    pe.wait_ge(mt_done.sem, mt_done.at(i, h + 1))
                    if h == 0:
                        pe.wait_ge(yoff_used.sem, yoff_used.at(i, 1))
                    a = h % 2 * 64
                    for c in range(NCH):
                        mm = nc.tensor.matmul(psum[a:a + 64, 6 + h // 2, c * CH:(c + 1) * CH],
                                              xdt[:, c, h * 64:(h + 1) * 64], seg[h % 2][:, c, :], start=True, stop=True)
                    mm.then_inc(mt_used.sem, 1)

                pe.wait_ge(row_used.sem, row_used.at(i, 2))
                sums(0)
                sums(1)
                nxt(4, 0)
                within(0)
                sums(2)
                nxt(4, 1)
                within(1)
                sums(3)
                nxt(5, 0)
                within(2)
                within(3)
                pe.wait_ge(seg_done.sem, seg_done.at(i, 4))
                tr(psum[:, 5, 0:P], hT[:, NCH - 1, 0:P], P)
                tr(psum[:, 5, P:256], hT[:, NCH - 1, P:256], P).then_inc(hfin_full.sem, 1)
                nxt(5, 1)
                pe.wait_ge(sqg_done.sem, sqg_done.at(i, 1))
                for h in range(2):
                    for q in range(2):
                        mm = nc.tensor.matmul(psum[:, 6 + h, 0:HALF], ones, ytmp[:, q, h * HALF:(h + 1) * HALF],
                                              start=(q == 0), stop=(q == 1))
                mm.then_inc(ssg_full.sem, 1)

            def project_out_terms(piece):
                if piece == 0:
                    pe.wait_ge(tile_out.sem, SG * 6)
                    pe.wait_ge(o1_ld[0], 16)
                terms = [(k, n) for k in range(o1_begun) for n in range(2)]
                for k, n in terms[len(terms) * piece // 12:len(terms) * (piece + 1) // 12]:
                    if n == 0 and k % 2 == 0:
                        pe.wait_ge(yt_done.sem, k // 2 + 1)
                    for h in range(2):
                        nc.tensor.matmul(psum[:, n * 2 + h, 0:HALF], o1_rooms[0][:, k, n * P:(n + 1) * P],
                                         yT[:, k, h * HALF:(h + 1) * HALF], start=(k == 0), stop=False)

            turn(0, 0, first=True)
            with pe.Fori(0, SG // 2 - 1) as i:
                turn(i * 2 + 1, 1)
                turn(i * 2 + 2, 0)
            turn(SG - 1, 1, more=False)

        @block.scalar
        def _(act):
            def last_tap(g, j, tiles, done):
                act.wait_ge(tile_out.sem, tile_out.at(g, tiles[-1] + 1))
                for c in tiles:
                    ct = (g * 2, g * 2 + 1, g + 16, g + 24)[c]
                    ins = nc.scalar.activation(acts[j][:, c, :], raw[:, c, 3:3 + T], ACT.Identity,
                                               bias=pT[:, bass.ds(ct + CB_, 1)], scale=cw[:, bass.ds(ct + 96, 1)])
                ins.then_inc(done.sem, 1)

            def turn(i, j, more=True, first=False):
                def nxt(n):
                    if more:
                        ssd_evacuate(act, i + 1, n)

                act_ = acts[j]
                act.wait_ge(conv_x_done.sem, conv_x_done.at(i, 1))
                nc.scalar.activation(act_[:, 0:2], act_[:, 0:2], ACT.Silu).then_inc(x_ready.sem, 1)
                act.wait_ge(tile_out.sem, tile_out.at(i, 6))
                nc.scalar.activation(zs, zraw, ACT.Silu).then_inc(z_ready.sem, 1)
                act.wait_ge(conv_bc_done.sem, conv_bc_done.at(i, 1))
                nc.scalar.activation(act_[:, 2:4], act_[:, 2:4], ACT.Silu).then_inc(bc_ready.sem, 1)
                if not first:
                    nc.scalar.activation(gstd, gstd, ACT.Sqrt).then_inc(stdg_done.sem, 1)
                act.wait_ge(e_full.sem, e_full.at(i, 1))
                nc.scalar.activation(eexp.rearrange("p q (h t) -> p (q h) t", h=2), psum[:, 4:8, 0:HALF],
                                     ACT.Exp).then_inc(e_ready.sem, 1)
                nxt(0)
                act.wait_ge(tok_full.sem, tok_full.at(i, 1))
                nc.scalar.activation(btok, psum[:, 6, :].rearrange("p (c n) -> p c n", c=NCH), ACT.Copy).then_inc(bc_out.sem, 1)
                act.wait_ge(tokx_done.sem, tokx_done.at(i, 1))
                nc.scalar.activation(xdt, psum[:, 4:6, :].rearrange("p b (c n) -> p (b c) n", c=2),
                                     ACT.Copy).then_inc(tok_out.sem, 1)
                nxt(1)
                act.wait_ge(sbc_full.sem, sbc_full.at(i, 1))
                nc.scalar.activation(bcs[0:NB, :], psum[0:NB, 6, 0:256], ACT.Copy).then_inc(sbc_out.sem, 1)
                if more:
                    last_tap(i + 1, 1 - j, (0, 1), init_x)
                nxt(2)
                for h in range(4):
                    act.wait_ge(seg_done.sem, seg_done.at(i, h + 1))
                    nc.scalar.activation(seg[h % 2], seg[h % 2], ACT.Exp).then_inc(dec_ready.sem, 1)
                    if h == 1:
                        nxt(3)
                        if more:
                            last_tap(i + 1, 1 - j, (2, 3), init_bc)
                act.wait_ge(hfin_full.sem, hfin_full.at(i, 1))
                if not first:
                    act.wait_ge(st_hfin, i * 16)
                nc.scalar.activation(hfin, psum[:, 5, 0:256].rearrange("p (q n) -> p q n", q=2),
                                     ACT.Copy).then_inc(hfin_out.sem, 1)
                act.wait_ge(z_ready.sem, z_ready.at(i, 1))
                nxt(4)
                nxt(5)
                act.wait_ge(gated.sem, gated.at(i, 1))
                nc.scalar.activation(ytmp, y, ACT.Square).then_inc(sqg_done.sem, 1)
                act.wait_ge(varg_done.sem, varg_done.at(i, 1))

            act.wait_ge(raw_zero, 1)
            last_tap(0, 0, (0, 1), init_x)
            last_tap(0, 0, (2, 3), init_bc)
            turn(0, 0, first=True)
            with act.Fori(0, SG // 2 - 1) as i:
                turn(i * 2 + 1, 1)
                turn(i * 2 + 2, 0)
            turn(SG - 1, 1, more=False)
            nc.scalar.activation(gstd, gstd, ACT.Sqrt).then_inc(stdg_done.sem, 1)

        @block.vector
        def _(dve):
            class Taps:

                def __init__(self, g, j, tiles, own, init, done):
                    self.g, self.act_, self.tiles, self.init, self.done = g, acts[j], tiles, init, done
                    self.s = Steps(dve, own)
                    self.s.turn(g)

                def tap(self, k):
                    g, act_ = self.g, self.act_
                    if k == 0:
                        dve.wait_ge(self.init.sem, self.init.at(g, 1))
                    else:
                        dve.wait_ge(self.s.own.sem, self.s.own.at(g, k))
                    for c in self.tiles:
                        ct = (g * 2, g * 2 + 1, g + 16, g + 24)[c]
                        w = cw[:, bass.ds(ct + 32 * k, 1)]
                        nc.vector.scalar_tensor_tensor(act_[:, c, 0:SEQ], raw[:, c, k:k + SEQ], w,
                                                       act_[:, c, 0:SEQ], ALU.mult, ALU.add)
                        ins = nc.vector.scalar_tensor_tensor(act_[:, c, SEQ:T], st[:, bass.ds(ct, 1), :, k], w,
                                                             act_[:, c, SEQ:T], ALU.mult, ALU.add)
                    if k < 2:
                        self.s.post(ins)
                        return
                    for c in self.tiles:
                        ct = (g * 2, g * 2 + 1, g + 16, g + 24)[c]
                        ins = nc.vector.tensor_copy(tail[:, bass.ds(ct, 1), :], raw[:, c:c + 1, SEQ:SEQ + 11])
                    self.s.post(ins, self.done)
                    self.s.turn(g)

            def taps_bc(g, j):
                bc = Taps(g, j, (2, 3), dve_bc, init_bc, conv_bc_done)
                for k in range(3):
                    bc.tap(k)

            def normalise(g):
                s = Steps(dve, dve_norm)
                s.turn(g)
                dve.wait_ge(stdg_done.sem, stdg_done.at(g, 1))
                s.link(nc.vector.reciprocal(gstd, gstd))
                for q in range(2):
                    ins = nc.vector.scalar_tensor_tensor(yT[:, bass.ds(g * 2 + q, 1), :].rearrange("p o t -> p (o t)"),
                                                         y[:, q, :], pT[:, bass.ds(g * 2 + (PR_GN + q), 1)], gstd,
                                                         ALU.mult, ALU.mult)
                s.post(ins, yt_done)
                s.turn(g)

            def turn(i, j, more=True, first=False):
                act_ = acts[j]
                s = Steps(dve, dve_own)
                s.turn(i)
                dve.wait_ge(dtb_full.sem, dtb_full.at(i, 1))
                dve.wait_ge(x_ready.sem, x_ready.at(i, 1))
                for q in range(2):
                    ins = nc.vector.tensor_tensor(xdtT[:, q, :].rearrange("p (h t) -> p h t", h=2),
                                                  act_[:, q, :].rearrange("p (h t) -> p h t", h=2),
                                                  halves(psum, 4 + 2 * q), ALU.mult)
                s.post(ins, xdt_done)
                if not first:
                    normalise(i - 1)
                dve.wait_ge(tok_full.sem, tok_full.at(i, 1))
                for c in range(NCH):
                    ins = nc.vector.tensor_tensor(xdte[:, c, :].rearrange("p (h n) -> p h n", h=4),
                                                  psum[:, 4 + c // 2, (c % 2) * 256:(c % 2) * 256 + 256]
                                                  .rearrange("p (h n) -> p h n", h=4),
                                                  toend[:, c, bass.ds(i * 4, 4)].unsqueeze(2).to_broadcast([P, 4, 64]),
                                                  ALU.mult)
                s.post(ins, tokx_done)
                s.post(nc.vector.tensor_tensor(cbm, psum[:, 7, :].rearrange("p (c n) -> p c n", c=NCH),
                                               const("causal").unsqueeze(1).to_broadcast([P, NCH, P]), ALU.mult),
                       cbm_done)
                taps = Taps(i + 1, 1 - j, (0, 1), dve_x, init_x, conv_x_done)

                def tap(k):
                    if more:
                        taps.tap(k)

                dve.wait_ge(state_full.sem, state_full.at(i, 1))

                def new_state(c):
                    return psum[:, 4 + c // 2, (c % 2) * 256:(c % 2) * 256 + 256]

                s.link(nc.vector.tensor_copy(hT[:, 0, :], new_state(0)))
                for c in range(1, NCH):
                    s.link(nc.vector.tensor_tensor(hT[:, c, :].rearrange("p (h n) -> p h n", h=4),
                                                   hT[:, c - 1, :].rearrange("p (h n) -> p h n", h=4),
                                                   decay[:, c, bass.ds(i * 4, 4)].unsqueeze(2).to_broadcast([P, 4, 64]),
                                                   ALU.mult))
                    s.link(nc.vector.tensor_tensor(hT[:, c, :], hT[:, c, :], new_state(c), ALU.add),
                           h_done if c == NCH - 1 else None)
                dve.wait_ge(yoff_full.sem, yoff_full.at(i, 1))
                dve.wait_ge(e_ready.sem, e_ready.at(i, 1))
                ins = nc.vector.tensor_tensor(ytmp[:, :, CH:SEQ], psum[:, 6:8, CH:SEQ], eexp[:, :, CH:SEQ], ALU.mult)
                s.post(ins, yoff_used)
                for r in range(2):
                    b0 = 4 * r
                    dve.wait_ge(row_full.sem, row_full.at(i, r + 1))
                    rows4 = psum[:, 4:6, :].rearrange("p k (b s n) -> p (k b) s n", b=2, s=2)
                    tmp = stmp.rearrange("p (b q n) -> p b q n", b=4, q=2)
                    for q in range(2):
                        ins = nc.vector.tensor_tensor(tmp[:, :, q, :], rows4[:, :, 0, :],
                                                      xdtT[:, q, SEQ + b0:SEQ + b0 + 4].unsqueeze(2)
                                                      .to_broadcast([P, 4, SN]), ALU.mult)
                    s.link(ins)
                    if r == 0:
                        dve.wait_ge(sdec_done.sem, sdec_done.at(i, 1))
                    s.link(nc.vector.tensor_tensor(sst[:, b0:b0 + 4], sst[:, b0:b0 + 4], tmp, ALU.add),
                           sst_done if r else None)
                    for q in range(2):
                        ins = nc.vector.tensor_tensor(tmp[:, :, q, :], sst[:, b0:b0 + 4, q, :], rows4[:, :, 1, :],
                                                      ALU.mult)
                    s.link(ins, row_used)
                    s.link(nc.vector.tensor_reduce(ysmp[:, b0:b0 + 4, :], tmp, AX.X, ALU.add))
                    tap(r)
                def differences(h):
                    dve.wait_ge(sum_full.sem, sum_full.at(i, h + 1))
                    if h >= 2:
                        dve.wait_ge(mt_used.sem, mt_used.at(i, h - 1))
                    for c in range(NCH):
                        ins = nc.vector.tensor_scalar(seg[h % 2][:, c, :], psum[:, 4 + h % 2, c * CH:(c + 1) * CH],
                                                      acs_tok[:, c, bass.ds(i * 4 + h, 1)], 0.0, ALU.subtract, ALU.min)
                    s.post(ins, seg_done)

                def product(h):
                    dve.wait_ge(dec_ready.sem, dec_ready.at(i, h + 1))
                    s.post(nc.vector.tensor_tensor(seg[h % 2], seg[h % 2], cbm, ALU.mult), mt_done)

                dve.wait_ge(cbm_done.sem, cbm_done.at(i, 1))
                differences(0)
                differences(1)
                product(0)
                product(1)
                tap(2)
                differences(2)
                differences(3)
                product(2)
                product(3)
                dve.wait_ge(mt_used.sem, mt_used.at(i, 4))
                for q in range(2):
                    ins = nc.vector.scalar_tensor_tensor(y[:, q, 0:SEQ], act_[:, q, 0:SEQ], dsk[:, bass.ds(i * 2 + q, 1)],
                                                         psum[:, 6 + q, :], ALU.mult, ALU.add)
                s.link(ins)
                s.post(nc.vector.tensor_tensor(y[:, :, CH:SEQ], y[:, :, CH:SEQ], ytmp[:, :, CH:SEQ], ALU.add))
                for q in range(2):
                    ins = nc.vector.scalar_tensor_tensor(y[:, q, SEQ:T], act_[:, q, SEQ:T], dsk[:, bass.ds(i * 2 + q, 1)],
                                                         ysmp[:, :, q], ALU.mult, ALU.add)
                s.link(ins)
                dve.wait_ge(z_ready.sem, z_ready.at(i, 1))
                s.link(nc.vector.tensor_tensor(y, y, zs, ALU.mult), gated)
                dve.wait_ge(ssg_full.sem, ssg_full.at(i, 1))
                s.post(nc.vector.tensor_scalar(gstd.rearrange("p (h t) -> p h t", h=2), halves(psum, 6), 1.0 / 256, EPS,
                                               ALU.mult, ALU.add), varg_done)
                s.turn(i)
                if more:
                    taps_bc(i + 1, 1 - j)

            dve.wait_ge(raw_zero, 1)
            x0 = Taps(0, 0, (0, 1), dve_x, init_x, conv_x_done)
            for k in range(3):
                x0.tap(k)
            taps_bc(0, 0)
            turn(0, 0, first=True)
            with dve.Fori(0, SG // 2 - 1) as i:
                turn(i * 2 + 1, 1)
                turn(i * 2 + 2, 0)
            turn(SG - 1, 1, more=False)
            normalise(SG - 1)
            dve.wait_ge(yt_done.sem, SG)


    def project_out(name, kin, src, w_dram, rooms, ld, loaded, norm_row, extra, begun=0):
        w_view = w_dram.rearrange("(k p) n -> p k n", p=P)
        full, added = sem(f"{name}_full"), sem(f"{name}_added")
        sq, summed, ssq, var, sd, rs, xnd = (sem(f"{name}_{x}") for x in ("sq", "summed", "ssq", "var", "sd", "rs", "xn"))
        with nc.Block() as block:
            @block.sync
            def _(sp):
                for n in range(2 * loaded, KT, 2):
                    if n >= 4:
                        sp.wait_ge(full, n - 2)
                    sp.dma_start(rooms[n // 2 % 2], w_view[:, :, n * P:(n + 2) * P]).then_inc(ld[n // 2 % 2], 16)
                if "sync" in extra:
                    extra["sync"](sp)

            @block.tensor
            def _(pe):
                for n in range(KT):
                    if n % 2 == 0:
                        pe.wait_ge(ld[n // 2 % 2], n // 4 * 16 + 16)
                    if n >= 2:
                        pe.wait_ge(added, n - 1)
                    for k in range(begun if n < 2 else 0, kin):
                        for h in range(2):
                            mm = nc.tensor.matmul(psum[:, n % 2 * 2 + h, 0:HALF],
                                                  rooms[n // 2 % 2][:, k, n % 2 * P:(n % 2 + 1) * P],
                                                  src[:, k, h * HALF:(h + 1) * HALF],
                                                  start=(k == 0), stop=(k == kin - 1))
                    mm.then_inc(full, 1)
                    if n == 3 and "tensor" in extra:
                        extra["tensor"](pe)
                pe.wait_ge(summed, KT - 1)
                for h in range(2):
                    mm = nc.tensor.matmul(psum[:, 2 + h, 0:HALF], ones, sumsq[:, h * HALF:(h + 1) * HALF],
                                          start=True, stop=True)
                mm.then_inc(ssq, 1)
                if "tensor_last" in extra:
                    extra["tensor_last"](pe, xnd)

            @block.scalar
            def _(act):
                for k in range(KT):
                    act.wait_ge(added, k + 1)
                    nc.scalar.activation(xn[:, k, :], xT[:, k, :], ACT.Square).then_inc(sq, 1)
                    if k == 3 and "scalar" in extra:
                        extra["scalar"](act)
                act.wait_ge(var, 1)
                nc.scalar.activation(std2, std2, ACT.Sqrt).then_inc(sd, 1)
                if "scalar_last" in extra:
                    extra["scalar_last"](act)

            @block.vector
            def _(dve):
                def accumulate(k):
                    dve.wait_ge(sq, k + 1)
                    if k > 1:
                        dve.wait_ge(summed, k - 1)
                    nc.vector.tensor_tensor(sumsq, xn[:, 0, :] if k == 1 else sumsq, xn[:, k, :], ALU.add).then_inc(summed, 1)

                for n in range(KT):
                    dve.wait_ge(full, n + 1)
                    x = xT[:, n, :].rearrange("p (h t) -> p h t", h=2)
                    nc.vector.tensor_tensor(x, halves(psum, n % 2 * 2), x, ALU.add).then_inc(added, 1)
                    if n >= 2:
                        accumulate(n - 1)
                accumulate(KT - 1)
                dve.wait_ge(ssq, 1)
                nc.vector.tensor_scalar(std2.rearrange("p (h t) -> p h t", h=2), halves(psum, 2), 1.0 / D, EPS,
                                        ALU.mult, ALU.add).then_inc(var, 1)
                dve.wait_ge(sd, 1)
                nc.vector.reciprocal(rstd2, std2).then_inc(rs, 1)
                dve.wait_ge(rs, 1)
                for k in range(KT):
                    nc.vector.scalar_tensor_tensor(xn[:, k, :], xT[:, k, :], pT[:, norm_row + k:norm_row + k + 1],
                                                   rstd2, ALU.mult, ALU.mult).then_inc(xnd, 1)
                dve.wait_ge(xnd, KT)
                if "vector_last" in extra:
                    extra["vector_last"](dve)

    arena.at = base_y
    w_rooms = [take(16 * 256).rearrange("p (k n) -> p k n", k=16) for _ in range(2)]
    std2, rstd2, sumsq = take(T), take(T), take(T)
    conv_rows = take(CONV)
    gT = take(T)
    peT = take(32)
    tr_full, tr_out, st_conv = sem("tr_full"), sem("tr_out"), sem("st_conv")

    w1 = arena.take_top(2 * 16 * P).rearrange("p (t j n) -> p t j n", t=2, j=16)
    w2k = arena.take_top(P)
    w2v = arena.take_top(DH)
    pebias = arena.take_top(2)
    ptab = arena.take_top(64).bitcast(I32)
    top_nsa = arena.size
    slot_a = arena.take_top(KT * 256).rearrange("p (k n) -> p k n", k=KT)
    slot_b = arena.take_top(KT * 256).rearrange("p (k n) -> p k n", k=KT)
    slot_c = arena.take_top(KT * P).rearrange("p (k n) -> p k n", k=KT)
    slot_d = arena.take_top(KT * 256).rearrange("p (k n) -> p k n", k=KT)
    wg = arena.take_top(KT * 3 * NH).rearrange("p (k n) -> p k n", k=KT)
    per = arena.take_top(P)
    ld_a, ld_b, ld_c, ld_d = (nc.alloc_semaphore(name=n) for n in ("ld_a", "ld_b", "ld_c", "ld_d"))
    ld_w1, ld_pre = sem("ld_w1"), sem("ld_pre")
    pre_pet, pre_pec, pre_full, pre_out, pre_gt, pre_gto, pre_gs = (sem(n) for n in (
        "pre_pet", "pre_pec", "pre_full", "pre_out", "pre_gt", "pre_gto", "pre_gs"))
    n_in = io["nsa_w_in"][0].rearrange("(k p) n -> p k n", p=P)

    pages_c = [arena.block[:, top_nsa - 4096:top_nsa].rearrange("p (t a c) -> p t a c", t=4, a=2)]
    ld_tab = nc.alloc_semaphore(name="ld_tab")
    ld_cmp = [nc.alloc_semaphore(name=f"ld_cmp{j}") for j in range(2)]
    wins = [arena.block[:, top_nsa - 7168:top_nsa - 5120].rearrange("p (t a c) -> p t a c", t=2, a=2)]
    ld_pg = [nc.alloc_semaphore(name=f"ld_pg{j}") for j in range(2)]

    def load_window(sp, b, j):
        sp.dma_start(wins[j].rearrange("p t a c -> p t (a c)"),
                     io["cache_win"][0, bass.ds(b, 1)].rearrange("o (t p a) k g d -> p (o t) (a k g d)", t=2, a=2))\
            .then_inc(ld_pg[j], 16)

    def load_pages(sp, b, half, room, landed):
        for n in range(8):
            page = sp.value_load(ptab[0:1, bass.ds(b * 8 + n, 1)], min_val=0, max_val=io["cache_kv"].shape[0] - 1)
            sp.dma_start(room[n % 2 * 64:n % 2 * 64 + 64, n // 2],
                         io["cache_kv"][bass.ds(page, 1), 0, :, 2 * half:2 * half + 2]
                         .rearrange("o (p a) t g d -> (o p) a (t g d)", a=2)).then_inc(landed, 16)

    hid_s = arena.block[:, top_nsa - 4096 - 1024:top_nsa - 4096 - 1024 + 2 * G * NCS].rearrange("p (t n) -> p t n", t=2)
    kct_s = arena.block[:, xn_at:xn_at + 2 * G * NPAIR].rearrange("p (t g n) -> p t g n", t=2, g=G)
    order = [ca[:, CA["causal"][0] + j * 1024:CA["causal"][0] + (j + 1) * 1024] for j in range(2)]
    ord_done, tk_full, tk_out, h_full, h_out = (Signal(nc.alloc_semaphore(name=n), per) for n, per in (
        ("ord_done", 4), ("tk_full", 8), ("tk_out", 8), ("h_full", 2), ("h_out", 2)))

    def order_pairs(dve, b, j, t):
        if t == 0:
            dve.wait_ge(ld_cmp[j], (b - j) * 64 + 128)
        if t >= 2:
            dve.wait_ge(tk_full.sem, tk_full.at(b, 2 * t - 2))
        nc.vector.tensor_copy(order[t % 2].rearrange("p (c a d) -> p a c d", a=2, d=DH),
                              pages_c[j][:, t].rearrange("p a (c d) -> p a c d", d=DH)).then_inc(ord_done.sem, 1)

    def turn_pairs(n, bank):
        for g in range(G):
            at = (n % 2 * G + g) * P
            mm = tr(psum[:, bank, g * P:(g + 1) * P], order[n // 2 % 2][:, at:at + P], P)
        mm.then_inc(tk_full.sem, 1)

    def pairs_out(act, b, n, bank):
        act.wait_ge(tk_full.sem, tk_full.at(b, n + 1))
        nc.scalar.activation(kct_s[:, n % 2, :, n // 2 * P:(n // 2 + 1) * P],
                             psum[:, bank, :].rearrange("p (g n) -> p g n", g=G), ACT.Copy).then_inc(tk_out.sem, 1)

    def hidden_layer(t, out):
        for j in range(16):
            mm = nc.tensor.matmul(out, w1[:, t, j, :], kct_s[:, t, :, j:j + 8 * (NCS - 1) + 1:8],
                                  start=(j == 0), stop=(j == 15))
        mm.then_inc(h_full.sem, 1)

    def hidden_out(act, b, t, src):
        act.wait_ge(h_full.sem, h_full.at(b, t + 1))
        nc.scalar.activation(hid_s[:, t, :], src, ACT.Silu, bias=pebias[:, t:t + 1]).then_inc(h_out.sem, 1)

    arena.at = base_all
    mixed = take(KT * T).rearrange("p (k t) -> p k t", k=KT)
    qsm = take(KT * NB).rearrange("p (k b) -> p k b", k=KT)
    zsm = take(3 * KT * NB).rearrange("p (r k b) -> p r k b", r=3, k=KT)
    kns = take(2 * G * NB).rearrange("p (r g b) -> p r g b", r=2, g=G)
    gsm = take(3 * NB).rearrange("p (r b) -> p r b", r=3)
    base_smp = arena.at
    gtok = take(4 * 3 * NH).rearrange("p (a h r) -> p a h r", a=4, r=3)
    base_nsa = arena.at
    assert base_nsa <= base_y

    def load_q(eng, g):
        eng.dma_start(slot_a, n_in[:, :, bass.ds(g * 256, 256)]).then_inc(ld_a, 16)

    def load_kv(eng, g):
        for t in range(4):
            eng.dma_start(slot_b[:, :, t * DH:(t + 1) * DH],
                          n_in[:, :, bass.ds(g * DH + (AW + 256 * t), DH)]).then_inc(ld_b, 16)

    def load_w(eng, g):
        for t in range(2):
            eng.dma_start(slot_c[:, :, t * DH:(t + 1) * DH],
                          n_in[:, :, bass.ds(g * DH + (AW + 256 * (4 + t)), DH)]).then_inc(ld_c, 16)

    def load_z(eng, g, r, slot, s):
        eng.dma_start(slot, n_in[:, :, bass.ds(g * 256 + (Z0 + AW * r), 256)]).then_inc(s, 16)

    def conv_pe(pe):
        for j in range(8):
            if j >= 4:
                pe.wait_ge(tr_out, j - 3)
            for c in range(4):
                mm = tr(psum[0:11, 4 + j % 4, c * P:(c + 1) * P], tail[:, 4 * j + c, :], P)
            mm.then_inc(tr_full, 1)

    def conv_act(act):
        for j in range(8):
            act.wait_ge(tr_full, j + 1)
            nc.scalar.activation(conv_rows[0:11, j * 512:(j + 1) * 512], psum[0:11, 4 + j % 4, :], ACT.Copy).then_inc(tr_out, 1)

    def conv_sp(sp):
        sp.dma_start(per[0:32, :], io["nsa_cmp_pe"][0].rearrange("t (j a) d -> (t j) (a d)", a=2)).then_inc(ld_pre, 16)
        sp.dma_start(wg, n_in[:, :, GATE0:Z0]).then_inc(ld_pre, 16)
        for t in range(2):
            sp.dma_start(w1[:, t], io["nsa_cmp_w1"][0, t].rearrange("(j p) n -> p j n", p=P)).then_inc(ld_w1, 16)
            sp.dma_start(w2k[:, t * DH:(t + 1) * DH], io["nsa_cmp_w2"][0, 0]).then_inc(ld_w1, 16)
        sp.dma_start(w2v, io["nsa_cmp_w2"][0, 1]).then_inc(ld_w1, 16)
        load_q(sp, 0)
        load_kv(sp, 0)
        load_w(sp, 0)
        load_z(sp, 0, 0, slot_d, ld_d)
        sp.wait_ge(tr_out, 8)
        sp.dma_start(io["conv_prompt"][0, 0], conv_rows[0:3, :]).then_inc(st_conv, 16)
        sp.dma_start(io["conv_sample"][0][:, 2, :], conv_rows[3:11, :]).then_inc(st_conv, 16)
        sp.wait_ge(st_conv, 32)
        sp.wait_ge(st_pass, 16 * 9)

    def gates_pe(pe, xnd):
        pe.wait_ge(ld_pre, 32)
        tr(psum[:, 0, 0:32], per[0:32, :], 32).then_inc(pre_pet, 1)
        pe.wait_ge(ld_w1, 80)
        pe.wait_ge(pre_pec, 1)
        for t in range(2):
            for j in range(16):
                mm = nc.tensor.matmul(psum[:, 1, t:t + 1], w1[:, t, j, :], peT[:, t * 16 + j:t * 16 + j + 1],
                                      start=(j == 0), stop=(j == 15))
        mm.then_inc(pre_full, 1)
        for h in range(2):
            for k in range(KT):
                if h == 0:
                    pe.wait_ge(xnd, k + 1)
                nc.tensor.matmul(psum[0:3 * NH, 6 + h, 0:HALF], wg[:, k, :], xn[:, k, h * HALF:(h + 1) * HALF],
                                 start=(k == 0), stop=(k == KT - 1))
        for r in range(3):
            for k in range(KT):
                mm = nc.tensor.matmul(psum[0:NH, 4, r * NB:(r + 1) * NB], wg[:, k, r:3 * NH:3], xn[:, k, SEQ:T],
                                      start=(k == 0), stop=(k == KT - 1))
        mm.then_inc(pre_gs, 1)
        pe.wait_ge(pre_gto, 2)
        for a in range(4):
            mm = tr(psum[:, 5, a * 48:(a + 1) * 48], gT[0:48, a * P:(a + 1) * P], 48)
        mm.then_inc(pre_gt, 1)

    def gates_act(act):
        act.wait_ge(pre_pet, 1)
        nc.scalar.activation(peT, psum[:, 0, 0:32], ACT.Copy).then_inc(pre_pec, 1)
        act.wait_ge(pre_full, 1)
        nc.scalar.activation(pebias, psum[:, 1, 0:2], ACT.Copy).then_inc(pre_out, 1)
        act.wait_ge(pre_gs, 1)
        nc.scalar.activation(gT[0:48, :].rearrange("p (h t) -> p h t", h=2), halves(psum, 6, 48), ACT.Sigmoid).then_inc(pre_gto, 1)
        nc.scalar.activation(gsm[0:NH], psum[0:NH, 4, 0:3 * NB].rearrange("p (r b) -> p r b", r=3), ACT.Sigmoid).then_inc(pre_gto, 1)
        act.wait_ge(pre_gto, 2)

    def gates_dve(dve):
        dve.wait_ge(pre_gt, 1)
        nc.vector.tensor_copy(gtok, psum[:, 5, 0:192].rearrange("p (a h r) -> p a h r", a=4, r=3)).then_inc(pre_out, 1)
        dve.wait_ge(pre_out, 2)

    project_out("o1", 16, yT, io["ssd_w_out"][0], w_rooms, o1_ld, 2, PR_N2,
                {"sync": conv_sp, "tensor": conv_pe, "scalar": conv_act,
                 "tensor_last": gates_pe, "scalar_last": gates_act, "vector_last": gates_dve},
                begun=o1_begun)

    free_semaphores()
    arena.at = base_nsa
    arena.size += KT * 3 * NH + P
    qraw = take(2 * T).rearrange("p (c t) -> p c t", c=2)
    kvraw = take(3 * T).rearrange("p (c t) -> p c t", c=3)
    zraw2 = take(6 * T).rearrange("p (c t) -> p c t", c=6)
    qT = take(2 * T).rearrange("p (c t) -> p c t", c=2)
    zs2 = take(6 * T).rearrange("p (c t) -> p c t", c=6)
    kd = take(2 * T).rearrange("p (r t) -> p r t", r=2)
    kcs = take(2 * T).rearrange("p (r t) -> p r t", r=2)
    vtok = take(4 * 3 * P).rearrange("p (a c n) -> p a c n", a=4, c=3)
    smtok = take(3 * P)
    strip = take(4 * SEQ).rearrange("p (h k) -> p h k", h=4)
    bct = take(4 * SEQ).rearrange("p (h q) -> p h q", h=4)
    shared = take(5 * SEQ)
    s_sb = [shared[:, j * SEQ:(j + 1) * SEQ] for j in range(3)]
    p_t = [shared[:, (3 + j) * SEQ:(4 + j) * SEQ] for j in range(2)]
    pct = shared[:, 0:4 * SEQ].rearrange("p (h q) -> p h q", h=4)
    osb = take(4 * 3 * 2 * P).rearrange("p (a r i n) -> p a r i n", a=4, r=3, i=2)
    mixt = shared[:, 0:SEQ]
    hid = take(2 * NCP).rearrange("p (t c) -> p t c", t=2)
    kct = take(NCP)
    vc = take(DH)
    cbias = take(16 * NCP).rearrange("p (e n) -> p e n", e=2)
    sc = take(16 * NCP).rearrange("p (e n) -> p e n", e=2)
    mx = take(16)
    dn = take(16)
    rg = take(16)
    top = take(32)
    ntop = take(32)
    den = take(32).rearrange("p (h u) -> p h u", h=4)
    rgs = take(8)

    ld_dup, ld_strip, st_kv = sem("ld_dup"), sem("ld_strip"), sem("st_kv")
    NT = 11
    UN = 32
    t_full, t_out = sig("t_full", NT), sig("t_out", NT)
    q_ready, z2_ready = sig("q_ready"), sig("z2_ready")
    kvt_full, kvt_out, cap_done = sig("kvt_full"), sig("kvt_out", 2), sig("cap_done")
    hid_full, hid_out, ckv_full, ckv_out, cb_full, cb_out = (
        sig("hid_full"), sig("hid_out"), sig("ckv_full"), sig("ckv_out"), sig("cb_full"), sig("cb_out"))
    sc_full, sc_ready, ec_done, pct_full, pct_out, oc_full, oc_out = (
        sig("sc_full"), sig("sc_ready"), sig("ec_done"), sig("pct_full"), sig("pct_out", 2), sig("oc_full"), sig("oc_out"))
    s_full, s_out, p_ready, pt_full, pt_act, pt_dve, pv_done, head_out = (
        sig("s_full", UN), sig("s_out", UN), sig("p_ready", UN), sig("pt_full", UN), sig("pt_act", UN // 2),
        sig("pt_dve", UN // 2), sig("pv_done", UN), sig("head_out", 4))
    of_full, of_out = sig("of_full", 6), sig("of_out", 6)
    top_done = sig("top_done", UN)
    carrier = sem("carrier2")
    dve_nsa = sig("dve_nsa", 3 + 4 + 8 + 4)

    def unit(u):
        return u // 8, u % 8 // 4, u % 4

    with nc.Block() as block:
        @block.sync
        def _(sp):
            def strips(i):
                for h in range(4):
                    sp.dma_start(strip[:, h, :], bass.AP(scr_f.tensor, (i * 4 + h) * FLEN + 384, [[1, P], [1, SEQ]]))\
                        .then_inc(ld_strip, 16)
                    sp.dma_start(bct[0:NCP, h, :], bass.AP(scr_f.tensor, (i * 4 + h) * FLEN, [[16, NCP], [1, SEQ]]))\
                        .then_inc(ld_strip, 16)

            def stores(i):
                sp.wait_ge(kvt_out.sem, kvt_out.at(i, 2))
                for a in range(4):
                    sp.dma_start(io["kv_prompt"][0, a * P:(a + 1) * P, 0, :, bass.ds(i, 1), :].rearrange("s t o d -> s t (o d)"),
                                 vtok[:, a, 0:2, :].rearrange("p c (t d) -> p (c t) d", t=2)).then_inc(st_kv, 16)
                    sp.dma_start(io["win_prompt"][0, 0, a * P:(a + 1) * P, :, bass.ds(i, 1), :].rearrange("s t o d -> s t (o d)"),
                                 vtok[:, a, 2, :].rearrange("p (t d) -> p t d", t=2)).then_inc(st_kv, 16)
                sp.dma_start(io["kv_sample"][:, 0, 0, :, bass.ds(i, 1), :].rearrange("s t o d -> s t (o d)"),
                             smtok[0:NB, 0:256].rearrange("p (t d) -> p t d", t=4)).then_inc(st_kv, 16)
                sp.dma_start(io["win_sample"][0, :, 511, :, bass.ds(i, 1), :].rearrange("s t o d -> s t (o d)"),
                             smtok[0:NB, 256:384].rearrange("p (t d) -> p t d", t=2)).then_inc(st_kv, 16)
                sp.dma_start(scr_new[:, :, bass.ds(i, 1), :].rearrange("s t o d -> s t (o d)"),
                             smtok[0:NB, 0:384].rearrange("p (t d) -> p t d", t=6)).then_inc(st_kv, 16)

            def early_loads(i):
                sp.wait_ge(t_full.sem, t_full.at(i - 1, 11))
                load_q(sp, i)
                load_kv(sp, i)
                load_w(sp, i)
                load_z(sp, i, 0, slot_d, ld_d)

            def late_loads(i):
                sp.wait_ge(t_full.sem, t_full.at(i, 2))
                load_z(sp, i, 1, slot_a, ld_a)
                sp.wait_ge(t_full.sem, t_full.at(i, 4))
                load_z(sp, i, 2, slot_b, ld_b)

            def turn(i, more=True, first=False):
                if more:
                    early_loads(i + 1)
                if not first:
                    sp.wait_ge(s_out.sem, s_out.at(i, 0))
                strips(i)
                stores(i)
                if more:
                    late_loads(i + 1)

            late_loads(0)
            turn(0, first=True)
            with sp.Fori(1, G - 1) as i:
                turn(i)
            turn(G - 1, more=False)
            sp.dma_start(ptab[0:1, :], io["page_table"].rearrange("b n -> (b n)").unsqueeze(0)).then_inc(ld_tab, 16)
            sp.wait_ge(ld_tab, 16)
            sp.wait_ge(t_full.sem, NT * G)
            load_pages(sp, 0, 0, pages_c[0], ld_cmp[0])
            load_window(sp, 0, 0)
            sp.wait_ge(st_kv, 16 * 11 * G)

        @block.gpsimd
        def _(pool):
            def turn(i, first=False):
                pool.wait_ge(t_out.sem, t_out.at(i, 5))
                if not first:
                    pool.wait_ge(pv_done.sem, pv_done.at(i, 0))
                    pool.wait_ge(cap_done.sem, cap_done.at(i, 0))
                    pool.sem_inc(carrier, 1)
                for half in range(2):
                    lo = slice(half * 64, half * 64 + 64)
                    n = T - half
                    for r in range(2):
                        pool.dma_start(kd[lo, r, :], kvraw[0:64, 1 + r, :]).then_inc(ld_dup, 16)
                        pool.dma_start(kcs[lo, r, 0:n], kvraw[r * 64:r * 64 + 64, 0, half:T]).then_inc(ld_dup, 16)
                pool.wait_ge(q_ready.sem, q_ready.at(i, 1))
                pool.wait_ge(z2_ready.sem, z2_ready.at(i, 1))
                nc.gpsimd.tensor_copy(qsm[:, bass.ds(i * 2, 2), :], qT[:, :, SEQ:T])
                for r in range(3):
                    nc.gpsimd.tensor_copy(zsm[:, r, bass.ds(i * 2, 2), :], zs2[:, 2 * r:2 * r + 2, SEQ:T])
                pool.wait_ge(ld_dup, i * 128 + 128)
                for r in range(2):
                    ins = nc.gpsimd.tensor_copy(kns[:, r, bass.ds(i, 1), :], kd[:, r:r + 1, SEQ:T])
                ins.then_inc(cap_done.sem, 1)

            turn(0, True)
            with pool.Fori(1, G) as i:
                turn(i)
            pool.wait_ge(cap_done.sem, G)

        @block.tensor
        def _(pe):
            def project(g, n, first=False):
                w, at, s, v = {0: (slot_a, 0, ld_a, g * 32 + 16), 1: (slot_a, 1, ld_a, g * 32 + 16),
                               2: (slot_b, 0, ld_b, g * 80 + 64), 3: (slot_b, 1, ld_b, g * 80 + 64),
                               4: (slot_c, 0, ld_c, g * 32 + 32),
                               5: (slot_d, 0, ld_d, g * 16 + 16), 6: (slot_d, 1, ld_d, g * 16 + 16),
                               7: (slot_a, 0, ld_a, g * 32 + 32), 8: (slot_a, 1, ld_a, g * 32 + 32),
                               9: (slot_b, 0, ld_b, g * 80 + 80), 10: (slot_b, 1, ld_b, g * 80 + 80)}[n]
                pe.wait_ge(s, v)
                pair = n % 2 * 2 if first else 0
                if not first:
                    pe.wait_ge(t_out.sem, t_out.at(g, n))
                elif n >= 2:
                    pe.wait_ge(t_out.sem, n - 1)
                for k in range(KT):
                    for h in range(2):
                        mm = nc.tensor.matmul(psum[:, pair + h, 0:HALF], w[:, k, at * P:(at + 1) * P],
                                              xn[:, k, h * HALF:(h + 1) * HALF], start=(k == 0), stop=(k == KT - 1))
                mm.then_inc(t_full.sem, 1)

            def first_sequence(u):
                if u in (4, 6, 11, 16):
                    for n in {4: (0, 1), 6: (2, 3), 11: (4, 5), 16: (6, 7)}[u]:
                        if n == 0:
                            pe.wait_ge(t_out.sem, NT * G)
                        if n % 2 == 0:
                            pe.wait_ge(ord_done.sem, n // 2 + 1)
                        if n >= 2:
                            pe.wait_ge(tk_out.sem, n - 1)
                        turn_pairs(n, n % 2)
                elif u in (19, 24):
                    t = (u - 19) // 5
                    pe.wait_ge(tk_out.sem, 8)
                    hidden_layer(t, psum[:, t, 0:G * NCS])

            def turn(i, more=True, first=False):
                def nxt(n):
                    if more:
                        project(i + 1, n)

                nxt(0)
                pe.wait_ge(t_out.sem, NT - 1 if first else t_out.at(i, 5))
                if not first:
                    pe.wait_ge(of_out.sem, of_out.at(i, 0))
                for c in range(3):
                    for a in range(4):
                        tr(psum[:, 2 + c, a * P:(a + 1) * P], kvraw[:, c, a * P:(a + 1) * P], P)
                for c in range(3):
                    mm = tr(psum[0:NB, 5, c * P:(c + 1) * P], kvraw[:, c, SEQ:T], P)
                mm.then_inc(kvt_full.sem, 1)
                pe.wait_ge(ld_dup, i * 128 + 128)
                for t in range(2):
                    for j in range(16):
                        mm = nc.tensor.matmul(psum[:, 6, t * NCP:(t + 1) * NCP], w1[:, t, j, :],
                                              kcs[:, t, 2 * j:2 * j + 16 * (NCP - 1) + 1:16], start=(j == 0), stop=(j == 15))
                mm.then_inc(hid_full.sem, 1)
                nxt(1)
                pe.wait_ge(hid_out.sem, hid_out.at(i, 1))
                nc.tensor.matmul(psum[:, 7, 0:NCP], w2k, hid[:, 0, :], start=True, stop=True)
                nc.tensor.matmul(psum[0:NCP, 7, 64:128], hid[:, 1, :], w2v, start=True, stop=True).then_inc(ckv_full.sem, 1)
                pe.wait_ge(ld_strip, i * 128 + 128)
                pe.wait_ge(kvt_out.sem, kvt_out.at(i, 2))
                pe.sem_inc(carrier, 1)
                for h in range(4):
                    for a in range(4):
                        o = (h // 2 * 4 + a) * NCP
                        mm = tr(psum[:, 2 + h % 2, o:o + NCP], bct[0:NCP, h, a * P:(a + 1) * P], NCP)
                mm.then_inc(cb_full.sem, 1)
                nxt(2)
                pe.wait_ge(q_ready.sem, q_ready.at(i, 1))
                pe.wait_ge(ckv_out.sem, ckv_out.at(i, 1))
                for h in range(4):
                    lo = slice(h % 2 * 64, h % 2 * 64 + 64)
                    for a in range(4):
                        o = (h // 2 * 4 + a) * NCP
                        mm = nc.tensor.matmul(psum[:, 4 + h % 2, o:o + NCP], qT[lo, h // 2, a * P:(a + 1) * P],
                                              kct[lo, :], start=True, stop=True)
                mm.then_inc(sc_full.sem, 1)
                nxt(3)
                pe.wait_ge(ec_done.sem, ec_done.at(i, 1))
                pe.wait_ge(cb_out.sem, cb_out.at(i, 1))
                for h in range(4):
                    for a in range(4):
                        o = (h // 2 * 4 + a) * NCP
                        mm = tr(psum[0:NCP, (2, 3, 6, 7)[h], a * P:(a + 1) * P], sc[:, h % 2, o:o + NCP], P)
                mm.then_inc(pct_full.sem, 1)
                nxt(4)
                pe.wait_ge(pct_out.sem, pct_out.at(i, 2))
                for h in range(4):
                    for a in range(4):
                        o = (h * 4 + a) * DH
                        mm = nc.tensor.matmul(psum[:, 4 + o // 512, o % 512:o % 512 + DH], pct[0:NCP, h, a * P:(a + 1) * P],
                                              vc[0:NCP, :], start=True, stop=True)
                mm.then_inc(oc_full.sem, 1)
                for u in range(UN + 2):
                    if u < UN:
                        h, r, a = unit(u)
                        lo = slice(h % 2 * 64, h % 2 * 64 + 64)
                        n = (a + 1) * P
                        if u >= 3:
                            pe.wait_ge(s_out.sem, s_out.at(i, u - 2))
                        if u == 2:
                            pe.wait_ge(oc_out.sem, oc_out.at(i, 1))
                        nc.tensor.matmul(psum[:, 2 + u % 3, 0:n], qT[lo, h // 2, a * P:(a + 1) * P], kd[lo, r, 0:n],
                                         start=True, stop=True).then_inc(s_full.sem, 1)
                    if 1 <= u <= UN:
                        v = u - 1
                        a = unit(v)[2]
                        pe.wait_ge(p_ready.sem, p_ready.at(i, v + 1))
                        if v == 0:
                            pe.wait_ge(oc_out.sem, oc_out.at(i, 1))
                        if v >= 2:
                            w = pt_act if v % 2 else pt_dve
                            pe.wait_ge(w.sem, w.at(i, v // 2))
                        for b in range(a + 1):
                            mm = tr(psum[:, 5 + v % 2, b * P:(b + 1) * P], s_sb[v % 3][:, b * P:(b + 1) * P], P)
                        mm.then_inc(pt_full.sem, 1)
                    if u >= 2:
                        v = u - 2
                        h, r, a = unit(v)
                        w = pt_act if v % 2 else pt_dve
                        pe.wait_ge(w.sem, w.at(i, v // 2 + 1))
                        if v % 8 == 0 and v:
                            pe.wait_ge(head_out.sem, head_out.at(i, v // 8))
                        for b in range(a + 1):
                            mm = nc.tensor.matmul(psum[:, 7, v % 8 * DH:(v % 8 + 1) * DH], p_t[v % 2][:, b * P:(b + 1) * P],
                                                  vtok[:, b, 1 + r, DH:P], start=(b == 0), stop=(b == a))
                        mm.then_inc(pv_done.sem, 1)
                    if u % 5 == 4 and u // 5 < 6:
                        nxt(5 + u // 5)
                    if not more:
                        first_sequence(u)
                pe.wait_ge(head_out.sem, head_out.at(i, 4))
                for j in range(6):
                    for a in range(4):
                        mm = tr(psum[:, 2 + j, a * P:(a + 1) * P], osb[:, a, j // 2, j % 2, :], P)
                    mm.then_inc(of_full.sem, 1)

            for n in range(NT):
                project(0, n, True)
            turn(0, first=True)
            with pe.Fori(1, G - 1) as i:
                turn(i)
            turn(G - 1, more=False)

        @block.scalar
        def _(act):
            def evacuate(g, n, first=False):
                act.wait_ge(t_full.sem, t_full.at(g, n + 1))
                dst = qraw[:, n, :] if n < 2 else kvraw[:, n - 2, :] if n < 5 else zraw2[:, n - 5, :]
                nc.scalar.activation(dst.rearrange("p (h t) -> p h t", h=2), halves(psum, n % 2 * 2 if first else 0),
                                     ACT.Copy).then_inc(t_out.sem, 1)

            def turn(i, more=True, first=False):
                def nxt(n):
                    if more:
                        evacuate(i + 1, n)

                act.wait_ge(t_out.sem, t_out.at(i, NT))
                if not first:
                    act.wait_ge(pv_done.sem, pv_done.at(i, 0))
                    act.wait_ge(cap_done.sem, cap_done.at(i, 0))
                nc.scalar.activation(qT, qraw, ACT.Copy, scale=DH ** -0.5).then_inc(q_ready.sem, 1)
                if not first:
                    act.wait_ge(of_out.sem, of_out.at(i, 0))
                nc.scalar.activation(zs2, zraw2, ACT.Silu).then_inc(z2_ready.sem, 1)
                act.wait_ge(kvt_full.sem, kvt_full.at(i, 1))
                if not first:
                    act.wait_ge(st_kv, i * (16 * 11))
                for c in range(3):
                    ins = nc.scalar.activation(vtok[:, :, c, :], psum[:, 2 + c, :].rearrange("p (a n) -> p a n", a=4), ACT.Copy)
                ins.then_inc(kvt_out.sem, 1)
                nc.scalar.activation(smtok[0:NB, :], psum[0:NB, 5, 0:384], ACT.Copy).then_inc(kvt_out.sem, 1)
                act.wait_ge(q_ready.sem, q_ready.at(i, 1))
                nxt(0)
                act.wait_ge(hid_full.sem, hid_full.at(i, 1))
                for t in range(2):
                    ins = nc.scalar.activation(hid[:, t, :], psum[:, 6, t * NCP:(t + 1) * NCP], ACT.Silu,
                                               bias=pebias[:, t:t + 1])
                ins.then_inc(hid_out.sem, 1)
                nxt(1)
                act.wait_ge(ckv_full.sem, ckv_full.at(i, 1))
                nc.scalar.activation(kct, psum[:, 7, 0:NCP], ACT.Copy)
                nc.scalar.activation(vc[0:NCP, :], psum[0:NCP, 7, 64:128], ACT.Copy).then_inc(ckv_out.sem, 1)
                act.wait_ge(cb_full.sem, cb_full.at(i, 1))
                nc.scalar.activation(cbias.rearrange("p e (x c) -> p e x c", c=NCP)[:, :, :, ::-1],
                                     psum[:, 2:4, 0:8 * NCP].rearrange("p e (x c) -> p e x c", c=NCP), ACT.Copy).then_inc(cb_out.sem, 1)
                act.wait_ge(ld_dup, i * 128 + 128)
                nxt(2)
                act.wait_ge(sc_ready.sem, sc_ready.at(i, 1))
                nc.scalar.activation(sc, sc, ACT.Exp).then_inc(ec_done.sem, 1)
                nxt(3)
                act.wait_ge(pct_full.sem, pct_full.at(i, 1))
                if not first:
                    act.wait_ge(of_out.sem, of_out.at(i, 0))
                for j in range(2):
                    nc.scalar.activation(pct[0:NCP, 2 * j:2 * j + 2, :], psum[0:NCP, (2, 6)[j]:(4, 8)[j], :],
                                         ACT.Copy).then_inc(pct_out.sem, 1)
                nxt(4)
                act.wait_ge(z2_ready.sem, z2_ready.at(i, 1))
                for u in range(UN + 1):
                    if u < UN:
                        h, r, a = unit(u)
                        n = (a + 1) * P
                        act.wait_ge(s_out.sem, s_out.at(i, u + 1))
                        nc.scalar.activation(s_sb[u % 3][:, 0:n], s_sb[u % 3][:, 0:n], ACT.Exp, bias=ntop[:, u:u + 1],
                                             accum_out=den[:, h, u % 8:u % 8 + 1]).then_inc(p_ready.sem, 1)
                    if u >= 1 and (u - 1) % 2:
                        v = u - 1
                        n = (unit(v)[2] + 1) * P
                        act.wait_ge(pt_full.sem, pt_full.at(i, v + 1))
                        if v >= 2:
                            act.wait_ge(pv_done.sem, pv_done.at(i, v - 1))
                        nc.scalar.activation(p_t[1][:, 0:n], psum[:, 6, 0:n], ACT.Copy).then_inc(pt_act.sem, 1)
                    if u % 5 == 4 and u // 5 < 6:
                        nxt(5 + u // 5)
                    if not more and u in (5, 7, 12, 17):
                        for n in {5: (0, 1), 7: (2, 3), 12: (4, 5), 17: (6, 7)}[u]:
                            pairs_out(act, 0, n, n % 2)
                    if not more and u in (21, 26):
                        t = (u - 21) // 5
                        hidden_out(act, 0, t, psum[:, t, 0:G * NCS])

            for n in range(NT):
                evacuate(0, n, True)
            turn(0, first=True)
            with act.Fori(1, G - 1) as i:
                turn(i)
            turn(G - 1, more=False)

        @block.vector
        def _(dve):
            def turn(i, more=True):
                s = Steps(dve, dve_nsa)
                s.turn(i)
                dve.wait_ge(sc_full.sem, sc_full.at(i, 1))
                dve.wait_ge(cb_out.sem, cb_out.at(i, 1))
                s.link(nc.vector.tensor_tensor(sc, psum[:, 4:6, 0:8 * NCP], cbias, ALU.add))
                sc_b = sc.rearrange("p e (x c) -> p (e x) c", c=NCP)
                s.link(nc.vector.tensor_reduce(mx, sc_b, AX.X, ALU.max))
                s.link(nc.vector.tensor_scalar(mx, mx, GUARD, None, ALU.max))
                s.post(nc.vector.tensor_tensor(sc_b, sc_b, mx.unsqueeze(2).to_broadcast([P, 16, NCP]), ALU.subtract),
                       sc_ready)
                dve.wait_ge(ec_done.sem, ec_done.at(i, 1))
                s.link(nc.vector.tensor_reduce(dn, sc_b, AX.X, ALU.add))
                s.link(nc.vector.tensor_scalar(dn, dn, 1e-30, None, ALU.max))
                s.link(nc.vector.reciprocal(dn, dn))
                for h in range(4):
                    o = h % 2 * 8 + h // 2 * 4
                    ins = nc.vector.tensor_tensor(rg[:, h * 4:h * 4 + 4], dn[:, o:o + 4],
                                                  gtok[:, :, bass.ds(i * 4 + h, 1), 0].rearrange("p a o -> p (a o)"), ALU.mult)
                s.link(ins)
                dve.wait_ge(oc_full.sem, oc_full.at(i, 1))
                for h in range(4):
                    ins = nc.vector.tensor_tensor(osb[:, :, 0, h // 2, h % 2 * DH:(h % 2 + 1) * DH],
                                                  psum[:, 4 + h // 2, h % 2 * 256:h % 2 * 256 + 256].rearrange("p (a d) -> p a d", a=4),
                                                  rg[:, h * 4:h * 4 + 4].unsqueeze(2).to_broadcast([P, 4, DH]), ALU.mult)
                s.post(ins, oc_out)
                dve.wait_ge(ld_strip, i * 128 + 128)
                for u in range(UN + 2):
                    if u < UN:
                        h, r, a = unit(u)
                        n = (a + 1) * P
                        if u >= 3:
                            dve.wait_ge(pt_full.sem, pt_full.at(i, u - 2))
                        dve.wait_ge(s_full.sem, s_full.at(i, u + 1))
                        dve.sem_inc(carrier, 1)
                        nc.vector.tensor_tensor_reduce(out=s_sb[u % 3][:, 0:n], in0=psum[:, 2 + u % 3, 0:n],
                                                       in1=strip[:, h, n - 1::-1], scale=1.0, scalar=-3e38,
                                                       op0=ALU.add, op1=ALU.max, accum_out=top[:, u:u + 1])\
                            .then_inc(top_done.sem, 1)
                        dve.wait_ge(top_done.sem, top_done.at(i, u + 1))
                        s.post(nc.vector.tensor_scalar(ntop[:, u:u + 1], top[:, u:u + 1], -1.0, None, ALU.mult), s_out)
                    if not more and u in (1, 9, 14):
                        for t in {1: (0, 1), 9: (2,), 14: (3,)}[u]:
                            order_pairs(dve, 0, 0, t)
                    if u >= 1 and (u - 1) % 2 == 0 and u - 1 < UN:
                        v = u - 1
                        n = (unit(v)[2] + 1) * P
                        dve.wait_ge(pt_full.sem, pt_full.at(i, v + 1))
                        if v >= 2:
                            dve.wait_ge(pv_done.sem, pv_done.at(i, v - 1))
                        s.post(nc.vector.tensor_copy(p_t[0][:, 0:n], psum[:, 5, 0:n]), pt_dve)
                    if u >= 2 and (u - 2) % 8 == 7:
                        h = (u - 2) // 8
                        dve.wait_ge(p_ready.sem, p_ready.at(i, h * 8 + 8))
                        s.link(nc.vector.reciprocal(rgs, den[:, h, :]))
                        s.link(nc.vector.tensor_tensor(rgs.rearrange("p (r a) -> p r a", r=2), rgs.rearrange("p (r a) -> p r a", r=2),
                                                       gtok[:, :, bass.ds(i * 4 + h, 1), 1:3].rearrange("p a o r -> p (o r) a"),
                                                       ALU.mult))
                        dve.wait_ge(pv_done.sem, pv_done.at(i, h * 8 + 8))
                        s.link(nc.vector.tensor_tensor(osb[:, :, 1:3, h // 2, h % 2 * DH:(h % 2 + 1) * DH].rearrange("p a r d -> p r a d"),
                                                       psum[:, 7, :].rearrange("p (r a d) -> p r a d", r=2, a=4),
                                                       rgs.rearrange("p (r a) -> p r a", r=2).unsqueeze(3).to_broadcast([P, 2, 4, DH]),
                                                       ALU.mult), head_out)
                for j in range(6):
                    r, k = j // 2, j % 2
                    m = mixed[:, bass.ds(i * 2 + k, 1), 0:SEQ].rearrange("p o t -> p (o t)")
                    dve.wait_ge(of_full.sem, of_full.at(i, j + 1))
                    if r == 0:
                        s.link(nc.vector.tensor_tensor(m, psum[:, 2 + j, :], zs2[:, j, 0:SEQ], ALU.mult), of_out)
                    else:
                        s.link(nc.vector.tensor_tensor(mixt, psum[:, 2 + j, :], zs2[:, j, 0:SEQ], ALU.mult))
                        s.link(nc.vector.tensor_tensor(m, m, mixt, ALU.add), of_out)
                s.turn(i)

            with dve.Fori(0, G - 1) as i:
                turn(i)
            turn(G - 1, more=False)


    free_semaphores()
    arena.at = base_smp
    arena.size = top_nsa - 7168
    o2_rooms = [arena.block[:, base_smp + j * 2048:base_smp + (j + 1) * 2048].rearrange("p (k n) -> p k n", k=KT)
                for j in range(2)]
    o2_ld = [sem("o2_ld0"), sem("o2_ld1")]
    pages_s = [take(4 * 2 * 512).rearrange("p (t a c) -> p t a c", t=4, a=2) for _ in range(2)]
    pages_c.append(take(4 * 2 * 512).rearrange("p (t a c) -> p t a c", t=4, a=2))
    wins.append(take(2 * 2 * 512).rearrange("p (t a c) -> p t a c", t=2, a=2))
    vnew = [take(512) for _ in range(2)]
    kselt = take(2 * 2 * NPAIR).rearrange("p (h a n) -> p h a n", h=2, a=2)
    kwint = take(2 * 2 * NWP).rearrange("p (h a n) -> p h a n", h=2, a=2)
    kcmp = take(2 * NCS).rearrange("p (h n) -> p h n", h=2)
    vcmp = take(G * DH)
    s_row = take(KEYS)
    b_row = take(KEYS)
    qsw = take(KT * NB).rearrange("p (k b) -> p k b", k=KT)
    qb = take(2 * NH * NB).rearrange("p (g h b) -> p g h b", g=2, h=NH)
    qcur = take(2 * NH).rearrange("p (g h) -> p g h", g=2)
    kcur = take(2 * 2).rearrange("p (r g) -> p r g", r=2)
    pcg = take(NCS)
    pcT = take(2 * NH)
    impH = take(NSEL)
    cand = take(14)
    keyed = take(14)
    dropped = take(16)
    stat = take(12)
    ptb = take(12 * NH)
    ptn = take(2 * NH)
    o_all = take(NB * 6 * NH).rearrange("p (b n) -> p b n", b=NB)
    o_swp = kselt.rearrange("p h a n -> p (h a n)")[:, 0:NB * 6 * NH].rearrange("p (b n) -> p b n", b=NB)
    msm = take(KT * NB).rearrange("p (k b) -> p k b", k=KT)
    mtmp = take(KT * NB).rearrange("p (k b) -> p k b", k=KT)
    S_SEL, S_NEWS, S_WIN, S_NEWW, S_CMP = 0, SKEYS - 1, SKEYS, SKEYS + WKEYS - 1, SKEYS + WKEYS

    ld_bias = sem("ld_bias")
    NLD = 16 * 11
    swap_full, swap_out, qb_done, pad_done, osw_full, osw_out = (
        sem(n) for n in ("swap_full", "swap_out", "qb_done", "pad_done", "osw_full", "osw_out"))
    ts_full, ts_out = sig("ts_full", 6), sig("ts_out", 6)
    kv_full, kv_out = sig("kvs_full"), sig("kvs_out", 2)
    cur_done, score_full, score_used, c_ready, c_exp, pc_done = (
        sig("cur_done"), sig("score_full"), sig("score_used"), sig("c_ready"), sig("c_exp"), sig("pc_done"))
    pcT_full, pcT_out, imp_full, imp_out, grp_full = (
        sig("pcT_full"), sig("pcT_out"), sig("imp_full"), sig("imp_out"), sig("grp_full"))
    w_ready, sel_ready, w_exp, sel_exp, probs_done = (
        sig("w_ready"), sig("sel_ready"), sig("w_exp"), sig("sel_exp"), sig("probs_done"))
    ptb_full, ptb_out, os_full, os_out = sig("ptb_full"), sig("ptb_out", 2), sig("os_full"), sig("os_out")
    dve_smp = sig("dve_smp", 0)
    dve_smp.per = 15
    dve_end = sig("dve_end", 6)
    carrier = sem("carrier3")

    with nc.Block() as block:
        @block.sync
        def _(sp):
            sp.dma_start(b_row[0:NH, :], scr_s).then_inc(ld_bias, 16)
            sp.wait_ge(pad_done, 2)

            def load(b, j):
                load_pages(sp, b, 1, pages_s[j], ld_pg[j])
                if not (isinstance(b, int) and b == 0):
                    load_window(sp, b, j)
                for r in range(2):
                    sp.dma_start(vnew[j][0:1, r * 256:(r + 1) * 256],
                                 scr_new[bass.ds(b, 1), 3 + 2 * r].rearrange("o g d -> o (g d)")).then_inc(ld_pg[j], 16)

            load(0, 0)
            load_pages(sp, 1, 0, pages_c[1], ld_cmp[1])
            load(1, 1)
            with sp.Fori(1, NB // 2) as i:
                for j in range(2):
                    sp.wait_ge(ord_done.sem, ord_done.at(i * 2 + j, -4))
                    sp.sem_inc(carrier, 1)
                    load_pages(sp, i * 2 + j, 0, pages_c[j], ld_cmp[j])
                    sp.wait_ge(os_full.sem, os_full.at(i * 2 + j, -1))
                    sp.sem_inc(carrier, 1)
                    load(i * 2 + j, j)
            sp.wait_ge(os_full.sem, NB - 1)
            for j in range(2):
                sp.dma_start(o2_rooms[j], io["nsa_w_out"][0].rearrange("(k p) n -> p k n", p=P)[:, :, j * 256:(j + 1) * 256])\
                    .then_inc(o2_ld[j], 16)

        @block.gpsimd
        def _(pool):
            nc.gpsimd.memset(vnew[0], 0.0)
            nc.gpsimd.memset(vnew[1], 0.0).then_inc(pad_done, 1)
            nc.gpsimd.memset(ptn, 0.0)
            nc.gpsimd.memset(dropped, 0.0)
            nc.gpsimd.memset(qb, 0.0).then_inc(pad_done, 1)

        @block.tensor
        def _(pe):
            def turn_kv(b, lo, hi):
                for n in range(lo, hi):
                    if n % 2 == 0:
                        pe.wait_ge(ord_done.sem, ord_done.at(b, n // 2 + 1))
                    if n < 2:
                        pe.wait_ge(ts_out.sem, ts_out.at(b, n - 1))
                    else:
                        pe.wait_ge(tk_out.sem, tk_out.at(b, n - 1))
                    turn_pairs(n, 4 + n % 2)

            def turn_keys(b, j, first):
                pe.wait_ge(ld_pg[j], ld_of(b, j))
                for n in range(6):
                    pe.wait_ge(tk_out.sem, tk_out.at(b, 7 + min(n, 1)))
                    if n >= 2:
                        pe.wait_ge(ts_out.sem, ts_out.at(b, n - 1))
                    for t in range(4):
                        if n < 4:
                            src = pages_s[j][:, t, n % 2, n // 2 * P:n // 2 * P + P]
                        else:
                            src = wins[j][:, t % 2, t // 2, (n - 4) * P:(n - 4) * P + P]
                        mm = tr(psum[:, 4 + n % 2, t * P:(t + 1) * P], src, P)
                    mm.then_inc(ts_full.sem, 1)

            def compress(b, t):
                pe.wait_ge(tk_out.sem, tk_out.at(b, 8))
                if t:
                    pe.wait_ge(h_out.sem, h_out.at(b, 1))
                else:
                    pe.wait_ge(kv_out.sem, kv_out.at(b, 0))
                hidden_layer(t, psum[:, 6, t * 256:t * 256 + G * NCS])

            def second(b, first):
                pe.wait_ge(h_out.sem, h_out.at(b, 2))
                if not first:
                    pe.wait_ge(ptb_out.sem, ptb_out.at(b, 0))
                for g in range(G):
                    nc.tensor.matmul(psum[g % 2 * DH:(g % 2 + 1) * DH, 7, 256 + g // 2 * NCS:256 + (g // 2 + 1) * NCS],
                                     w2k[:, 0:DH], hid_s[:, 0, g * NCS:(g + 1) * NCS], start=True, stop=True)
                for g in range(G):
                    mm = nc.tensor.matmul(psum[0:NCS, 6, g * DH:(g + 1) * DH], hid_s[:, 1, g * NCS:(g + 1) * NCS], w2v,
                                          start=True, stop=True)
                mm.then_inc(kv_full.sem, 1)

            def turn(b, j, more=True, first=False):
                pe.wait_ge(cur_done.sem, cur_done.at(b, 1))
                pe.wait_ge(kv_out.sem, kv_out.at(b, 2))
                pe.wait_ge(ts_out.sem, ts_out.at(b, 6))
                if not first:
                    pe.wait_ge(os_out.sem, os_out.at(b, 0))
                for a in range(2):
                    for g in range(2):
                        nc.tensor.matmul(psum[0:NH, a, :], qcur[:, g, :], kselt[:, g, a, :], start=(g == 0), stop=(g == 1))
                for g in range(2):
                    nc.tensor.matmul(psum[0:NH, 2, :], qcur[:, g, :], kwint[:, g].rearrange("p a n -> p (a n)"),
                                     start=(g == 0), stop=(g == 1))
                for r in range(2):
                    for g in range(2):
                        nc.tensor.matmul(psum[0:NH, 3, r:r + 1], qcur[:, g, :], kcur[:, r, g:g + 1],
                                         start=(g == 0), stop=(g == 1))
                for g in range(2):
                    mm = nc.tensor.matmul(psum[0:NH, 3, 64:64 + NCS], qcur[:, g, :], kcmp[:, g, :],
                                          start=(g == 0), stop=(g == 1))
                mm.then_inc(score_full.sem, 1)
                if more:
                    turn_kv(b + 1, 0, 6)
                pe.wait_ge(pc_done.sem, pc_done.at(b, 1))
                pe.wait_ge(score_used.sem, score_used.at(b, 1))
                pe.sem_inc(carrier, 1)
                tr(psum[0:NCS, 3, 0:NH], s_row[0:NH, S_CMP:S_CMP + NCS], NH)
                tr(psum[0:NCS, 3, NH:2 * NH], pcg[0:NH, :], NH).then_inc(pcT_full.sem, 1)
                if more:
                    turn_kv(b + 1, 6, 8)
                    compress(b + 1, 0)
                pe.wait_ge(pcT_out.sem, pcT_out.at(b, 1))
                pe.sem_inc(carrier, 1)
                nc.tensor.matmul(psum[0:NH, 3, 64:64 + NSEL], pcT[0:NCS, 0:NH], const("overlap", NCS),
                                 start=True, stop=True).then_inc(imp_full.sem, 1)
                if more:
                    turn_keys(b + 1, 1 - j, False)
                pe.wait_ge(imp_out.sem, imp_out.at(b, 1))
                pe.sem_inc(carrier, 1)
                nc.tensor.matmul(psum[0:NH, 3, 128:128 + NSEL], const("group", NH), impH[0:NH, :],
                                 start=True, stop=True).then_inc(grp_full.sem, 1)
                if more:
                    compress(b + 1, 1)
                pe.wait_ge(probs_done.sem, probs_done.at(b, 1))
                pe.sem_inc(carrier, 1)
                for n in range(12):
                    at = n * P if n < 8 else S_WIN + (n - 8) * P
                    tr(psum[:, 7, n * NH:(n + 1) * NH], s_row[0:NH, at:at + P], NH)
                for r, at in enumerate((S_NEWS, S_NEWW)):
                    mm = tr(psum[0:1, 7, (12 + r) * NH:(13 + r) * NH], s_row[0:NH, at:at + 1], NH)
                mm.then_inc(ptb_full.sem, 1)
                pe.wait_ge(ptb_out.sem, ptb_out.at(b, 2))
                for g in range(2):
                    def out(r):
                        o = (g * 3 + r) * NH
                        return psum[:, 2, o:o + NH]

                    nc.tensor.matmul(out(0), vcmp[0:NCS, g * P:(g + 1) * P], pcT[0:NCS, NH:2 * NH], start=True, stop=True)
                    for n in range(8):
                        nc.tensor.matmul(out(1), pages_s[j][:, n % 4, n // 4, 256 + g * P:256 + (g + 1) * P],
                                         ptb[:, n * NH:(n + 1) * NH], start=(n == 0), stop=False)
                    nc.tensor.matmul(out(1), vnew[j][:, g * P:(g + 1) * P], ptn[:, 0:NH], start=False, stop=True)
                    for n in range(4):
                        nc.tensor.matmul(out(2), wins[j][:, n % 2, n // 2, 256 + g * P:256 + (g + 1) * P],
                                         ptb[:, (8 + n) * NH:(9 + n) * NH], start=(n == 0), stop=False)
                    mm = nc.tensor.matmul(out(2), vnew[j][:, 256 + g * P:256 + (g + 1) * P], ptn[:, NH:2 * NH],
                                          start=False, stop=True)
                mm.then_inc(os_full.sem, 1)
                if more:
                    second(b + 1, False)

            def ld_of(b, j):
                return (b - j) * (NLD // 2) + NLD

            nc.tensor.matmul(psum[:, 7, 0:KT * NB], const("swap"), qsm.rearrange("p k b -> p (k b)"),
                             start=True, stop=True).then_inc(swap_full, 1)
            turn_keys(0, 0, True)
            pe.wait_ge(swap_out, 1)
            second(0, True)
            pe.wait_ge(pad_done, 2)
            turn(0, 0, first=True)
            turn(1, 1)
            with pe.Fori(1, NB // 2 - 1) as i:
                turn(i * 2, 0)
                turn(i * 2 + 1, 1)
            turn(NB - 2, 0)
            turn(NB - 1, 1, more=False)
            pe.wait_ge(os_out.sem, NB)
            for h in range(2):
                mm = nc.tensor.matmul(psum[:, h, 0:384], const("swap"), o_all[:, 4 * h:4 * h + 4, :].rearrange("p b n -> p (b n)"),
                                      start=True, stop=True)
            mm.then_inc(osw_full, 1)

        @block.scalar
        def _(act):
            def kv_out_of(b, n):
                pairs_out(act, b, n, 4 + n % 2)

            def hidden(b, t):
                hidden_out(act, b, t, psum[:, 6, t * 256:t * 256 + G * NCS])

            def second_out(b):
                act.wait_ge(kv_full.sem, kv_full.at(b, 1))
                nc.scalar.activation(kcmp, psum[:, 7, 256:256 + 2 * NCS].rearrange("p (h n) -> p h n", h=2), ACT.Copy).then_inc(kv_out.sem, 1)
                nc.scalar.activation(vcmp[0:NCS, :], psum[0:NCS, 6, 0:256], ACT.Copy).then_inc(kv_out.sem, 1)

            def turn(b, more=True):
                if more:
                    act.wait_ge(h_full.sem, h_full.at(b, 2))
                    for n in range(4):
                        kv_out_of(b + 1, n)
                act.wait_ge(c_ready.sem, c_ready.at(b, 1))
                nc.scalar.activation(s_row[0:NH, S_CMP:S_CMP + NCS], s_row[0:NH, S_CMP:S_CMP + NCS], ACT.Exp,
                                     bias=stat[0:NH, 0:1], accum_out=stat[0:NH, 1:2]).then_inc(c_exp.sem, 1)
                if more:
                    for n in range(4, 8):
                        kv_out_of(b + 1, n)
                act.wait_ge(w_ready.sem, w_ready.at(b, 1))
                nc.scalar.activation(s_row[0:NH, S_WIN:S_CMP], s_row[0:NH, S_WIN:S_CMP], ACT.Exp,
                                     bias=stat[0:NH, 4:5], accum_out=stat[0:NH, 5:6]).then_inc(w_exp.sem, 1)
                if more:
                    hidden(b + 1, 0)
                act.wait_ge(sel_ready.sem, sel_ready.at(b, 1))
                nc.scalar.activation(s_row[0:NH, S_SEL:S_WIN], s_row[0:NH, S_SEL:S_WIN], ACT.Exp,
                                     bias=stat[0:NH, 8:9], accum_out=stat[0:NH, 9:10]).then_inc(sel_exp.sem, 1)
                if more:
                    hidden(b + 1, 1)
                act.wait_ge(ptb_full.sem, ptb_full.at(b, 1))
                nc.scalar.activation(ptb, psum[:, 7, 0:12 * NH], ACT.Copy).then_inc(ptb_out.sem, 1)
                nc.scalar.activation(ptn[0:1, :], psum[0:1, 7, 12 * NH:14 * NH], ACT.Copy).then_inc(ptb_out.sem, 1)
                if more:
                    act.wait_ge(os_full.sem, os_full.at(b, 1))
                    second_out(b + 1)

            act.wait_ge(swap_full, 1)
            nc.scalar.activation(qsw, psum[:, 7, 0:KT * NB].rearrange("p (k b) -> p k b", k=KT), ACT.Copy).then_inc(swap_out, 1)
            act.wait_ge(pad_done, 2)
            second_out(0)
            with act.Fori(0, NB - 1) as b:
                turn(b)
            turn(NB - 1, more=False)

        @block.vector
        def _(dve):
            def current(b):
                nc.vector.tensor_copy(qcur, qb[:, :, :, bass.ds(b, 1)].rearrange("p g h o -> p g (h o)"))
                k4 = kns.rearrange("p r (h e) b -> p r h e b", e=2)
                for e in range(2):
                    lo = slice(e * 64, e * 64 + 64)
                    ins = nc.vector.tensor_copy(kcur[lo], k4[lo, :, :, e, bass.ds(b, 1)].rearrange("p r h o -> p r (h o)"))
                ins.then_inc(cur_done.sem, 1)

            def keys_out_of(b, n):
                dve.wait_ge(ts_full.sem, ts_full.at(b, n + 1))
                dst = kselt[:, n // 2, n % 2, :] if n < 4 else kwint[:, n - 4].rearrange("p a n -> p (a n)")
                nc.vector.tensor_copy(dst, psum[:, 4 + n % 2, :]).then_inc(ts_out.sem, 1)

            def turn(b, j, more=True, first=False):
                s = Steps(dve, dve_smp)
                s.turn(b)
                if more:
                    for t in range(2):
                        if not first:
                            dve.wait_ge(tk_full.sem, tk_full.at(b + 1, 0))
                        order_pairs(dve, b + 1, 1 - j, t)
                row = s_row[0:NH]
                bias = b_row[0:NH]
                dve.wait_ge(score_full.sem, score_full.at(b, 1))
                if not (isinstance(b, int) and b == 0):
                    dve.wait_ge(ptb_full.sem, ptb_full.at(b, 0))
                s.link(nc.vector.tensor_tensor(row[:, S_CMP:], psum[0:NH, 3, 64:64 + NCS], bias[:, S_CMP:], ALU.add))
                s.link(nc.vector.tensor_reduce(stat[0:NH, 0:1], row[:, S_CMP:], AX.X, ALU.max))
                s.post(nc.vector.tensor_scalar(stat[0:NH, 0:1], stat[0:NH, 0:1], -1.0, None, ALU.mult), c_ready)
                nc.vector.tensor_tensor(row[:, S_NEWS:S_NEWS + 1], psum[0:NH, 3, 0:1], bias[:, S_NEWS:S_NEWS + 1], ALU.add)
                nc.vector.tensor_tensor(row[:, S_NEWW:S_NEWW + 1], psum[0:NH, 3, 1:2], bias[:, S_NEWW:S_NEWW + 1], ALU.add)
                nc.vector.tensor_tensor(row[:, S_WIN:S_NEWW], psum[0:NH, 2, :], bias[:, S_WIN:S_NEWW], ALU.add)
                s.link(nc.vector.tensor_tensor(row[:, S_SEL:S_NEWS].rearrange("p (a n) -> p a n", a=2), psum[0:NH, 0:2, :],
                                               bias[:, S_SEL:S_NEWS].rearrange("p (a n) -> p a n", a=2), ALU.add), score_used)
                s.link(nc.vector.tensor_reduce(stat[0:NH, 4:5], row[:, S_WIN:S_CMP], AX.X, ALU.max))
                s.post(nc.vector.tensor_scalar(stat[0:NH, 4:5], stat[0:NH, 4:5], -1.0, None, ALU.mult), w_ready)
                if more:
                    order_pairs(dve, b + 1, 1 - j, 2)
                dve.wait_ge(c_exp.sem, c_exp.at(b, 1))
                s.link(nc.vector.reciprocal(stat[0:NH, 2:3], stat[0:NH, 1:2]))
                s.link(nc.vector.tensor_scalar(row[:, S_CMP:], row[:, S_CMP:], stat[0:NH, 2:3], None, ALU.mult))
                s.post(nc.vector.tensor_scalar(pcg[0:NH, :], row[:, S_CMP:], gsm[0:NH, 0, bass.ds(b, 1)], None, ALU.mult),
                       pc_done)
                if more:
                    order_pairs(dve, b + 1, 1 - j, 3)
                dve.wait_ge(pcT_full.sem, pcT_full.at(b, 1))
                s.post(nc.vector.tensor_copy(pcT[0:NCS, :], psum[0:NCS, 3, 0:2 * NH]), pcT_out)
                dve.wait_ge(imp_full.sem, imp_full.at(b, 1))
                s.post(nc.vector.tensor_copy(impH[0:NH, :], psum[0:NH, 3, 64:64 + NSEL]), imp_out)
                if more:
                    for n in range(6):
                        keys_out_of(b + 1, n)
                dve.wait_ge(grp_full.sem, grp_full.at(b, 1))
                s.link(nc.vector.tensor_reduce(stat[0:NH, 3:4], psum[0:NH, 3, 129:143], AX.X, ALU.min))
                s.link(nc.vector.tensor_scalar(cand[0:NH, :], psum[0:NH, 3, 129:143], stat[0:NH, 3:4], None, ALU.is_le))
                s.link(nc.vector.tensor_tensor(keyed[0:NH, :], cand[0:NH, :], const("order", NH), ALU.mult))
                s.link(nc.vector.tensor_reduce(stat[0:NH, 7:8], keyed[0:NH, :], AX.X, ALU.max))
                s.link(nc.vector.tensor_scalar(dropped[0:NH, 1:15], keyed[0:NH, :], stat[0:NH, 7:8], NEG, ALU.is_equal, ALU.mult))
                sel = row[:, S_SEL:S_NEWS].rearrange("p (a s n) -> p a s n", a=2, s=16)
                s.link(nc.vector.tensor_tensor(sel, sel, dropped[0:NH, :].unsqueeze(1).unsqueeze(3).to_broadcast([NH, 2, 16, 32]),
                                               ALU.add))
                s.link(nc.vector.tensor_reduce(stat[0:NH, 8:9], row[:, S_SEL:S_WIN], AX.X, ALU.max))
                s.post(nc.vector.tensor_scalar(stat[0:NH, 8:9], stat[0:NH, 8:9], -1.0, None, ALU.mult), sel_ready)
                dve.wait_ge(w_exp.sem, w_exp.at(b, 1))
                s.link(nc.vector.reciprocal(stat[0:NH, 6:7], stat[0:NH, 5:6]))
                s.link(nc.vector.tensor_scalar(row[:, S_WIN:S_CMP], row[:, S_WIN:S_CMP], stat[0:NH, 6:7],
                                               gsm[0:NH, 2, bass.ds(b, 1)], ALU.mult, ALU.mult))
                dve.wait_ge(sel_exp.sem, sel_exp.at(b, 1))
                s.link(nc.vector.reciprocal(stat[0:NH, 10:11], stat[0:NH, 9:10]))
                s.link(nc.vector.tensor_scalar(row[:, S_SEL:S_WIN], row[:, S_SEL:S_WIN], stat[0:NH, 10:11],
                                               gsm[0:NH, 1, bass.ds(b, 1)], ALU.mult, ALU.mult), probs_done)
                if more:
                    current(b + 1)
                dve.wait_ge(os_full.sem, os_full.at(b, 1))
                s.link(nc.vector.tensor_copy(o_all[:, bass.ds(b, 1), :].rearrange("p o n -> p (o n)"), psum[:, 2, 0:6 * NH]), os_out)
                s.turn(b)

            dve.wait_ge(pad_done, 2)
            dve.wait_ge(swap_out, 1)
            dve.wait_ge(ld_bias, 16)
            for gp in range(2):
                for g2 in range(2):
                    lo = slice(g2 * 64, g2 * 64 + 64)
                    for h2 in range(2):
                        src = qsm if g2 == h2 else qsw
                        g = 2 * gp + g2
                        ins = nc.vector.tensor_copy(qb[lo, gp, 4 * g + h2:4 * g + 4:2, :], src[lo, 2 * g:2 * g + 2, :])
            ins.then_inc(qb_done, 1)
            dve.wait_ge(qb_done, 1)
            current(0)
            for n in range(6):
                keys_out_of(0, n)
            turn(0, 0)
            turn(1, 1)
            with dve.Fori(1, NB // 2 - 1) as i:
                turn(i * 2, 0)
                turn(i * 2 + 1, 1)
            turn(NB - 2, 0)
            turn(NB - 1, 1, more=False)
            dve.wait_ge(osw_full, 1)
            nc.vector.tensor_copy(o_swp.rearrange("p (h b) n -> p h (b n)", h=2), psum[:, 0:2, 0:384]).then_inc(osw_out, 1)
            dve.wait_ge(osw_out, 1)
            s = Steps(dve, dve_end)
            s.turn(0)
            for r in range(3):
                for gp in range(2):
                    for g2 in range(2):
                        g = 2 * gp + g2
                        for h2 in range(2):
                            lo = slice(h2 * 64, h2 * 64 + 64)
                            src = o_all if g2 == h2 else o_swp
                            at = (gp * 3 + r) * NH + 4 * g + h2
                            ins = nc.vector.tensor_tensor((mtmp if r else msm)[lo, 2 * g:2 * g + 2, :],
                                                          src[lo, :, at:at + 3:2].rearrange("p b i -> p i b"),
                                                          zsm[lo, r, 2 * g:2 * g + 2, :], ALU.mult)
                s.link(ins)
                if r:
                    s.link(nc.vector.tensor_tensor(msm, msm, mtmp, ALU.add))
            s.link(nc.vector.tensor_copy(mixed[:, :, SEQ:T], msm))
            s.turn(0)


    arena.at = base_smp
    w_rooms = [take(KT * 256).rearrange("p (k n) -> p k n", k=KT) for _ in range(2)]
    std2, rstd2, sumsq = take(T), take(T), take(T)
    ytok = take(4 * D).rearrange("p (a d) -> p a d", a=4)
    ysamp = take(D)
    y_full, y_out, st_y = sem("y_full"), sem("y_out"), sem("st_y")
    y_jobs = [(a, half) for half in range(2) for a in range(5)]

    def result_pe(pe, xnd):
        for j, (a, half) in enumerate(y_jobs):
            if j >= 8:
                pe.wait_ge(y_out, j - 7)
            for c in range(4):
                k = half * 4 + c
                pe.wait_ge(xnd, k + 1)
                if a < 4:
                    mm = tr(psum[:, j % 8, c * P:(c + 1) * P], xn[:, k, a * P:(a + 1) * P], P)
                else:
                    mm = tr(psum[0:NB, j % 8, c * P:(c + 1) * P], xn[:, k, SEQ:T], P)
            mm.then_inc(y_full, 1)

    def result_act(act):
        for j, (a, half) in enumerate(y_jobs):
            act.wait_ge(y_full, j + 1)
            cols = slice(half * 512, half * 512 + 512)
            if a < 4:
                nc.scalar.activation(ytok[:, a, cols], psum[:, j % 8, :], ACT.Copy).then_inc(y_out, 1)
            else:
                nc.scalar.activation(ysamp[0:NB, cols], psum[0:NB, j % 8, :], ACT.Copy).then_inc(y_out, 1)

    def result_sp(sp):
        for a in range(4):
            sp.wait_ge(y_out, 6 + a)
            sp.dma_start(io["y_prompt"][0, a * P:(a + 1) * P, :], ytok[:, a, :]).then_inc(st_y, 16)
        sp.wait_ge(y_out, 10)
        sp.dma_start(io["y_sample"].rearrange("b s d -> (b s) d"), ysamp[0:NB, :]).then_inc(st_y, 16)
        sp.wait_ge(st_y, 80)

    project_out("o2", KT, mixed, io["nsa_w_out"][0], w_rooms, o2_ld, 2, PR_NF,
                {"sync": result_sp, "tensor_last": result_pe, "scalar_last": result_act})



INS = ['x_prompt', 'x_sample', 'state_ssm', 'state_conv', 'cache_kv', 'cache_win', 'page_table', 'rel_bias',
       'final_norm', 'ssd_norm', 'ssd_w_in', 'ssd_conv_w', 'ssd_conv_b', 'ssd_dt_bias', 'ssd_a_log', 'ssd_d',
       'ssd_gnorm', 'ssd_w_out', 'nsa_norm', 'nsa_w_in', 'nsa_cmp_pe', 'nsa_cmp_w1', 'nsa_cmp_w2', 'nsa_w_out']
OUTS = [("y_prompt", (1, SEQ, D)), ("y_sample", (NB, 1, D)), ("ssm_prompt", (1, 1, SH, SP_, SN)),
        ("conv_prompt", (1, 1, 3, CONV)), ("kv_prompt", (1, SEQ, 1, 4, G, DH)), ("win_prompt", (1, 1, 512, 2, G, DH)),
        ("ssm_sample", (1, NB, SH, SP_, SN)), ("conv_sample", (1, NB, 3, CONV)),
        ("kv_sample", (NB, 1, 1, 4, G, DH)), ("win_sample", (1, NB, 512, 2, G, DH))]


def kernel(**inputs):
    import concourse.bacc as _bacc
    from concourse.bass_utils import run_bass_kernel_spmd as _run

    nc = _bacc.Bacc("TRN2", target_bir_lowering=False, num_devices=1)
    arrays = {name: np.ascontiguousarray(inputs[name]) for name in INS}
    arrays["const_a"], arrays["const_b"] = constants()
    io = {name: nc.dram_tensor("in_" + name, a.shape, mybir.dt.from_np(a.dtype), kind="ExternalInput").ap()
          for name, a in arrays.items()}
    for name, shape in OUTS:
        io[name] = nc.dram_tensor("out_" + name, shape, F32, kind="ExternalOutput").ap()
    build(nc, io)
    r = _run(nc, [{"in_" + name: a for name, a in arrays.items()}], core_ids=[0])
    return tuple(r.results[0]["out_" + name] for name, _shape in OUTS)
```
